# Optimizing a Trainium2 kernel written in Bass

```python
import jax, jax.numpy as jnp
from jax import lax
import numpy as np

D_MODEL = 1024
BATCH = 1
SEQ = 512
DEPTH = 1

N_MEM = 256
D_MIX = D_MODEL
D_A = D_MIX // 4
D_B = D_MIX // 4
D_C = D_MIX // 2
H_A = 4
H_B = 4
H_C = 4
DH_A = D_A // H_A
DH_B = D_B // H_B
DH_C = D_C // H_C
CHUNK = 128
CONV_B = 31
CONV_C = 4
CONV_F = 3
N_XHEADS = 4
DH_X = D_MODEL // N_XHEADS
D_FF = ((8 * D_MODEL // 3 + 255) // 256) * 256
D_IN = 2 * D_A + 2 * D_B + 2 * D_C + 2 * H_C
RMS_EPS = 1e-6
LN_EPS = 1e-5


def rmsnorm(x, g):
    xf = x.astype(jnp.float32)
    y = xf * lax.rsqrt(jnp.mean(xf * xf, axis=-1, keepdims=True) + RMS_EPS)
    return (y * g.astype(jnp.float32)).astype(x.dtype)

def standardize(x):
    xf = x.astype(jnp.float32)
    mu = jnp.mean(xf, axis=-1, keepdims=True)
    var = jnp.mean(jnp.square(xf - mu), axis=-1, keepdims=True)
    return (xf - mu) * lax.rsqrt(var + LN_EPS)

def causal_dwconv(x, w, b):
    K, C = w.shape
    y = lax.conv_general_dilated(
        x, w[:, None, :].astype(x.dtype), window_strides=(1,),
        padding=[(K - 1, 0)], dimension_numbers=('NWC', 'WIO', 'NWC'),
        feature_group_count=C)
    return y + b.astype(x.dtype)

def gmlp_spatial_gating(u, v, ln_g, ln_b, w_s, b_s):
    Bsz, S, _ = v.shape
    vn = (standardize(v) * ln_g + ln_b).astype(v.dtype)
    vn = vn.reshape(Bsz, S // CHUNK, CHUNK, H_A, DH_A)
    mask = jnp.tril(jnp.ones((CHUNK, CHUNK), dtype=bool))
    w = jnp.where(mask, w_s, 0.0).astype(v.dtype)
    s = jnp.einsum('hts,bcshd->bcthd', w, vn) + b_s.T.astype(v.dtype)[None, None, :, :, None]
    return u * s.reshape(Bsz, S, D_A)

def conformer_conv(a, g, conv_w, conv_b, gn_g, gn_b):
    Bsz, S, _ = a.shape
    y = a * jax.nn.sigmoid(g)
    y = causal_dwconv(y, conv_w, conv_b)
    yn = standardize(y.reshape(Bsz, S, H_B, DH_B)).reshape(Bsz, S, D_B)
    y = (yn * gn_g + gn_b).astype(a.dtype)
    return jax.nn.silu(y)

def mlstm_chunkwise(q, k, v, logi, logf):
    Bsz, H, S, DH = q.shape
    NC = S // CHUNK
    q = q * (DH ** -0.5)

    def to_chunks(a):
        a = a.reshape((Bsz, H, NC, CHUNK) + a.shape[3:])
        return jnp.moveaxis(a, 2, 0)

    qc, kc, vc, ic, fc = (to_chunks(t) for t in (q, k, v, logi, logf))
    mask = jnp.tril(jnp.ones((CHUNK, CHUNK), dtype=bool))

    def step(carry, inp):
        C, n, m = carry
        qt, kt, vt, it, ft = inp
        bcum = jnp.cumsum(ft, axis=-1)
        dmat = bcum[..., :, None] - bcum[..., None, :] + it[..., None, :]
        dmat = jnp.where(mask, dmat, -jnp.inf)
        inter = bcum + m[..., None]
        m_t = jnp.maximum(inter, jnp.max(dmat, axis=-1))
        w_intra = jnp.exp(dmat - m_t[..., None])
        w_inter = jnp.exp(inter - m_t)
        scores = jnp.einsum('bhtd,bhsd->bhts', qt, kt) * w_intra
        num = (w_inter[..., None] * jnp.einsum('bhtd,bhde->bhte', qt, C)
               + jnp.einsum('bhts,bhse->bhte', scores, vt))
        den = w_inter * jnp.einsum('bhtd,bhd->bht', qt, n) + jnp.sum(scores, axis=-1)
        h = num / jnp.maximum(jnp.abs(den), jnp.exp(-m_t))[..., None]
        btot = bcum[..., -1]
        gdec = btot[..., None] - bcum + it
        m_new = jnp.maximum(btot + m, jnp.max(gdec, axis=-1))
        decay = jnp.exp(btot + m - m_new)
        wg = jnp.exp(gdec - m_new[..., None])
        C_new = decay[..., None, None] * C + jnp.einsum('bhs,bhsd,bhse->bhde', wg, kt, vt)
        n_new = decay[..., None] * n + jnp.einsum('bhs,bhsd->bhd', wg, kt)
        return (C_new, n_new, m_new), h

    init = (jnp.zeros((Bsz, H, DH, DH), jnp.float32),
            jnp.zeros((Bsz, H, DH), jnp.float32),
            jnp.zeros((Bsz, H), jnp.float32))
    _, hs = lax.scan(step, init, (qc, kc, vc, ic, fc))
    return jnp.moveaxis(hs, 0, 2).reshape(Bsz, H, S, DH)

def mlstm_group(xc, oc, gi, gf, b_igate, b_fgate, conv_w, conv_b, w_q, w_k, w_v, hn_g, skip):
    Bsz, S, _ = xc.shape
    xconv = jax.nn.silu(causal_dwconv(xc, conv_w, conv_b))
    xh = xconv.reshape(Bsz, S, H_C, DH_C)
    xv = xc.reshape(Bsz, S, H_C, DH_C)
    q = jnp.einsum('bshd,hde->bhse', xh, w_q).astype(jnp.float32)
    k = jnp.einsum('bshd,hde->bhse', xh, w_k).astype(jnp.float32)
    v = jnp.einsum('bshd,hde->bhse', xv, w_v).astype(jnp.float32)
    logi = jnp.transpose(gi.astype(jnp.float32) + b_igate.astype(jnp.float32), (0, 2, 1))
    logf = jax.nn.log_sigmoid(jnp.transpose(gf.astype(jnp.float32) + b_fgate.astype(jnp.float32), (0, 2, 1)))
    hcell = mlstm_chunkwise(q, k, v, logi, logf)
    hcell = jnp.transpose(hcell, (0, 2, 1, 3))
    hnorm = (standardize(hcell) * hn_g.reshape(H_C, DH_C)).reshape(Bsz, S, D_C).astype(xc.dtype)
    return jax.nn.sigmoid(oc) * (hnorm + skip * xconv)

def hybrid_mixer(hn, w_in, b_igate, b_fgate, ln_a_g, ln_a_b, w_s, b_s,
                 conv_b_w, conv_b_b, gn_b_g, gn_b_b, conv_c_w, conv_c_b,
                 w_q_c, w_k_c, w_v_c, hn_c_g, skip_c, w_out):
    z = hn @ w_in
    o0 = 2 * D_A
    o1 = o0 + 2 * D_B
    o2 = o1 + D_C
    o3 = o2 + D_C
    o4 = o3 + H_C
    za = jax.nn.gelu(z[..., :o0], approximate=False)
    y_a = gmlp_spatial_gating(za[..., :D_A], za[..., D_A:], ln_a_g, ln_a_b, w_s, b_s)
    zb = z[..., o0:o1]
    y_b = conformer_conv(zb[..., :D_B], zb[..., D_B:], conv_b_w, conv_b_b, gn_b_g, gn_b_b)
    y_c = mlstm_group(z[..., o1:o2], z[..., o2:o3], z[..., o3:o4], z[..., o4:],
                      b_igate, b_fgate, conv_c_w, conv_c_b, w_q_c, w_k_c, w_v_c, hn_c_g, skip_c)
    return jnp.concatenate([y_a, y_b, y_c], axis=-1) @ w_out

def cross_attention(hn, mn, w_xq, w_xkv, w_xo):
    Bsz, S, _ = hn.shape
    M = mn.shape[1]
    q = (hn @ w_xq).reshape(Bsz, S, N_XHEADS, DH_X)
    kv = mn @ w_xkv
    k = kv[..., :D_MODEL].reshape(Bsz, M, N_XHEADS, DH_X)
    v = kv[..., D_MODEL:].reshape(Bsz, M, N_XHEADS, DH_X)
    s = jnp.einsum('bshd,bmhd->bhsm', q, k).astype(jnp.float32) * (DH_X ** -0.5)
    p = jax.nn.softmax(s, axis=-1).astype(v.dtype)
    o = jnp.einsum('bhsm,bmhd->bshd', p, v).reshape(Bsz, S, D_MODEL)
    return o @ w_xo

def conv_glu(hn, w_up, conv_f_w, conv_f_b, w_down):
    up = hn @ w_up
    gate = jax.nn.gelu(causal_dwconv(up[..., :D_FF], conv_f_w, conv_f_b), approximate=False)
    return (gate * up[..., D_FF:]) @ w_down

def first_inputs(seed: int = 0) -> dict:
    key = jax.random.key(seed)
    ks = iter(jax.random.split(key, 48))

    def nrm(shape, scale):
        return jax.random.normal(next(ks), shape, jnp.float32) * scale

    L = DEPTH
    return {
        "x": nrm((BATCH, SEQ, D_MODEL), 1.0),
        "mem": nrm((BATCH, N_MEM, D_MODEL), 1.0),
        "norm_mix_g": 1.0 + nrm((L, D_MODEL), 0.02),
        "w_in": nrm((L, D_MODEL, D_IN), D_MODEL ** -0.5),
        "b_igate": nrm((L, H_C), 0.1),
        "b_fgate": jax.random.uniform(next(ks), (L, H_C), jnp.float32, 3.0, 6.0),
        "ln_a_g": 1.0 + nrm((L, D_A), 0.02),
        "ln_a_b": nrm((L, D_A), 0.02),
        "w_s": nrm((L, H_A, CHUNK, CHUNK), CHUNK ** -0.5),
        "b_s": 1.0 + nrm((L, H_A, CHUNK), 0.1),
        "conv_b_w": nrm((L, CONV_B, D_B), CONV_B ** -0.5),
        "conv_b_b": nrm((L, D_B), 0.02),
        "gn_b_g": 1.0 + nrm((L, D_B), 0.02),
        "gn_b_b": nrm((L, D_B), 0.02),
        "conv_c_w": nrm((L, CONV_C, D_C), CONV_C ** -0.5),
        "conv_c_b": nrm((L, D_C), 0.02),
        "w_q_c": nrm((L, H_C, DH_C, DH_C), DH_C ** -0.5),
        "w_k_c": nrm((L, H_C, DH_C, DH_C), DH_C ** -0.5),
        "w_v_c": nrm((L, H_C, DH_C, DH_C), DH_C ** -0.5),
        "hn_c_g": 1.0 + nrm((L, D_C), 0.02),
        "skip_c": 1.0 + nrm((L, D_C), 0.02),
        "w_out": nrm((L, D_MIX, D_MODEL), D_MIX ** -0.5),
        "norm_x_g": 1.0 + nrm((L, D_MODEL), 0.02),
        "norm_mem_g": 1.0 + nrm((L, D_MODEL), 0.02),
        "w_xq": nrm((L, D_MODEL, D_MODEL), D_MODEL ** -0.5),
        "w_xkv": nrm((L, D_MODEL, 2 * D_MODEL), D_MODEL ** -0.5),
        "w_xo": nrm((L, D_MODEL, D_MODEL), D_MODEL ** -0.5),
        "norm_ffn_g": 1.0 + nrm((L, D_MODEL), 0.02),
        "w_up": nrm((L, D_MODEL, 2 * D_FF), D_MODEL ** -0.5),
        "conv_f_w": nrm((L, CONV_F, D_FF), CONV_F ** -0.5),
        "conv_f_b": nrm((L, D_FF), 0.02),
        "w_down": nrm((L, D_FF, D_MODEL), D_FF ** -0.5),
        "final_g": 1.0 + nrm((D_MODEL,), 0.02),
    }

def first_block(x, mem, norm_mix_g, w_in, b_igate, b_fgate, ln_a_g, ln_a_b, w_s, b_s,
              conv_b_w, conv_b_b, gn_b_g, gn_b_b, conv_c_w, conv_c_b,
              w_q_c, w_k_c, w_v_c, hn_c_g, skip_c, w_out,
              norm_x_g, norm_mem_g, w_xq, w_xkv, w_xo,
              norm_ffn_g, w_up, conv_f_w, conv_f_b, w_down, final_g):
    h = x
    for l in range(DEPTH):
        hn = rmsnorm(h, norm_mix_g[l])
        h = h + hybrid_mixer(hn, w_in[l], b_igate[l], b_fgate[l], ln_a_g[l], ln_a_b[l],
                             w_s[l], b_s[l], conv_b_w[l], conv_b_b[l], gn_b_g[l], gn_b_b[l],
                             conv_c_w[l], conv_c_b[l], w_q_c[l], w_k_c[l], w_v_c[l],
                             hn_c_g[l], skip_c[l], w_out[l])
        hn = rmsnorm(h, norm_x_g[l])
        mn = rmsnorm(mem, norm_mem_g[l])
        h = h + cross_attention(hn, mn, w_xq[l], w_xkv[l], w_xo[l])
        hn = rmsnorm(h, norm_ffn_g[l])
        h = h + conv_glu(hn, w_up[l], conv_f_w[l], conv_f_b[l], w_down[l])
    return rmsnorm(h, final_g)


DEPTH_2 = 2

NSA_HEADS = 8
NSA_KV_GROUPS = 2
NSA_HPG = NSA_HEADS // NSA_KV_GROUPS
NSA_HEAD_DIM = 64
NSA_WIDTH = NSA_HEADS * NSA_HEAD_DIM
NSA_KV_WIDTH = NSA_KV_GROUPS * NSA_HEAD_DIM
NSA_N_KV = 6
CMP_BLOCK = 32
CMP_STRIDE = 16
SEL_BLOCK = 64
SEL_TOP_N = 16
WINDOW = 512
NSA_QBLOCK = 64
POOL_WINDOWS = (2, 4, 8, 16)
POOL_GROUPS = len(POOL_WINDOWS)
POOL_WIDTH = D_MODEL - NSA_WIDTH
POOL_GROUP_DIM = POOL_WIDTH // POOL_GROUPS
A_IN = NSA_WIDTH + NSA_N_KV * NSA_KV_WIDTH + 3 * NSA_HEADS + POOL_WIDTH
GLA_HEADS = 4
GLA_KEY_WIDTH = D_MODEL // 2
GLA_VAL_WIDTH = D_MODEL
GLA_DK = GLA_KEY_WIDTH // GLA_HEADS
GLA_DV = GLA_VAL_WIDTH // GLA_HEADS
GLA_GATE_RANK = 16
GLA_TAU = 16.0
GLA_CHUNK = 64
C_IN = 2 * GLA_KEY_WIDTH + 2 * GLA_VAL_WIDTH + GLA_GATE_RANK
D_FF_2 = 4 * D_MODEL
N_EVEN = (DEPTH_2 + 1) // 2
N_ODD = DEPTH_2 // 2
ALPHA = (2 * DEPTH_2) ** 0.25
BETA = (8 * DEPTH_2) ** -0.25
MASK_VALUE = -1e30
FORCE_SCORE = 1e4


def layer_norm(x, g, b):
    xf = x.astype(jnp.float32)
    mu = jnp.mean(xf, axis=-1, keepdims=True)
    var = jnp.mean(jnp.square(xf - mu), axis=-1, keepdims=True)
    return ((xf - mu) * lax.rsqrt(var + LN_EPS) * g + b).astype(x.dtype)

def masked_softmax(s, mask):
    s = jnp.where(mask, s.astype(jnp.float32), MASK_VALUE)
    m = jnp.max(s, axis=-1, keepdims=True)
    e = jnp.where(mask, jnp.exp(s - m), 0.0)
    return e / jnp.maximum(jnp.sum(e, axis=-1, keepdims=True), 1e-30)

def compress_blocks(k, pos, w1, b1, w2):
    S = k.shape[2]
    n_cmp = (S - CMP_BLOCK) // CMP_STRIDE + 1
    idx = np.arange(n_cmp)[:, None] * CMP_STRIDE + np.arange(CMP_BLOCK)[None, :]
    blocks = k[:, :, idx, :] + pos
    flat = blocks.reshape(blocks.shape[:3] + (CMP_BLOCK * NSA_HEAD_DIM,))
    return jax.nn.gelu(flat @ w1 + b1) @ w2

def selection_map(n_cmp, n_sel):
    sub = np.arange(n_cmp)[:, None] + np.arange(CMP_BLOCK // CMP_STRIDE)[None, :]
    owner = sub // (SEL_BLOCK // CMP_STRIDE)
    return (owner[:, :, None] == np.arange(n_sel)[None, None, :]).sum(1).astype(np.float32)

def pool_mixer(u, pool_w, pool_scale):
    B, S, _ = u.shape
    uf = u.astype(jnp.float32).reshape(B, S, POOL_GROUPS, POOL_GROUP_DIM)
    cs = jnp.pad(jnp.cumsum(uf, axis=1), ((0, 0), (1, 0), (0, 0), (0, 0)))
    count_base = jnp.arange(1, S + 1, dtype=jnp.float32)
    outs = []
    for g, w in enumerate(POOL_WINDOWS):
        c = cs[:, :, g]
        lower = jnp.pad(c[:, :S + 1 - w], ((0, 0), (w - 1, 0), (0, 0)))
        mean = (c[:, 1:] - lower) / jnp.minimum(count_base, float(w))[None, :, None]
        outs.append(mean - uf[:, :, g])
    r = jnp.stack(outs, axis=2)
    y = jnp.einsum('bsgc,gcd->bsgd', r, pool_w.astype(jnp.float32))
    return (y.reshape(B, S, POOL_WIDTH) * pool_scale).astype(u.dtype)

def nsa_pool_mixer(x, w_in, cmp_pos, cmp_w1, cmp_b1, cmp_w2, pool_w, pool_scale, w_out):
    B, S, _ = x.shape
    G, HPG, DH = NSA_KV_GROUPS, NSA_HPG, NSA_HEAD_DIM
    h = x @ w_in
    o1 = NSA_WIDTH
    o2 = o1 + NSA_N_KV * NSA_KV_WIDTH
    o3 = o2 + 3 * NSA_HEADS
    q = h[..., :o1].reshape(B, S, G, HPG, DH).transpose(0, 2, 3, 1, 4)
    kv = h[..., o1:o2].reshape(B, S, NSA_N_KV, G, DH).transpose(2, 0, 3, 1, 4)
    gates = jax.nn.sigmoid(h[..., o2:o3].astype(jnp.float32))
    gates = gates.reshape(B, S, G, HPG, 3).transpose(0, 2, 3, 1, 4)
    u = h[..., o3:]
    k_cmp, v_cmp, k_slc, v_slc, k_win, v_win = kv[0], kv[1], kv[2], kv[3], kv[4], kv[5]

    kc = compress_blocks(k_cmp, cmp_pos[0], cmp_w1[0], cmp_b1[0], cmp_w2[0])
    vc = compress_blocks(v_cmp, cmp_pos[1], cmp_w1[1], cmp_b1[1], cmp_w2[1])
    n_cmp = kc.shape[2]
    n_sel = S // SEL_BLOCK
    top_n = min(SEL_TOP_N, n_sel)
    sel_map = jnp.asarray(selection_map(n_cmp, n_sel))
    cmp_end = jnp.arange(n_cmp) * CMP_STRIDE + CMP_BLOCK - 1
    ks_b = k_slc.reshape(B, G, n_sel, SEL_BLOCK, DH)
    vs_b = v_slc.reshape(B, G, n_sel, SEL_BLOCK, DH)
    kw = jnp.pad(k_win, ((0, 0), (0, 0), (WINDOW, 0), (0, 0)))
    vw = jnp.pad(v_win, ((0, 0), (0, 0), (WINDOW, 0), (0, 0)))
    bi = jnp.arange(B)[:, None, None, None]
    gi = jnp.arange(G)[None, :, None, None]
    scale = DH ** -0.5

    def query_block(i):
        t0 = i * NSA_QBLOCK
        t = t0 + jnp.arange(NSA_QBLOCK)
        qb = lax.dynamic_slice_in_dim(q, t0, NSA_QBLOCK, axis=3) * scale
        gb = lax.dynamic_slice_in_dim(gates, t0, NSA_QBLOCK, axis=3)
        s_c = jnp.einsum('bghqd,bgcd->bghqc', qb, kc)
        p_c = masked_softmax(s_c, cmp_end[None, :] <= t[:, None])
        o_c = jnp.einsum('bghqc,bgcd->bghqd', p_c.astype(vc.dtype), vc)
        imp = jnp.einsum('bghqc,cj->bgqj', p_c, sel_map)
        blk = jnp.arange(n_sel)[None, :]
        cur = (t // SEL_BLOCK)[:, None]
        forced = (blk == 0) | (blk == cur) | (blk == cur - 1)
        imp = jnp.where(forced, FORCE_SCORE, jnp.where(blk > cur, -FORCE_SCORE, imp))
        _, sel = lax.top_k(imp, top_n)
        k_sel = ks_b[bi, gi, sel].reshape(B, G, NSA_QBLOCK, top_n * SEL_BLOCK, DH)
        v_sel = vs_b[bi, gi, sel].reshape(B, G, NSA_QBLOCK, top_n * SEL_BLOCK, DH)
        kpos = (sel[..., None] * SEL_BLOCK + jnp.arange(SEL_BLOCK)).reshape(
            B, G, NSA_QBLOCK, top_n * SEL_BLOCK)
        s_s = jnp.einsum('bghqd,bgqnd->bghqn', qb, k_sel)
        p_s = masked_softmax(s_s, (kpos <= t[:, None])[:, :, None])
        o_s = jnp.einsum('bghqn,bgqnd->bghqd', p_s.astype(v_sel.dtype), v_sel)
        k_w = lax.dynamic_slice_in_dim(kw, t0, WINDOW + NSA_QBLOCK, axis=2)
        v_w = lax.dynamic_slice_in_dim(vw, t0, WINDOW + NSA_QBLOCK, axis=2)
        wpos = t0 - WINDOW + jnp.arange(WINDOW + NSA_QBLOCK)
        wmask = ((wpos[None, :] <= t[:, None]) & (wpos[None, :] > t[:, None] - WINDOW)
                 & (wpos[None, :] >= 0))
        s_w = jnp.einsum('bghqd,bgkd->bghqk', qb, k_w)
        p_w = masked_softmax(s_w, wmask)
        o_w = jnp.einsum('bghqk,bgkd->bghqd', p_w.astype(v_w.dtype), v_w)
        o = gb[..., 0:1] * o_c + gb[..., 1:2] * o_s + gb[..., 2:3] * o_w
        return o.astype(x.dtype)

    ob = lax.map(query_block, jnp.arange(S // NSA_QBLOCK))
    o_nsa = ob.transpose(1, 0, 4, 2, 3, 5).reshape(B, S, NSA_WIDTH)
    o_pool = pool_mixer(u, pool_w, pool_scale)
    return jnp.concatenate([o_nsa, o_pool], axis=-1) @ w_out

def gla_mixer(x, w_in, gate_w2, gate_b, norm_g, w_out):
    B, S, _ = x.shape
    N, C, H = S // GLA_CHUNK, GLA_CHUNK, GLA_HEADS
    h = x @ w_in
    o1 = GLA_KEY_WIDTH
    o2 = o1 + GLA_KEY_WIDTH
    o3 = o2 + GLA_VAL_WIDTH
    o4 = o3 + GLA_VAL_WIDTH
    q_, k_, v_, r, a = h[..., :o1], h[..., o1:o2], h[..., o2:o3], h[..., o3:o4], h[..., o4:]
    loga = jax.nn.log_sigmoid((a @ gate_w2 + gate_b).astype(jnp.float32)) / GLA_TAU

    def heads(t, d):
        return t.reshape(B, N, C, H, d).transpose(0, 3, 1, 2, 4).astype(jnp.float32)

    q = heads(q_, GLA_DK) * GLA_DK ** -0.5
    k = heads(k_, GLA_DK)
    v = heads(v_, GLA_DV)
    b = jnp.cumsum(heads(loga, GLA_DK), axis=3)
    q_t = q * jnp.exp(b)
    k_t = k * jnp.exp(-b)
    causal = jnp.tril(jnp.ones((C, C), dtype=bool))
    att = jnp.where(causal, jnp.einsum('bhncd,bhnjd->bhncj', q_t, k_t), 0.0)
    o_intra = jnp.einsum('bhncj,bhnje->bhnce', att, v)
    b_last = b[:, :, :, -1:, :]
    upd = jnp.einsum('bhncd,bhnce->bhnde', k * jnp.exp(b_last - b), v)
    decay = jnp.exp(b_last[:, :, :, 0])

    def step(state, inp):
        d, u = inp
        return d[..., None] * state + u, state

    s0 = jnp.zeros((B, H, GLA_DK, GLA_DV), jnp.float32)
    _, s_prev = lax.scan(step, s0, (jnp.moveaxis(decay, 2, 0), jnp.moveaxis(upd, 2, 0)))
    s_prev = jnp.moveaxis(s_prev, 0, 2)
    o = o_intra + jnp.einsum('bhncd,bhnde->bhnce', q_t, s_prev)
    o = o * lax.rsqrt(jnp.mean(jnp.square(o), axis=-1, keepdims=True) + LN_EPS) * norm_g
    o = o.transpose(0, 2, 3, 1, 4).reshape(B, S, GLA_VAL_WIDTH).astype(x.dtype)
    return (o * jax.nn.silu(r)) @ w_out

def sqrelu_mlp(x, w1, w2):
    return jnp.square(jax.nn.relu(x @ w1)) @ w2

def second_inputs(seed: int = 0) -> dict:
    key = jax.random.key(seed)
    ks = jax.random.split(key, 24)

    def nrm(k, shape, scale):
        return jax.random.normal(k, shape, jnp.float32) * scale

    DH = NSA_HEAD_DIM
    return {
        "x": nrm(ks[0], (BATCH, SEQ, D_MODEL), 1.0),
        "a_w_in": nrm(ks[1], (N_EVEN, D_MODEL, A_IN), D_MODEL ** -0.5),
        "a_cmp_pos": nrm(ks[2], (N_EVEN, 2, CMP_BLOCK, DH), 0.1),
        "a_cmp_w1": nrm(ks[3], (N_EVEN, 2, CMP_BLOCK * DH, DH), (CMP_BLOCK * DH) ** -0.5),
        "a_cmp_b1": nrm(ks[4], (N_EVEN, 2, DH), 0.02),
        "a_cmp_w2": nrm(ks[5], (N_EVEN, 2, DH, DH), DH ** -0.5),
        "a_pool_w": nrm(ks[6], (N_EVEN, POOL_GROUPS, POOL_GROUP_DIM, POOL_GROUP_DIM), POOL_GROUP_DIM ** -0.5),
        "a_pool_scale": 1.0 + nrm(ks[7], (N_EVEN, POOL_WIDTH), 0.1),
        "a_w_out": nrm(ks[8], (N_EVEN, D_MODEL, D_MODEL), BETA * D_MODEL ** -0.5),
        "c_w_in": nrm(ks[9], (N_ODD, D_MODEL, C_IN), D_MODEL ** -0.5),
        "c_gate_w2": nrm(ks[10], (N_ODD, GLA_GATE_RANK, GLA_KEY_WIDTH), GLA_GATE_RANK ** -0.5),
        "c_gate_b": nrm(ks[11], (N_ODD, GLA_KEY_WIDTH), 0.1),
        "c_norm_g": 1.0 + nrm(ks[12], (N_ODD, GLA_DV), 0.1),
        "c_w_out": nrm(ks[13], (N_ODD, D_MODEL, D_MODEL), BETA * D_MODEL ** -0.5),
        "ln1_g": 1.0 + nrm(ks[14], (DEPTH_2, D_MODEL), 0.05),
        "ln1_b": nrm(ks[15], (DEPTH_2, D_MODEL), 0.02),
        "ln2_g": 1.0 + nrm(ks[16], (DEPTH_2, D_MODEL), 0.05),
        "ln2_b": nrm(ks[17], (DEPTH_2, D_MODEL), 0.02),
        "mlp_w1": nrm(ks[18], (DEPTH_2, D_MODEL, D_FF_2), D_MODEL ** -0.5),
        "mlp_w2": nrm(ks[19], (DEPTH_2, D_FF_2, D_MODEL), BETA * D_FF_2 ** -0.5),
    }

def second_block(x, a_w_in, a_cmp_pos, a_cmp_w1, a_cmp_b1, a_cmp_w2, a_pool_w, a_pool_scale,
              a_w_out, c_w_in, c_gate_w2, c_gate_b, c_norm_g, c_w_out,
              ln1_g, ln1_b, ln2_g, ln2_b, mlp_w1, mlp_w2):
    for i in range(DEPTH_2):
        j = i // 2
        if i % 2 == 0:
            mix = nsa_pool_mixer(x, a_w_in[j], a_cmp_pos[j], a_cmp_w1[j], a_cmp_b1[j],
                                 a_cmp_w2[j], a_pool_w[j], a_pool_scale[j], a_w_out[j])
        else:
            mix = gla_mixer(x, c_w_in[j], c_gate_w2[j], c_gate_b[j], c_norm_g[j], c_w_out[j])
        x = layer_norm(ALPHA * x + mix, ln1_g[i], ln1_b[i])
        x = layer_norm(ALPHA * x + sqrelu_mlp(x, mlp_w1[i], mlp_w2[i]), ln2_g[i], ln2_b[i])
    return x


def setup_inputs(seed=0):
    out = dict(first_inputs(seed))
    for name, value in second_inputs(seed + 1).items():
        if name != "x":
            out[name + "_2"] = value
    return out


def reference(
    x, mem, norm_mix_g, w_in, b_igate, b_fgate, ln_a_g, ln_a_b, w_s, b_s, conv_b_w, conv_b_b,
    gn_b_g, gn_b_b, conv_c_w, conv_c_b, w_q_c, w_k_c, w_v_c, hn_c_g, skip_c, w_out, norm_x_g,
    norm_mem_g, w_xq, w_xkv, w_xo, norm_ffn_g, w_up, conv_f_w, conv_f_b, w_down, final_g,
    a_w_in_2, a_cmp_pos_2, a_cmp_w1_2, a_cmp_b1_2, a_cmp_w2_2, a_pool_w_2, a_pool_scale_2,
    a_w_out_2, c_w_in_2, c_gate_w2_2, c_gate_b_2, c_norm_g_2, c_w_out_2, ln1_g_2, ln1_b_2,
    ln2_g_2, ln2_b_2, mlp_w1_2, mlp_w2_2,
):
    x = first_block(
        x, mem, norm_mix_g, w_in, b_igate, b_fgate, ln_a_g, ln_a_b, w_s, b_s, conv_b_w,
        conv_b_b, gn_b_g, gn_b_b, conv_c_w, conv_c_b, w_q_c, w_k_c, w_v_c, hn_c_g, skip_c,
        w_out, norm_x_g, norm_mem_g, w_xq, w_xkv, w_xo, norm_ffn_g, w_up, conv_f_w, conv_f_b,
        w_down, final_g,
    )
    return second_block(
        x, a_w_in_2, a_cmp_pos_2, a_cmp_w1_2, a_cmp_b1_2, a_cmp_w2_2, a_pool_w_2,
        a_pool_scale_2, a_w_out_2, c_w_in_2, c_gate_w2_2, c_gate_b_2, c_norm_g_2, c_w_out_2,
        ln1_g_2, ln1_b_2, ln2_g_2, ln2_b_2, mlp_w1_2, mlp_w2_2,
    )


_drawn_inputs = setup_inputs


def setup_inputs(seed=0):
    import zlib

    import numpy as np

    out = dict(_drawn_inputs(seed))
    spreads = {}
    factors = {'b_igate': 64.0,
     'ln_a_g': 8.0,
     'ln_a_b': 8.0,
     'conv_b_b': 4.263,
     'gn_b_g': 8.0,
     'gn_b_b': 8.0,
     'conv_c_b': 3.972,
     'hn_c_g': 7.498,
     'skip_c': 8.0,
     'norm_x_g': 8.0,
     'norm_mem_g': 8.0,
     'norm_ffn_g': 4.052,
     'conv_f_b': 5.231,
     'a_cmp_pos_2': 7.066,
     'a_cmp_b1_2': 39.956,
     'c_gate_b_2': 5.258}
    for name, (base, spread) in spreads.items():
        noise = np.random.default_rng([zlib.crc32(name.encode()), seed]).standard_normal(out[name].shape)
        drawn = base * np.exp(spread * noise) if base else spread * noise
        out[name] = __import__('jax').numpy.asarray(drawn.astype(out[name].dtype))
    for name, factor in factors.items():
        out[name] = (out[name] * factor).astype(out[name].dtype)
    return out
```

```python
from contextlib import ExitStack

import numpy as np

import concourse.bass as bass
from concourse import mybir

F32 = mybir.dt.float32
F32R = mybir.dt.float32r
ACT = mybir.ActivationFunctionType
ALU = mybir.AluOpType
AX = mybir.AxisListType

P = 128
D = 1024
S = 512
MEM = 256
KC = D // P
TB = S // P
DFF = 2816
FC = DFF // P
HID = 4096
GROUPS = HID // P // KC
CONV_B, CONV_C, CONV_F = 31, 4, 3
RING = 4
TILE = KC * P
RMS_EPS, LN_EPS = 1e-6, 1e-5
ALPHA = 4.0 ** 0.25
N_CMP, CMP_BLOCK, CMP_STRIDE = 31, 32, 16
GLA_CHUNK = 64
NEG = -1e30

GLU_GROUPS = [8, 8, 6]
STAGES = [("mix_in", 17), ("mem_kv", 16), ("mix_out", 8), ("xq", 8), ("xo", 8),
          ("glu0", 24), ("glu1", 24), ("glu2", 20),
          ("nsa_in", 15), ("nsa_out", 8), ("mlp_a", 64), ("gla_in", 25), ("gla_out", 8), ("mlp_b", 64)]
START, END = {}, {}
_at = 0
for _name, _n in STAGES:
    START[_name], END[_name] = _at, _at + _n
    _at += _n
N_TILES = _at

NORMS = ["mem", "mix", "xat", "ffn", "fin", "ln1a", "ln2a", "ln1b", "ln2b"]
LAYER_NORMS = NORMS[5:]


def chunks_before(name):
    return KC * NORMS.index(name)


PARAMS = [("norm_mix_g", 8), ("norm_x_g", 8), ("norm_mem_g", 8), ("norm_ffn_g", 8), ("final_g", 8),
          ("ln1_g", 16), ("ln1_b", 16), ("ln2_g", 16), ("ln2_b", 16),
          ("conv_b_w", 2 * CONV_B), ("conv_b_b", 2), ("gn_b_g", 2), ("gn_b_b", 2),
          ("conv_c_w", 4 * CONV_C), ("conv_c_b", 4), ("hn_c_g", 4), ("skip_c", 4),
          ("conv_f_w", FC * CONV_F), ("conv_f_b", FC), ("pool_scale", 4), ("cmp_b1", 2), ("cmp_pos", 64),
          ("gate_b", 4), ("gla_g", 2), ("b_igate", 1), ("b_fgate", 1)]
CONSTS = [("ident", P), ("tri01", P), ("causal_neg", P), ("avg64", P), ("avg128", P), ("ones", P),
          ("den_sel", 16), ("row_sel", 4 * P)]
SMALL1 = [("wqkv", 12 * P), ("wsT", 4 * P), ("ln_a_g", 256), ("ln_a_b", 256), ("b_s", 4 * P)]
SMALL2 = [("gate_w2", 512), ("pool_w", 512), ("cmp_w2", 256), ("cmp_neg", 512), ("cmp01", 512),
          ("keep", 512), ("gla01", 256), ("pool_inv", 64)]


def columns(table):
    at, out = 0, {}
    for name, n in table:
        out[name] = (at, n)
        at += n
    return out, at


def tile_of(w, k0, kc, cols):
    out = np.zeros((P, KC, P), np.float32)
    block = w[k0 * P:(k0 + kc) * P, cols]
    out[:, :kc, :block.shape[1]] = block.reshape(kc, P, block.shape[1]).transpose(1, 0, 2)
    return out.reshape(P, TILE)


def chunk(c):
    return slice(c * P, (c + 1) * P)


def weight_stream(i):
    w_in, w_up, w_down = i["w_in"][0], i["w_up"][0], i["w_down"][0]
    a_in, c_in = i["a_w_in_2"][0], i["c_w_in_2"][0]
    tiles = []

    def add(w, cols, k0=0, kc=KC):
        tiles.append(tile_of(w, k0, kc, cols))

    def add_wide(w, width):
        per = TILE // width
        for k0 in range(0, KC, per):
            tiles.append(w[k0 * P:(k0 + per) * P].reshape(per, P, width).transpose(1, 0, 2).reshape(P, TILE))

    gates = np.zeros((D, P), np.float32)
    gates[:, 0:4], gates[:, 32:36] = w_in[:, 2048:2052], w_in[:, 2052:2056]
    add(gates, slice(0, P))
    for c in [8, 9, 10, 11, 4, 5, 6, 7, 12, 13, 14, 15]:
        add(w_in, chunk(c))
    add_wide(w_in[:, 256:512], 256)
    for c in (0, 1):
        add(w_in, chunk(c))
    for c in range(KC):
        add(i["w_xkv"][0], chunk(c))
    for half in range(2):
        add_wide(i["w_xkv"][0][:, D + half * 512:D + (half + 1) * 512], 512)
    for name in ("w_out", "w_xq", "w_xo"):
        for c in range(KC):
            add(i[name][0], chunk(c))
    f0 = 0
    for n in GLU_GROUPS:
        for f in range(f0, f0 + n):
            add(w_up, chunk(f))
            add(w_up, chunk(FC + f))
        for c in range(KC):
            add(w_down, chunk(c), f0, n)
        f0 += n
    add(a_in, slice(1280, 1304))
    for c in (0, 1, 2, 4):
        add(a_in, slice(512 + c * P, 512 + (c + 1) * P))
    add_wide(np.concatenate([a_in[:, 512 + c * P:512 + (c + 1) * P] for c in (3, 5)], axis=1), 256)
    order = np.arange(512).reshape(2, 4, 64).transpose(1, 0, 2).reshape(512)
    q = a_in[:, :512].reshape(D, 2, 4, 64).transpose(0, 2, 1, 3).reshape(D, 512)
    for c in range(4):
        add(q, chunk(c))
    for c in range(4):
        add(a_in, slice(1304 + c * P, 1304 + (c + 1) * P))
    a_out = i["a_w_out_2"][0]
    a_out = np.concatenate([a_out[:512].reshape(2, 4, 64, D).transpose(1, 0, 2, 3).reshape(512, D), a_out[512:]])
    for c in range(KC):
        add(a_out, chunk(c))

    def mlp(layer):
        for g in range(GROUPS):
            for j in range(KC):
                add(i["mlp_w1_2"][layer], chunk(g * KC + j))
            for c in range(KC):
                add(i["mlp_w2_2"][layer], chunk(c), g * KC, KC)

    mlp(0)
    add(c_in, slice(3072, 3088))
    for c in range(8):
        add(c_in, chunk(c))
    for half in range(2):
        add_wide(c_in[:, D + half * 512:D + (half + 1) * 512], 512)
    for c in range(16, 24):
        add(c_in, chunk(c))
    for c in range(KC):
        add(i["c_w_out_2"][0], chunk(c))
    mlp(1)
    return np.stack(tiles)


def by_feature(v):
    v = np.asarray(v)
    v = v.reshape(-1, v.shape[-1] // P, P)
    return v.transpose(2, 0, 1).reshape(P, -1)


def pack(table, values):
    where, width = columns(table)
    out = np.zeros((P, width), np.float32)
    for name, (at, n) in where.items():
        v = np.asarray(values[name])
        out[:v.shape[0], at:at + n] = v.reshape(v.shape[0], n)
    return out


def params(i):
    col4 = lambda v: v[0][:, None]
    return pack(PARAMS, {
        "norm_mix_g": by_feature(i["norm_mix_g"][0]), "norm_x_g": by_feature(i["norm_x_g"][0]),
        "norm_mem_g": by_feature(i["norm_mem_g"][0]), "norm_ffn_g": by_feature(i["norm_ffn_g"][0]),
        "final_g": by_feature(i["final_g"]),
        "ln1_g": by_feature(i["ln1_g_2"]), "ln1_b": by_feature(i["ln1_b_2"]),
        "ln2_g": by_feature(i["ln2_g_2"]), "ln2_b": by_feature(i["ln2_b_2"]),
        "conv_b_w": by_feature(i["conv_b_w"][0]), "conv_b_b": by_feature(i["conv_b_b"][0]),
        "gn_b_g": by_feature(i["gn_b_g"][0]), "gn_b_b": by_feature(i["gn_b_b"][0]),
        "conv_c_w": by_feature(i["conv_c_w"][0]), "conv_c_b": by_feature(i["conv_c_b"][0]),
        "hn_c_g": by_feature(i["hn_c_g"][0]), "skip_c": by_feature(i["skip_c"][0]),
        "conv_f_w": by_feature(i["conv_f_w"][0]), "conv_f_b": by_feature(i["conv_f_b"][0]),
        "pool_scale": by_feature(i["a_pool_scale_2"][0]),
        "cmp_b1": np.concatenate([i["a_cmp_b1_2"][0].T] * 2),
        "cmp_pos": np.concatenate([i["a_cmp_pos_2"][0].transpose(2, 0, 1).reshape(64, 64)] * 2),
        "gate_b": by_feature(i["c_gate_b_2"][0]), "gla_g": by_feature(i["c_norm_g_2"][0]),
        "b_igate": col4(i["b_igate"]), "b_fgate": col4(i["b_fgate"])})


def block_diagonal(w):
    out = np.zeros((P, w.shape[1], P), np.float32)
    out[:64, :, :64] = w
    out[64:, :, 64:] = w
    return out


def shape_constants():
    r = np.arange(P)
    avg64 = (r[:, None] // 64 == r[None, :] // 64) / 64.0
    den_sel = np.zeros((P, 4, 4)); row_sel = np.zeros((4, 4, P))
    for h in range(4):
        den_sel[:, h, h] = 1.0
        row_sel[h, h, :] = 1.0
    return pack(CONSTS, {
        "ident": np.eye(P), "tri01": r[:, None] <= r[None, :],
        "causal_neg": np.where(r[None, :] <= r[:, None], 0.0, NEG),
        "avg64": avg64, "avg128": np.full((P, P), 1.0 / P), "ones": np.ones((P, P)),
        "den_sel": den_sel.reshape(P, 16), "row_sel": row_sel.reshape(4, 4 * P)})


def small1(i):
    wqkv = np.stack([i["w_q_c"][0], i["w_k_c"][0], i["w_v_c"][0]])
    return pack(SMALL1, {
        "wqkv": wqkv.transpose(2, 0, 1, 3).reshape(P, 12 * P),
        "wsT": i["w_s"][0].transpose(2, 0, 1).reshape(P, 4 * P),
        "ln_a_g": np.broadcast_to(i["ln_a_g"][0], (P, 256)), "ln_a_b": np.broadcast_to(i["ln_a_b"][0], (P, 256)),
        "b_s": i["b_s"][0].reshape(1, 4 * P)})


def small2(i):
    t = np.arange(S).reshape(TB, P).T
    seen = (np.arange(N_CMP) * CMP_STRIDE + CMP_BLOCK - 1)[None, None, :] <= t[:, :, None]
    cmp01 = np.zeros((P, TB, 4, 32)); cmp_neg = np.zeros((P, TB, 4, 32))
    cmp01[..., :N_CMP] = seen[:, :, None, :]
    cmp_neg[..., :N_CMP] = np.where(seen, 0.0, NEG)[:, :, None, :]
    pool_inv = np.zeros((P, 4, 16))
    for g in range(4):
        pool_inv[:, g] = 1.0 / np.minimum(np.arange(1, 17), 2 ** (g + 1))
    j = np.arange(P) % GLA_CHUNK
    gla01 = np.broadcast_to((j[:, None] <= np.arange(GLA_CHUNK)[None, :])[:, None, :], (P, TB, GLA_CHUNK))
    return pack(SMALL2, {
        "gate_w2": i["c_gate_w2_2"][0], "pool_w": i["a_pool_w_2"][0].transpose(1, 0, 2).reshape(P, 512),
        "cmp_w2": block_diagonal(i["a_cmp_w2_2"][0].transpose(1, 0, 2)).reshape(P, 256),
        "cmp_neg": cmp_neg.reshape(P, 512), "cmp01": cmp01.reshape(P, 512),
        "keep": np.broadcast_to(np.arange(S) % GLA_CHUNK != 0, (P, S)),
        "gla01": gla01.reshape(P, 256), "pool_inv": pool_inv.reshape(P, 64)})


def memory_map(nc):
    m = {}
    at = 16512

    def place(name, shape, dtype, offset):
        m[name] = nc.alloc_sbuf_tensor_at(name, [P] + shape, dtype, offset=offset, align_bytes=4)[:]

    def region(nbytes):
        nonlocal at
        start = at
        at += nbytes
        return start

    def fill(start, table):
        for name, shape in table:
            place(name, shape, F32, start)
            start += 4 * int(np.prod(shape))
        return start

    ring = region(4 * RING * TILE)
    place("raw", [RING, TILE], F32, ring)
    place("w_hi", [RING, KC, P], F32R, region(4 * RING * TILE))
    place("w_lo", [RING, KC, P], F32R, region(4 * RING * TILE))
    place("h", [KC, S], F32, region(4 * KC * S))
    x = region(8 * KC * S)
    place("x_hi", [KC, S], F32R, x)
    place("x_lo", [KC, S], F32R, x + 4 * KC * S)
    y = region(8 * KC * S)
    place("y_hi", [KC, S], F32R, y)
    place("y_lo", [KC, S], F32R, y + 4 * KC * S)
    place("z", [RING, S], F32, region(4 * RING * S))
    place("const", [columns(CONSTS)[1]], F32, region(4 * columns(CONSTS)[1]))
    place("par", [columns(PARAMS)[1]], F32, region(4 * columns(PARAMS)[1] + 8))
    small = region(4 * columns(SMALL2)[1])
    place("small1", [columns(SMALL1)[1]], F32, small)
    place("small2", [columns(SMALL2)[1]], F32, small)
    arena = fill(at, [("sq", [2, S]), ("xt", [2, S]), ("rstd", [S]), ("mean", [S])])
    end = nc.sbuf_usable_end

    a = fill(arena, [("mem_k", [KC, MEM]), ("mem_v", [2, D])])
    place("mem_in", [KC, MEM], F32, arena)
    e = fill(a, [("xc", [4, S + CONV_C - 1]), ("xconv", [4, S]), ("b_in", [2, S + CONV_B - 1]), ("v_tok", [TB, 256]),
                 ("v_stats", [TB, 6]), ("v_mv", [TB, 2]), ("v_rstd", [TB]), ("g_col", [TB, 4])])
    assert e <= end, (e, end)
    fill(x, [("row_t", [S]), ("row_F", [S]), ("row_M", [S]), ("row_em", [S]), ("row_den", [S]),
             ("q_c", [S]), ("k_c", [S]), ("v_c", [TB, P]), ("w_c", [TB, S]), ("p_c", [TB, S])])
    place("mn_hi", [KC, MEM], F32R, y)
    place("mn_lo", [KC, MEM], F32R, y + 4 * KC * MEM)
    place("cell", [4, S], F32, y + 4 * 4 * S)
    place("u_a", [2, S], F32, y + 4 * 8 * S)
    place("conv_b", [2, S], F32, y + 4 * 10 * S)
    place("oc_gate", [4, S], F32, y + 4 * 12 * S)
    place("q_x", [KC, S], F32, a)
    e = fill(a + 4 * KC * S, [("xa_neg", [4]), ("xa_sum", [4]), ("xa_max", [4])])
    assert e <= end
    fill(x, [("p_x", [2, TB, MEM]), ("pt_x", [2, S])])
    fill(arena, [("g_in", [2, S + CONV_F - 1]), ("g_act", [2, S])])
    e = fill(arena, [("k_cmp", [2, S]), ("blocks", [2, N_CMP, CMP_BLOCK]), ("k_br", [2, S]), ("v_br", [2, TB, P]),
                     ("q_n", [4, S]), ("u_n", [4, S + 16]), ("gate_f", [S]), ("gate_t", [TB, 24]), ("hid_c", [2, 32]),
                     ("kc", [32]), ("vc", [P]), ("n_max", [2, TB]), ("n_neg", [2, TB]), ("n_sum", [2, TB]),
                     ("n_r", [2, TB]), ("c_mx", [16]), ("c_sum", [16])])
    assert e <= end, (e, end)
    place("pool_s", [2, S + 16], F32, arena + 4 * 2 * S)
    fill(x, [("p_n", [2, TB, S]), ("pt_n", [TB, S])])
    place("e_c", [2, 16, 32], F32, x)
    place("w_cmp", [2, CMP_BLOCK, P], F32, y)
    place("pct0", [4, S], F32, y + 4 * 4 * S)
    place("pct1", [4, S], F32, y + 4 * 12 * S)
    e = fill(arena, [("a_g", [S]), ("q_g", [4, S]), ("k_g", [4, S]), ("v_g", [TB, D]), ("gz", [S]), ("gt", [S]),
                     ("gb", [S]), ("decay", [4, 8])])
    assert e <= end, (e, end)
    place("kt_g", [4, S], F32, y + 4 * 4 * S)
    place("r_g", [KC, S], F32, y + 4 * 8 * S)
    fill(x, [("att_g", [TB, GLA_CHUNK]), ("kd_tok", [TB, P]), ("state", [8, 256]), ("o_g", [2, S])])
    return m


class Program:

    def __init__(self, nc, ctx, dram):
        self.nc, self.ctx, self.dram = nc, ctx, dram
        self.m = memory_map(nc)
        self.acc = ctx.enter_context(nc.psum_tensor("acc", [P, RING, 512], F32))[:]
        self.misc = ctx.enter_context(nc.psum_tensor("misc", [P, 4, 512], F32))[:]
        self.sems = {}
        self.tables = [(self.m["const"], columns(CONSTS)[0]), (self.m["par"], columns(PARAMS)[0]),
                       (self.m["small1"], columns(SMALL1)[0]), (self.m["small2"], columns(SMALL2)[0])]

    def sem(self, name):
        if name not in self.sems:
            self.sems[name] = self.ctx.enter_context(self.nc.semaphore(name))
        return self.sems[name]

    def view(self, name):
        for tensor, where in self.tables:
            if name in where:
                at, n = where[name]
                return tensor[:, at:at + n]
        raise KeyError(name)

    def col(self, name, c, rows=P):
        return self.view(name)[0:rows, c:c + 1]


class Own:

    def __init__(self, engine, sem, base=0):
        self.engine, self.sem, self.base, self.n = engine, sem, base, 0

    def mark(self, instruction):
        instruction.then_inc(self.sem, 1)
        self.n += 1
        return self.n

    def settle(self, n=None):
        self.engine.wait_ge(self.sem, self.base + (self.n if n is None else n))

    def link(self, instruction):
        self.mark(instruction)
        self.settle()


def blk(b, n=P):
    return slice(b * n, (b + 1) * n)


def bf(ap):
    return ap.bitcast(F32)


def tensor_program(pr, pe):
    nc, m, acc, misc, sem = pr.nc, pr.m, pr.acc, pr.misc, pr.sem
    mm, turn = nc.tensor.matmul, nc.tensor.transpose
    ident, ones = pr.view("ident"), pr.view("ones")
    x_hi, x_lo, y_hi, y_lo = m["x_hi"], m["x_lo"], m["y_hi"], m["y_lo"]

    def claim(t):
        pe.wait_ge(sem("weights_split"), t + 1)
        if not isinstance(t, int) or t >= RING:
            pe.wait_ge(sem("tile_out"), t - RING + 1)

    def dense(t, slot, hi, lo, kc=KC, n=S, norm=None, ready=None, first=1):
        if norm:
            ready, first = "norm_ready", chunks_before(norm) + 1
        claim(t)
        out = acc[:, slot, 0:n]
        for k in range(kc):
            if ready:
                pe.wait_ge(sem(ready), first + k)
            mm(out, m["w_hi"][:, slot, k], hi[:, k, 0:n], start=k == 0, stop=False)
            mm(out, m["w_hi"][:, slot, k], lo[:, k, 0:n], start=False, stop=False)
            last = mm(out, m["w_lo"][:, slot, k], hi[:, k, 0:n], start=False, stop=k == kc - 1)
        last.then_inc(sem("tile_done"), 1)

    def tokens(t0, width, hi, lo, blocks):
        per = TILE // width
        tiles = KC // per
        pe.wait_ge(sem("tile_out"), t0)
        for j in range(tiles):
            claim(t0 + j)
            w_hi, w_lo = (m[w][:, (t0 + j) % RING].rearrange("p k n -> p (k n)") for w in ("w_hi", "w_lo"))
            for b in range(blocks):
                per_bank = 512 // width
                first, final = b % per_bank == 0, b % per_bank == per_bank - 1
                out = acc[:, (t0 + b // per_bank) % RING, blk(b % per_bank, width)]
                for i in range(per):
                    k = j * per + i
                    mm(out, hi[:, k, blk(b)], w_hi[:, blk(i, width)], start=k == 0 and first, stop=False)
                    mm(out, hi[:, k, blk(b)], w_lo[:, blk(i, width)], start=False, stop=False)
                    last = mm(out, lo[:, k, blk(b)], w_hi[:, blk(i, width)], start=False,
                              stop=k == KC - 1 and final)
            last.then_inc(sem("tile_done"), 1)

    def stage(name, hi, lo, n, at=0, width=S, norm=None, ready=None):
        for i in range(n):
            t = START[name] + at + i
            dense(t, t % RING, hi, lo, n=width, norm=norm if i == 0 else None, ready=ready if i == 0 else None)

    def sum_squares(name, n=S):
        for k in range(KC):
            pe.wait_ge(sem("norm_sq"), chunks_before(name) + k + 1)
            mm(misc[:, 1, 0:n], ones, m["sq"][:, k % 2, 0:n], start=k == 0, stop=k == KC - 1)\
                .then_inc(sem("norm_summed"), 1)

    def sum_features(name, resid, first):
        for k in range(KC):
            pe.wait_ge(sem(resid), first + k)
            last = mm(misc[:, 0, :], ones, m["h"][:, k], start=k == 0, stop=k == KC - 1)
        last.then_inc(sem("ln_mean"), 1)

    pe.wait_ge(sem("const_in"), 16)
    sum_squares("mem", MEM)
    sum_squares("mix")
    stage("mix_in", x_hi, x_lo, 13, norm="mix")
    tokens(13, 256, x_hi, x_lo, TB)
    stage("mix_in", x_hi, x_lo, 2, at=15)
    pe.wait_ge(sem("norm_ready"), KC)
    stage("mem_kv", m["mn_hi"], m["mn_lo"], 8, width=MEM)
    for half in range(2):
        tokens(START["mem_kv"] + 8 + 4 * half, 512, m["mn_hi"], m["mn_lo"], MEM // P)

    ws = pr.view("wsT").rearrange("p (h t) -> p h t", h=4)
    b_s = pr.view("b_s")
    pe.wait_ge(sem("small1_in"), 16)
    pe.wait_ge(sem("v_a_ready"), 1)
    for c in range(2):
        for tb in range(TB):
            for hh in range(2):
                head = 2 * c + hh
                out = misc[blk(hh, 64), c, blk(tb)]
                mm(out, m["v_tok"][:, tb, blk(head, 64)], ws[:, head], start=True, stop=False)
                last = mm(out, ones[0:1, 0:64], b_s[0:1, blk(head)], start=False, stop=True)
        last.then_inc(sem("gating"), 1)

    pe.wait_ge(sem("rows"), 2)
    for sb in range(TB):
        last = turn(misc[:, 3, blk(sb, 4)], m["z"][0:4, 0, blk(sb)], ident[0:4, 0:4])
    last.then_inc(sem("g_turned"), 1)

    row_sel = pr.view("row_sel").rearrange("p (h n) -> p h n", h=4)
    den_sel = pr.view("den_sel").rearrange("p (h n) -> p h n", h=4)
    wqkv = pr.view("wqkv").rearrange("p (x h e) -> p x h e", x=3, h=4)

    def std_mean(i, src, avg, ready, count):
        pe.wait_ge(sem(ready), count)
        if i >= 2:
            pe.wait_ge(sem("std_centred"), i - 1)
        mm(misc[:, i % 2, :], pr.view(avg), src, start=True, stop=True).then_inc(sem("std_mean"), 1)

    def std_var(i, avg):
        pe.wait_ge(sem("std_sq"), i + 1)
        if i >= 2:
            pe.wait_ge(sem("std_rstd"), i - 1)
        mm(misc[:, 2 + i % 2, :], pr.view(avg), m["sq"][:, i % 2], start=True, stop=True)\
            .then_inc(sem("std_var"), 1)

    pe.wait_ge(sem("y_ready"), 2)
    pe.wait_ge(sem("g_col"), 1)
    for c in range(2):
        std_mean(c, m["conv_b"][:, c], "avg64", "conv_b", c + 1)
    for c in range(2):
        std_var(c, "avg64")
    pe.wait_ge(sem("std_rstd"), 2)

    for head in range(4):
        pe.wait_ge(sem("xconv"), head + 1)
        if head:
            pe.wait_ge(sem("p_c"), 4 * head)
            pe.wait_ge(sem("cell_out"), head)
            pe.wait_ge(sem("den_added"), head)
        xconv = m["xconv"][:, head]
        mm(misc[:, 0, :], wqkv[:, 0, head], xconv, start=True, stop=True).then_inc(sem("qkv"), 1)
        mm(misc[:, 1, :], wqkv[:, 1, head], xconv, start=True, stop=True).then_inc(sem("qkv"), 1)
        for tb in range(TB):
            at = CONV_C - 1 + tb * P
            last = mm(misc[:, 2, blk(tb)], m["xc"][:, head, at:at + P], wqkv[:, 2, head], start=True, stop=True)
        last.then_inc(sem("qkv"), 1)
        pe.wait_ge(sem("rows"), 3)
        mm(misc[:, 3, :], row_sel[0:4, head], m["row_M"][0:4], start=True, stop=True).then_inc(sem("M_spread"), 1)
        pe.wait_ge(sem("qkv_out"), 3 * head + 3)

        def scores(sb):
            mm(misc[:, sb % 2, sb * P:S], m["k_c"][:, blk(sb)], m["q_c"][:, sb * P:S], start=True, stop=True)\
                .then_inc(sem("scores_c"), 1)

        scores(0)
        scores(1)
        for sb in range(TB):
            pe.wait_ge(sem("p_c"), 4 * head + sb + 1)
            p = m["p_c"][:, sb, sb * P:S]
            mm(misc[:, 2, sb * P:S], m["v_c"][:, sb], p, start=sb == 0, stop=sb == TB - 1)
            last = mm(misc[0:4, 3, sb * P:S], den_sel[:, head], p, start=sb == 0, stop=sb == TB - 1)
            if sb + 2 < TB:
                scores(sb + 2)
        last.then_inc(sem("cell_sum"), 1)

    pe.wait_ge(sem("den_ready"), 1)
    for head in range(4):
        if head == 2:
            pe.wait_ge(sem("cell_out"), 4)
        mm(misc[:, head, :], row_sel[0:4, head], m["row_den"][0:4], start=True, stop=True)\
            .then_inc(sem("den_spread"), 1)
    for i in range(2, 6):
        std_mean(i, m["cell"][:, i - 2], "avg128", "cell_ready", 4)
    for i in range(2, 6):
        std_var(i, "avg128")

    stage("mix_out", y_hi, y_lo, KC, ready="y_ready")
    sum_squares("xat")
    stage("xq", x_hi, x_lo, KC, norm="xat")

    def x_scores(head):
        for tb in range(TB):
            i = 4 * head + tb
            if i == 0:
                pe.wait_ge(sem("tile_out"), END["xq"])
            if i >= 2:
                pe.wait_ge(sem("xa_exp"), i - 1)
            for c in range(2):
                last = mm(misc[:, tb % 2, 0:MEM], m["q_x"][:, 2 * head + c, blk(tb)], m["mem_k"][:, 2 * head + c],
                          start=c == 0, stop=c == 1)
            last.then_inc(sem("xa_scores"), 1)

    x_scores(0)
    for head in range(4):
        if head < 3:
            x_scores(head + 1)
        if head:
            pe.wait_ge(sem("xa_pt"), 2 * head)
        for tb in range(TB):
            pe.wait_ge(sem("xa_p"), 4 * head + tb + 1)
            for mb in range(2):
                last = turn(misc[:, 2 + mb, blk(tb)], m["p_x"][:, head % 2, tb, blk(mb)], ident)
        last.then_inc(sem("xa_turned"), 1)
        pe.wait_ge(sem("xa_pt"), 2 * head + 2)
        for e in range(2):
            c = 2 * head + e
            if head >= 2:
                pe.wait_ge(sem("xa_y"), c - 3)
            for mb in range(2):
                last = mm(acc[:, c % 4, :], m["mem_v"][:, mb, blk(c)], m["pt_x"][:, mb], start=mb == 0, stop=mb == 1)
            last.then_inc(sem("xa_o"), 1)
    pe.wait_ge(sem("xa_y"), KC)
    stage("xo", y_hi, y_lo, KC)

    sum_squares("ffn")

    def glu_group(g, t0, n):
        for j in range(2 * n):
            dense(t0 + j, (START["glu0"] + j) % RING, x_hi, x_lo, norm="ffn" if j == 0 else None)
        for c in range(KC):
            j = 2 * n + c
            dense(t0 + j, (START["glu0"] + j) % RING, y_hi, y_lo, kc=n,
                  ready="glu_hidden" if c == 0 else None, first=8 * g + 1)

    with pe.Fori(0, 2) as g:
        glu_group(g, g * 24 + START["glu0"], 8)
    glu_group(2, START["glu2"], 6)
    sum_squares("fin")

    stage("nsa_in", x_hi, x_lo, 5, norm="fin")
    tokens(START["nsa_in"] + 5, 256, x_hi, x_lo, TB)
    stage("nsa_in", x_hi, x_lo, 8, at=7)
    for tb in range(TB):
        last = turn(misc[:, 2, tb * 32:tb * 32 + 24], m["gate_f"][0:24, blk(tb)], ident[0:24, 0:24])
    last.then_inc(sem("gates_turned"), 1)
    pe.wait_ge(sem("small2_in"), 16)
    pe.wait_ge(sem("w_cmp_in"), 16)
    pe.wait_ge(sem("blocks"), 4)
    for i in range(2):
        for j in range(CMP_BLOCK):
            last = mm(misc[:, 0, i * 32:i * 32 + N_CMP], m["w_cmp"][:, i, j], m["blocks"][:, i, :, j],
                      start=j == 0, stop=j == CMP_BLOCK - 1)
    last.then_inc(sem("cmp_hidden"), 1)
    cmp_w2 = pr.view("cmp_w2").rearrange("p (i e) -> p i e", i=2)
    pe.wait_ge(sem("gate_t"), 1)
    pe.wait_ge(sem("cmp_act"), 2)
    mm(misc[:, 3, 0:N_CMP], cmp_w2[:, 0], m["hid_c"][:, 0, 0:N_CMP], start=True, stop=True)\
        .then_inc(sem("cmp_kv"), 1)
    mm(misc[0:N_CMP, 2, 256:384], m["hid_c"][:, 1, 0:N_CMP], cmp_w2[:, 1], start=True, stop=True)\
        .then_inc(sem("cmp_kv"), 1)
    pe.wait_ge(sem("cmp_kv_out"), 2)
    pe.wait_ge(sem("tile_out"), START["nsa_in"] + 11)
    for g in range(2):
        for tb in range(TB):
            for c in range(4):
                at = (tb * 4 + c) * 32
                last = mm(misc[:, g, at:at + N_CMP], m["q_n"][blk(g, 64), c, blk(tb)], m["kc"][blk(g, 64), 0:N_CMP],
                          start=True, stop=True)
        last.then_inc(sem("cmp_scores"), 1)
    pe.wait_ge(sem("cmp_p"), 2)
    for g in range(2):
        for c in range(4):
            if g:
                pe.wait_ge(sem("cmp_pt"), c + 1)
            for tb in range(TB):
                last = turn(misc[0:N_CMP, c, blk(tb)], m["e_c"][:, g, tb * 4 + c, 0:N_CMP], ident)
            last.then_inc(sem("cmp_turned"), 1)
    pe.wait_ge(sem("cmp_pt"), 8)
    pe.wait_ge(sem("tile_out"), END["nsa_in"])

    def n_scores(i, tb):
        c, g, br = i // 4, i // 2 % 2, i % 2
        n = (tb + 1) * P
        if 4 * i + tb >= 2:
            pe.wait_ge(sem("n_exp"), 4 * i + tb - 1)
        mm(acc[:, tb % 2, 0:n], m["q_n"][blk(g, 64), c, blk(tb)], m["k_br"][blk(g, 64), br, 0:n], start=True, stop=False)
        mm(acc[:, tb % 2, tb * P:n], ident, pr.view("causal_neg"), start=False, stop=True)\
            .then_inc(sem("n_scores"), 1)

    for tb in range(TB):
        n_scores(0, tb)
    for i in range(16):
        c, g, br = i // 4, i // 2 % 2, i % 2
        if i < 15:
            n_scores(i + 1, 0)
            n_scores(i + 1, 1)
        pe.wait_ge(sem("n_p"), 4 * i + 4)
        for sb in range(TB):
            for tb in range(sb, TB):
                last = turn(misc[:, sb, blk(tb)], m["p_n"][:, i % 2, tb, blk(sb)], ident)
            last.then_inc(sem("n_turned"), 1)
        if i < 15:
            n_scores(i + 1, 2)
            n_scores(i + 1, 3)
        out = acc[blk(g, 64), 2 + c % 2]
        if br == 0:
            if c >= 2 and g == 0:
                pe.wait_ge(sem("n_y"), c - 1)
            mm(out, m["vc"][0:N_CMP, blk(g, 64)], m["pct%d" % g][0:N_CMP, c], start=True, stop=False)
        for sb in range(TB):
            pe.wait_ge(sem("n_pt"), 4 * i + sb + 1)
            last = mm(out[:, sb * P:S], m["v_br"][:, br, sb, blk(g, 64)], m["pt_n"][:, sb, sb * P:S],
                      start=False, stop=br == 1 and sb == TB - 1)
        last.then_inc(sem("n_o"), 1)
    pool_w = pr.view("pool_w").rearrange("p (g n) -> p g n", g=4)
    pe.wait_ge(sem("pool_r"), 4)
    for g in range(4):
        mm(misc[:, g, :], pool_w[:, g], m["u_n"][:, g, 16:], start=True, stop=True).then_inc(sem("pool_o"), 1)
    pe.wait_ge(sem("n_y"), KC)
    stage("nsa_out", y_hi, y_lo, KC)

    def layer_norm(name, resid, first):
        sum_features(name, resid, first)
        sum_squares(name)

    def mlp(name, norm, hidden):
        with pe.Fori(0, GROUPS) as g:
            t0 = g * 16 + START[name]
            for j in range(16):
                slot = (START[name] + j) % RING
                if j < 8:
                    dense(t0 + j, slot, x_hi, x_lo, norm=norm if j == 0 else None)
                else:
                    dense(t0 + j, slot, y_hi, y_lo, ready=hidden if j == 8 else None, first=g * 8 + 1)

    layer_norm("ln1a", "nsa_resid", 1)
    mlp("mlp_a", "ln1a", "mlp_a_hidden")
    layer_norm("ln2a", "mlp_a_resid", 8 + 8 * (GROUPS - 1) + 1)

    stage("gla_in", x_hi, x_lo, 9, norm="ln2a")
    gate_w2 = pr.view("gate_w2").rearrange("p (h n) -> p h n", h=4)
    pe.wait_ge(sem("tile_out"), START["gla_in"] + 1)
    for head in range(4):
        mm(misc[:, head, :], gate_w2[0:16, head], m["a_g"][0:16], start=True, stop=True).then_inc(sem("gla_z"), 1)
    for half in range(2):
        tokens(START["gla_in"] + 9 + 4 * half, 512, x_hi, x_lo, TB)
    stage("gla_in", x_hi, x_lo, 8, at=17)

    def gla_local(head):
        pe.wait_ge(sem("gla_k"), head + 1)
        if head:
            pe.wait_ge(sem("gla_att"), head)
            pe.wait_ge(sem("gla_kd"), head)
        for n in range(8):
            last = mm(misc[blk(n % 2, 64), 0, blk(n // 2, 64)], m["kt_g"][:, head, blk(n, 64)],
                      m["q_g"][:, head, blk(n, 64)], start=True, stop=True)
        last.then_inc(sem("gla_scores"), 1)
        for tb in range(TB):
            last = turn(misc[:, 3, blk(tb)], m["k_g"][:, head, blk(tb)], ident)
        last.then_inc(sem("gla_turned"), 1)
        pe.wait_ge(sem("gla_kd"), head + 1)
        for n in range(7):
            i = 7 * head + n
            if i >= 2:
                pe.wait_ge(sem("gla_state"), i - 1)
            mm(misc[:, 1 + i % 2, 0:256], m["kd_tok"][blk(n % 2, 64), n // 2], m["v_g"][blk(n % 2, 64), n // 2, blk(head, 256)],
               start=True, stop=True).then_inc(sem("gla_update"), 1)

    def gla_out(head):
        pe.wait_ge(sem("gla_att"), head + 1)
        pe.wait_ge(sem("gla_state"), 7 * head + 7)
        if head:
            pe.wait_ge(sem("gla_rstd"), head)
        for n in range(8):
            for e in range(2):
                at = e * 256 + n // 2 * 64
                out = acc[:, 2 * (head % 2) + n % 2, at:at + 64]
                mm(out, m["v_g"][blk(n % 2, 64), n // 2, head * 256 + e * P:head * 256 + (e + 1) * P],
                   m["att_g"][blk(n % 2, 64), n // 2], start=True, stop=False)
                last = mm(out, m["state"][:, n, blk(e)], m["q_g"][:, head, blk(n, 64)], start=False, stop=True)
        last.then_inc(sem("gla_o"), 1)

    def gla_sum(head):
        for e in range(2):
            pe.wait_ge(sem("gla_sq"), 2 * head + 2)
            last = mm(acc[:, 2 * ((head + 1) % 2), :], ones, m["sq"][:, e], start=e == 0, stop=e == 1)
        last.then_inc(sem("gla_ss"), 1)

    gla_local(0)
    pe.wait_ge(sem("tile_out"), END["gla_in"])
    for head in range(4):
        gla_out(head)
        gla_sum(head)
        if head < 3:
            gla_local(head + 1)
    pe.wait_ge(sem("gla_y"), KC)
    stage("gla_out", y_hi, y_lo, KC)
    layer_norm("ln1b", "gla_resid", 1)
    mlp("mlp_b", "ln1b", "mlp_b_hidden")
    layer_norm("ln2b", "mlp_b_resid", 8 + 8 * (GROUPS - 1) + 1)


def scalar_program(pr, act):
    nc, m, acc, misc, sem = pr.nc, pr.m, pr.acc, pr.misc, pr.sem
    f = nc.scalar.activation
    z = m["z"]
    own = Own(act, sem("act_step"))

    def out(t, slot, dst, func=ACT.Copy, src=None, **more):
        act.wait_ge(sem("tile_done"), t + 1)
        f(dst, acc[:, slot] if src is None else src, func, **more).then_inc(sem("tile_out"), 1)

    def out_wide(t, last, dst, func=ACT.Copy, src=None):
        act.wait_ge(sem("tile_done"), last + 1)
        f(dst, acc[:, t % RING] if src is None else src, func).then_inc(sem("tile_out"), 1)

    def rsqrt(dst, src, scale, eps, name):
        own.link(f(dst, src, ACT.Ln, bias=eps, scale=scale))
        f(dst, dst, ACT.Exp, scale=-0.5).then_inc(sem(name), 1)

    def squares(name, src, n=S, ready=None, first=1, eps=RMS_EPS):
        before = chunks_before(name)
        for k in range(KC):
            if ready:
                act.wait_ge(sem(ready), first + k)
            if k >= 2:
                act.wait_ge(sem("norm_summed"), before + k - 1)
            f(m["sq"][:, k % 2, 0:n], src[:, k], ACT.Square).then_inc(sem("norm_sq"), 1)
        act.wait_ge(sem("norm_summed"), before + KC)
        rsqrt(m["rstd"][:, 0:n], misc[:, 1, 0:n], 1.0 / D, eps, "norm_rstd")

    def residual_out(name, resid):
        for k in range(KC):
            t = START[name] + k
            if k >= RING:
                act.wait_ge(sem(resid), k - RING + 1)
            out(t, t % RING, z[:, t % RING])

    act.dma_start(m["small1"], pr.dram["small1"]).then_inc(sem("small1_in"), 16)

    act.wait_ge(sem("mem_in"), 16)
    squares("mem", m["mem_in"], MEM)
    act.wait_ge(sem("x_in"), 16)
    act.wait_ge(sem("norm_ready"), KC)
    squares("mix", m["h"])
    act.wait_ge(sem("par_in"), 16)
    act.wait_ge(sem("tile_done"), 1)
    own.mark(f(z[0:4, 0], acc[0:4, 0], ACT.Identity, bias=pr.col("b_igate", 0, 4)))
    out(0, 0, z[0:4, 1], src=acc[32:36, 0])
    for c in range(4):
        out(1 + c, (1 + c) % RING, m["xc"][:, c, CONV_C - 1:])
    for c in range(2):
        out(5 + c, (5 + c) % RING, m["b_in"][:, c, CONV_B - 1:])
    for c in range(2):
        out(7 + c, (7 + c) % RING, z[:, 2 + c], ACT.Sigmoid)
    for c in range(4):
        out(9 + c, (9 + c) % RING, m["oc_gate"][:, c], ACT.Sigmoid)
    for i in range(2):
        out_wide(13 + i, 14, m["v_tok"][:, 2 * i:2 * i + 2], ACT.Gelu,
                 src=acc[:, (13 + i) % RING].rearrange("p (b n) -> p b n", b=2))
    for c in range(2):
        out(15 + c, (15 + c) % RING, m["u_a"][:, c], ACT.Gelu)
    for c in range(4):
        act.wait_ge(sem("xconv_pre"), c + 1)
        f(m["xconv"][:, c], m["xconv"][:, c], ACT.Silu).then_inc(sem("xconv"), 1)

    fr, rt = z[0:4, 1], m["row_t"][0:4]
    own.link(f(fr, fr, ACT.Identity, bias=pr.col("b_fgate", 0, 4)))
    own.link(f(rt, fr, ACT.Abs))
    own.link(f(rt, rt, ACT.Exp, scale=-1.0))
    f(rt, rt, ACT.Ln, bias=1.0).then_inc(sem("row_ln"), 1)
    act.wait_ge(sem("v_a_stats"), 1)
    rsqrt(m["v_rstd"], m["v_mv"][:, :, 1], 1.0, LN_EPS, "v_a_rstd")
    act.wait_ge(sem("rows"), 4)
    f(m["row_em"][0:4], m["row_em"][0:4], ACT.Exp, scale=-1.0).then_inc(sem("row_em"), 1)

    for c in range(8):
        t = START["mem_kv"] + c
        out(t, t % RING, m["mem_k"][:, c], src=acc[:, t % RING, 0:MEM])
    for half in range(2):
        t = START["mem_kv"] + 8 + 4 * half
        out_wide(t, t + 3, m["mem_v"][:, 0, blk(half, 512)])
        f(m["mem_v"][:, 1, blk(half, 512)], acc[:, (t + 1) % RING], ACT.Copy).then_inc(sem("tile_out"), 3)
    act.wait_ge(sem("g_turned"), 1)
    f(m["g_col"], misc[:, 3, 0:16].rearrange("p (b h) -> p b h", b=TB), ACT.Copy).then_inc(sem("g_col"), 1)

    ring = [m["rstd"], m["mean"]]

    def std(i, src):
        act.wait_ge(sem("std_centred"), i + 1)
        if i >= 2:
            act.wait_ge(sem("std_var"), i - 1)
        f(m["sq"][:, i % 2], src, ACT.Square).then_inc(sem("std_sq"), 1)

    def std_rstd(i):
        act.wait_ge(sem("std_var"), i + 1)
        if i >= 2:
            act.wait_ge(sem("std_scaled"), i - 1)
        rsqrt(ring[i % 2], misc[:, 2 + i % 2, :], 1.0, LN_EPS, "std_rstd")

    for c in range(2):
        std(c, m["conv_b"][:, c])
    for c in range(2):
        std_rstd(c)
    for c in range(2):
        act.wait_ge(sem("std_scaled"), c + 1)
        f(m["conv_b"][:, c], m["conv_b"][:, c], ACT.Silu, scale=pr.col("gn_b_g", c), bias=pr.col("gn_b_b", c))\
            .then_inc(sem("conv_b_act"), 1)

    for head in range(4):
        for x, dst in enumerate((m["q_c"], m["k_c"], m["v_c"])):
            act.wait_ge(sem("qkv"), 3 * head + x + 1)
            src = misc[:, x, :] if x < 2 else misc[:, x, :].rearrange("p (b n) -> p b n", b=TB)
            f(dst, src, ACT.Copy).then_inc(sem("qkv_out"), 1)
        for sb in range(TB):
            act.wait_ge(sem("gap"), 4 * head + sb + 1)
            w = m["w_c"][:, sb, sb * P:]
            f(w, w, ACT.Exp, scale=-1.0).then_inc(sem("w_exp"), 1)
        act.wait_ge(sem("cell_sum"), head + 1)
        f(m["cell"][:, head], misc[:, 2, :], ACT.Copy).then_inc(sem("cell_out"), 1)
    act.wait_ge(sem("den_added"), 4)
    f(m["row_den"][0:4], m["row_den"][0:4], ACT.Abs).then_inc(sem("den_abs"), 1)
    for i in range(2, 6):
        std(i, m["cell"][:, i - 2])
        if i >= 3:
            std_rstd(i - 1)
    std_rstd(5)

    residual_out("mix_out", "mix_resid")
    squares("xat", m["h"], ready="mix_resid")
    for c in range(KC):
        t = START["xq"] + c
        out(t, t % RING, m["q_x"][:, c])

    def x_exp(head):
        for tb in range(TB):
            act.wait_ge(sem("xa_max"), 4 * head + tb + 1)
            if head >= 2:
                act.wait_ge(sem("xa_turned"), head - 1)
            f(m["p_x"][:, head % 2, tb], misc[:, tb % 2, 0:MEM], ACT.Exp, scale=1.0 / 16, bias=m["xa_neg"][:, tb:tb + 1],
              accum_out=m["xa_sum"][:, tb:tb + 1]).then_inc(sem("xa_exp"), 1)

    x_exp(0)
    for head in range(4):
        if head < 3:
            x_exp(head + 1)
        act.wait_ge(sem("xa_turned"), head + 1)
        for mb in range(2):
            f(m["pt_x"][:, mb], misc[:, 2 + mb, :], ACT.Copy).then_inc(sem("xa_pt"), 1)
    residual_out("xo", "xo_resid")
    squares("ffn", m["h"], ready="xo_resid")

    def glu_group(g, t0, n):
        for j in range(n):
            t = t0 + 2 * j
            slot = (START["glu0"] + 2 * j) % RING
            act.wait_ge(sem("glu_conv"), g * 8 + (j + 1))
            out(t, slot, m["g_in"][:, j % 2, CONV_F - 1:])
            act.wait_ge(sem("glu_conv"), g * 8 + (j + 3))
            f(m["g_act"][:, j % 2], m["g_act"][:, j % 2], ACT.Gelu).then_inc(sem("glu_gelu"), 1)
            if j < 2:
                act.wait_ge(sem("glu_resid"), g * 8 + 2)
            else:
                act.wait_ge(sem("glu_hidden"), g * 8 + (j - 1))
            out(t + 1, (slot + 1) % RING, z[:, (slot + 1) % RING])
        for c in range(KC):
            t = t0 + 2 * n + c
            slot = (START["glu0"] + 2 * n + c) % RING
            if c >= RING:
                act.wait_ge(sem("glu_resid"), g * 8 + (2 + c - RING + 1))
            out(t, slot, z[:, slot])

    with act.Fori(0, 2) as g:
        glu_group(g, g * 24 + START["glu0"], 8)
    glu_group(2, START["glu2"], 6)
    act.dma_start(m["small2"], pr.dram["small2"]).then_inc(sem("small2_in"), 16)
    act.dma_start(m["w_cmp"], pr.dram["w_cmp"]).then_inc(sem("w_cmp_in"), 16)
    squares("fin", m["h"], ready="glu_resid", first=2 + 16 + 1)

    t0 = START["nsa_in"]
    out(t0, t0 % RING, m["gate_f"][0:24], ACT.Sigmoid, src=acc[0:24, t0 % RING])
    for dst, j in ((m["k_cmp"][:, 0], 1), (m["k_cmp"][:, 1], 2), (m["k_br"][:, 0], 3), (m["k_br"][:, 1], 4)):
        out(t0 + j, (t0 + j) % RING, dst)
    for i in range(2):
        out_wide(t0 + 5 + i, t0 + 6, m["v_br"].rearrange("p r b n -> p b r n")[:, 2 * i:2 * i + 2],
                 src=acc[:, (t0 + 5 + i) % RING].rearrange("p (b r n) -> p b r n", b=2, r=2))
    for c in range(4):
        out(t0 + 7 + c, (t0 + 7 + c) % RING, m["q_n"][:, c])
    for c in range(4):
        out(t0 + 11 + c, (t0 + 11 + c) % RING, m["u_n"][:, c, 16:])
    act.wait_ge(sem("gates_turned"), 1)
    f(m["gate_t"], misc[:, 2, 0:P].rearrange("p (b n) -> p b n", b=TB)[:, :, 0:24], ACT.Copy).then_inc(sem("gate_t"), 1)
    act.wait_ge(sem("cmp_hidden"), 1)
    for i in range(2):
        f(m["hid_c"][:, i, 0:N_CMP], misc[:, 0, i * 32:i * 32 + N_CMP], ACT.Gelu_apprx_tanh, bias=pr.col("cmp_b1", i))\
            .then_inc(sem("cmp_act"), 1)
    act.wait_ge(sem("cmp_kv"), 1)
    f(m["kc"][:, 0:N_CMP], misc[:, 3, 0:N_CMP], ACT.Copy).then_inc(sem("cmp_kv_out"), 1)
    act.wait_ge(sem("cmp_kv"), 2)
    f(m["vc"][0:N_CMP], misc[0:N_CMP, 2, 256:384], ACT.Copy).then_inc(sem("cmp_kv_out"), 1)
    for g in range(2):
        act.wait_ge(sem("cmp_gap"), g + 1)
        e = m["e_c"][:, g, :, 0:N_CMP]
        f(e, e, ACT.Exp, scale=0.125).then_inc(sem("cmp_exp"), 1)
    for g in range(2):
        for c in range(4):
            act.wait_ge(sem("cmp_turned"), 4 * g + c + 1)
            f(m["pct%d" % g][0:N_CMP, c], misc[0:N_CMP, c, :], ACT.Copy).then_inc(sem("cmp_pt"), 1)

    def n_exp(i, tb):
        n = (tb + 1) * P
        act.wait_ge(sem("n_max"), 4 * i + tb + 1)
        if i >= 2 and tb == 0:
            act.wait_ge(sem("n_turned"), 4 * (i - 2) + 4)
        f(m["p_n"][:, i % 2, tb, 0:n], acc[:, tb % 2, 0:n], ACT.Exp, scale=0.125, bias=m["n_neg"][:, i % 2, tb:tb + 1],
          accum_out=m["n_sum"][:, i % 2, tb:tb + 1]).then_inc(sem("n_exp"), 1)

    act.wait_ge(sem("cmp_turned"), 8)
    for tb in range(TB):
        n_exp(0, tb)
    for i in range(16):
        if i < 15:
            n_exp(i + 1, 0)
            n_exp(i + 1, 1)
        for sb in range(TB):
            act.wait_ge(sem("n_turned"), 4 * i + sb + 1)
            if i:
                act.wait_ge(sem("n_o"), i)
            f(m["pt_n"][:, sb, sb * P:], misc[:, sb, sb * P:], ACT.Copy).then_inc(sem("n_pt"), 1)
        if i < 15:
            n_exp(i + 1, 2)
            n_exp(i + 1, 3)
    for g in range(4):
        act.wait_ge(sem("pool_o"), g + 1)
        f(m["u_n"][:, g, 16:], misc[:, g, :], ACT.Copy, scale=pr.col("pool_scale", g)).then_inc(sem("pool_out"), 1)
    residual_out("nsa_out", "nsa_resid")

    def layer_norm(name):
        i = LAYER_NORMS.index(name)
        act.wait_ge(sem("ln_mean"), i + 1)
        f(m["mean"], misc[:, 0, :], ACT.Copy, scale=1.0 / D).then_inc(sem("ln_mean_out"), 1)
        squares(name, m["h"], ready="ln_centred", first=KC * i + 1, eps=LN_EPS)

    def mlp(name):
        hidden, resid = sem(name + "_hidden"), sem(name + "_resid")
        with act.Fori(0, GROUPS) as g:
            for j in range(16):
                t, slot = g * 16 + (START[name] + j), (START[name] + j) % RING
                if j < 4:
                    act.wait_ge(resid, g * 8 + (j + 5))
                elif j < 8:
                    act.wait_ge(hidden, g * 8 + (j - 3))
                elif j < 12:
                    act.wait_ge(hidden, g * 8 + (j - 3))
                else:
                    act.wait_ge(resid, g * 8 + (8 + j - 8 - RING + 1))
                out(t, slot, z[:, slot], ACT.Relu if j < 8 else ACT.Copy)

    layer_norm("ln1a")
    mlp("mlp_a")
    layer_norm("ln2a")

    t0 = START["gla_in"]
    out(t0, t0 % RING, m["a_g"][0:16], src=acc[0:16, t0 % RING])
    for c in range(4):
        out(t0 + 1 + c, (t0 + 1 + c) % RING, m["q_g"][:, c])
    for c in range(4):
        out(t0 + 5 + c, (t0 + 5 + c) % RING, m["k_g"][:, c])
    gz, gt, gb = m["gz"], m["gt"], m["gb"]
    for head in range(4):
        act.wait_ge(sem("gla_z"), head + 1)
        if head:
            act.wait_ge(sem("gla_k"), head)
        own.link(f(gz, misc[:, head, :], ACT.Identity, bias=pr.col("gate_b", head)))
        own.link(f(gt, gz, ACT.Abs))
        own.link(f(gt, gt, ACT.Exp, scale=-1.0))
        f(gt, gt, ACT.Ln, bias=1.0).then_inc(sem("gla_ln"), 1)
        act.wait_ge(sem("gla_b"), head + 1)
        f(gz, gb, ACT.Exp, scale=1.0 / 16).then_inc(sem("gla_exp"), 1)
        f(gt, gb, ACT.Exp, scale=-1.0 / 16).then_inc(sem("gla_exp"), 1)
        own.mark(f(m["decay"][:, head], gb.rearrange("p (n c) -> p n c", c=GLA_CHUNK)[:, :, GLA_CHUNK - 1],
                   ACT.Exp, scale=1.0 / 16))
        act.wait_ge(sem("gla_rest"), head + 1)
        f(gz, gz, ACT.Exp, scale=1.0 / 16).then_inc(sem("gla_exp"), 1)
        if head % 2:
            t = t0 + 9 + 4 * (head // 2)
            for b in range(TB):
                out_wide(t + b, t + 3, m["v_g"][:, b, blk(head // 2, 512)])
    for c in range(KC):
        out(t0 + 17 + c, (t0 + 17 + c) % RING, m["r_g"][:, c], ACT.Silu)

    def gla_kd(head):
        act.wait_ge(sem("gla_turned"), head + 1)
        f(m["kd_tok"], misc[:, 3, :].rearrange("p (b n) -> p b n", b=TB), ACT.Copy).then_inc(sem("gla_kd"), 1)

    gla_kd(0)
    for head in range(4):
        act.wait_ge(sem("gla_o"), head + 1)
        if head:
            act.wait_ge(sem("gla_y"), 2 * head)
        for odd in range(2):
            def chunks(a):
                return a.rearrange("p e (b odd c) -> p e b odd c", odd=2, c=GLA_CHUNK)[:, :, :, odd]
            src = acc[:, 2 * (head % 2) + odd, :].rearrange("p (e b c) -> p e b c", e=2, c=GLA_CHUNK)
            f(chunks(m["sq"]), src, ACT.Square).then_inc(sem("gla_sq"), 1)
            f(chunks(m["o_g"]), src, ACT.Copy).then_inc(sem("gla_o_out"), 1)
        act.wait_ge(sem("gla_ss"), head + 1)
        rsqrt(m["rstd"], acc[:, 2 * ((head + 1) % 2), :], 1.0 / 256, LN_EPS, "gla_rstd")
        if head < 3:
            gla_kd(head + 1)
    residual_out("gla_out", "gla_resid")
    layer_norm("ln1b")
    mlp("mlp_b")
    layer_norm("ln2b")
    for k in range(KC):
        act.wait_ge(sem("norm_ready"), chunks_before("ln2b") + k + 1)
        act.dma_start(pr.dram["out"][:, k], m["h"][:, k]).then_inc(sem("stored"), 16)
    act.wait_ge(sem("stored"), 16 * KC)


def vector_program(pr, dve):
    nc, m, acc, misc, sem = pr.nc, pr.m, pr.acc, pr.misc, pr.sem
    v = nc.vector
    z, h, xt = m["z"], m["h"], m["xt"]
    own = Own(dve, sem("dve_step"))

    def split(src, hi, lo, name, step=own):
        step.link(v.tensor_copy(hi, src))
        v.tensor_tensor(lo, src, bf(hi), ALU.subtract).then_inc(sem(name), 1)

    def rms(name, src, gain, hi, lo, n=S, keep=False):
        dve.wait_ge(sem("norm_rstd"), NORMS.index(name) + 1)
        for k in range(KC):
            x = src[:, k] if keep else xt[:, k % 2, 0:n]
            own.link(v.scalar_tensor_tensor(x, src[:, k], pr.col(gain, k), m["rstd"][:, 0:n], ALU.mult, ALU.mult))
            split(x, hi[:, k], lo[:, k], "norm_ready")

    def residual(name, resid, scale=1.0):
        for k in range(KC):
            t = START[name] + k
            dve.wait_ge(sem("tile_out"), t + 1)
            if scale == 1.0:
                v.tensor_tensor(h[:, k], h[:, k], z[:, t % RING], ALU.add).then_inc(sem(resid), 1)
            else:
                v.scalar_tensor_tensor(h[:, k], h[:, k], scale, z[:, t % RING], ALU.mult, ALU.add)\
                    .then_inc(sem(resid), 1)

    dve.wait_ge(sem("par_in"), 16)
    rms("mem", m["mem_in"], "norm_mem_g", m["mn_hi"], m["mn_lo"], MEM)
    rms("mix", h, "norm_mix_g", m["x_hi"], m["x_lo"])
    own.mark(v.memset(m["xc"][:, :, 0:CONV_C - 1], 0.0))
    own.mark(v.memset(m["b_in"][:, :, 0:CONV_B - 1], 0.0))
    dve.wait_ge(sem("const_in"), 16)
    dve.wait_ge(sem("small1_in"), 16)
    ws = pr.view("wsT").rearrange("p (h t) -> p h t", h=4)
    dve.wait_ge(sem("norm_ready"), 2 * KC)
    own.mark(v.memset(xt[0:4, 1], 1.0))
    own.settle()
    for head in range(4):
        own.mark(v.tensor_tensor(ws[:, head], ws[:, head], pr.view("tri01"), ALU.mult))

    def conv_step(dst, src, w, bias):
        if bias is not None:
            return v.tensor_scalar(dst, src, w, bias, ALU.mult, ALU.add)
        return v.scalar_tensor_tensor(dst, src, w, dst, ALU.mult, ALU.add)

    dve.wait_ge(sem("tile_out"), 5)
    before = own.n
    for j in range(CONV_C):
        for c in range(4):
            if j:
                own.settle(before + 4 * (j - 1) + c + 1)
            step = conv_step(m["xconv"][:, c], m["xc"][:, c, j:j + S], pr.col("conv_c_w", 4 * j + c),
                             pr.col("conv_c_b", c) if j == 0 else None)
            if j < CONV_C - 1:
                own.mark(step)
            else:
                step.then_inc(sem("xconv_pre"), 1)
    dve.wait_ge(sem("tile_out"), 9)
    for c in range(2):
        own.mark(v.tensor_tensor(m["b_in"][:, c, CONV_B - 1:], m["b_in"][:, c, CONV_B - 1:], z[:, 2 + c], ALU.mult))

    dve.wait_ge(sem("tile_out"), 15)
    for tb in range(TB):
        own.mark(v.bn_stats(m["v_stats"][:, tb], m["v_tok"][:, tb]))
    own.settle()
    for tb in range(TB):
        last = v.bn_aggr(m["v_mv"][:, tb], m["v_stats"][:, tb])
        if tb < TB - 1:
            own.mark(last)
    last.then_inc(sem("v_a_stats"), 1)

    li, fr, row = z[0:4, 0], z[0:4, 1], lambda name: m[name][0:4]
    dve.wait_ge(sem("row_ln"), 1)
    own.link(v.scalar_tensor_tensor(fr, fr, 0.0, row("row_t"), ALU.min, ALU.subtract))
    v.tensor_tensor_scan(row("row_F"), xt[0:4, 1], fr, 0.0, ALU.mult, ALU.add).then_inc(sem("rows"), 1)
    dve.wait_ge(sem("rows"), 1)
    v.tensor_tensor(li, li, row("row_F"), ALU.subtract).then_inc(sem("rows"), 1)
    dve.wait_ge(sem("rows"), 2)
    v.tensor_tensor_scan(row("row_M"), li, li, 0.0, ALU.max, ALU.max).then_inc(sem("rows"), 1)
    dve.wait_ge(sem("rows"), 3)
    v.tensor_tensor(row("row_em"), row("row_F"), row("row_M"), ALU.add).then_inc(sem("rows"), 1)

    dve.wait_ge(sem("v_a_rstd"), 1)
    vt, mv = m["v_tok"], m["v_mv"]
    for tb in range(TB):
        own.mark(v.tensor_scalar(vt[:, tb], vt[:, tb], mv[:, tb, 0:1], m["v_rstd"][:, tb:tb + 1],
                                 ALU.subtract, ALU.mult))
    before = own.n - TB
    for tb in range(TB):
        own.settle(before + tb + 1)
        own.mark(v.tensor_tensor(vt[:, tb], vt[:, tb], pr.view("ln_a_g"), ALU.mult))
    for tb in range(TB):
        own.settle(before + TB + tb + 1)
        last = v.tensor_tensor(vt[:, tb], vt[:, tb], pr.view("ln_a_b"), ALU.add)
    last.then_inc(sem("v_a_ready"), 1)

    before = own.n
    for j in range(CONV_B):
        for c in range(2):
            if j:
                own.settle(before + 2 * (j - 1) + c + 1)
            elif c == 0:
                own.settle()
            step = conv_step(m["conv_b"][:, c], m["b_in"][:, c, j:j + S], pr.col("conv_b_w", 2 * j + c),
                             pr.col("conv_b_b", c) if j == 0 else None)
            if j < CONV_B - 1:
                own.mark(step)
            else:
                step.then_inc(sem("conv_b"), 1)

    for c in range(2):
        dve.wait_ge(sem("gating"), c + 1)
        own.link(v.tensor_tensor(xt[:, c], m["u_a"][:, c], misc[:, c, :], ALU.mult))
        split(xt[:, c], m["y_hi"][:, c], m["y_lo"][:, c], "y_ready")

    def centre(i, src):
        dve.wait_ge(sem("std_mean"), i + 1)
        v.tensor_tensor(src, src, misc[:, i % 2, :], ALU.subtract).then_inc(sem("std_centred"), 1)

    ring = [m["rstd"], m["mean"]]
    for c in range(2):
        centre(c, m["conv_b"][:, c])
    for c in range(2):
        dve.wait_ge(sem("std_rstd"), c + 1)
        v.tensor_tensor(m["conv_b"][:, c], m["conv_b"][:, c], ring[c], ALU.mult).then_inc(sem("std_scaled"), 1)
    for c in range(2):
        dve.wait_ge(sem("conv_b_act"), c + 1)
        own.link(v.tensor_copy(xt[:, c], m["conv_b"][:, c]))
        split(xt[:, c], m["y_hi"][:, 2 + c], m["y_lo"][:, 2 + c], "y_ready")

    dve.wait_ge(sem("g_col"), 1)
    for head in range(4):
        dve.wait_ge(sem("M_spread"), head + 1)
        for sb in range(TB):
            v.tensor_scalar(m["w_c"][:, sb, sb * P:], misc[:, 3, sb * P:], m["g_col"][:, sb, head:head + 1], 0.0,
                            ALU.subtract, ALU.max).then_inc(sem("gap"), 1)
        for sb in range(TB):
            dve.wait_ge(sem("w_exp"), 4 * head + sb + 1)
            own.link(v.tensor_tensor(m["w_c"][:, sb, blk(sb)], m["w_c"][:, sb, blk(sb)], pr.view("tri01"), ALU.mult))
            dve.wait_ge(sem("scores_c"), 4 * head + sb + 1)
            v.scalar_tensor_tensor(m["p_c"][:, sb, sb * P:], misc[:, sb % 2, sb * P:], float(P) ** -0.5,
                                   m["w_c"][:, sb, sb * P:], ALU.mult, ALU.mult).then_inc(sem("p_c"), 1)
        dve.wait_ge(sem("cell_sum"), head + 1)
        den = row("row_den")
        if head == 0:
            v.tensor_copy(den, misc[0:4, 3, :]).then_inc(sem("den_added"), 1)
        else:
            dve.wait_ge(sem("den_added"), head)
            v.tensor_tensor(den, den, misc[0:4, 3, :], ALU.add).then_inc(sem("den_added"), 1)
    dve.wait_ge(sem("den_abs"), 1)
    dve.wait_ge(sem("row_em"), 1)
    own.link(v.tensor_tensor(den, den, row("row_em"), ALU.max))
    v.reciprocal(den, den).then_inc(sem("den_ready"), 1)
    dve.wait_ge(sem("cell_out"), 4)
    for head in range(4):
        dve.wait_ge(sem("den_spread"), head + 1)
        v.tensor_tensor(m["cell"][:, head], m["cell"][:, head], misc[:, head, :], ALU.mult)\
            .then_inc(sem("cell_ready"), 1)
    dve.wait_ge(sem("cell_ready"), 4)

    def cell_final(i):
        head = i - 2
        cell = m["cell"][:, head]
        x = xt[:, i % 2]
        dve.wait_ge(sem("std_rstd"), i + 1)
        v.scalar_tensor_tensor(x, cell, pr.col("hn_c_g", head), ring[i % 2], ALU.mult, ALU.mult)\
            .then_inc(sem("std_scaled"), 1)
        dve.wait_ge(sem("std_scaled"), i + 1)
        own.link(v.scalar_tensor_tensor(x, m["xconv"][:, head], pr.col("skip_c", head), x, ALU.mult, ALU.add))
        own.link(v.tensor_tensor(x, x, m["oc_gate"][:, head], ALU.mult))
        split(x, m["y_hi"][:, 4 + head], m["y_lo"][:, 4 + head], "y_ready")

    for i in range(2, 6):
        centre(i, m["cell"][:, i - 2])
        if i >= 4:
            cell_final(i - 2)
    cell_final(4)
    cell_final(5)
    residual("mix_out", "mix_resid")
    rms("xat", h, "norm_x_g", m["x_hi"], m["x_lo"])

    def x_max(head, tb):
        dve.wait_ge(sem("xa_scores"), 4 * head + tb + 1)
        own.link(v.tensor_reduce(m["xa_max"][:, tb:tb + 1], misc[:, tb % 2, 0:MEM], AX.X, ALU.max))
        v.tensor_scalar(m["xa_neg"][:, tb:tb + 1], m["xa_max"][:, tb:tb + 1], -1.0 / 16, None, ALU.mult)\
            .then_inc(sem("xa_max"), 1)

    def x_norm(head, tb):
        dve.wait_ge(sem("xa_exp"), 4 * head + tb + 1)
        own.link(v.reciprocal(m["xa_sum"][:, tb:tb + 1], m["xa_sum"][:, tb:tb + 1]))
        p = m["p_x"][:, head % 2, tb]
        v.tensor_scalar(p, p, m["xa_sum"][:, tb:tb + 1], None, ALU.mult).then_inc(sem("xa_p"), 1)

    def x_out(head):
        for c in (2 * head, 2 * head + 1):
            dve.wait_ge(sem("xa_o"), c + 1)
            split(acc[:, c % 4, :], m["y_hi"][:, c], m["y_lo"][:, c], "xa_y")

    x_max(0, 0)
    for i in range(16):
        if i < 15:
            x_max((i + 1) // 4, (i + 1) % 4)
        x_norm(i // 4, i % 4)
        if i % 4 == 3 and i > 3:
            x_out(i // 4 - 1)
    x_out(3)
    residual("xo", "xo_resid")
    rms("ffn", h, "norm_ffn_g", m["x_hi"], m["x_lo"])

    for b in range(2):
        v.memset(m["g_in"][:, b, 0:CONV_F - 1], 0.0).then_inc(sem("glu_conv"), 1)
    dve.wait_ge(sem("norm_ready"), chunks_before("ffn") + KC)
    for b in range(2):
        v.memset(xt[:, b, 0:1], 0.0).then_inc(sem("glu_resid"), 1)
    dve.wait_ge(sem("glu_resid"), 2)
    conv_w = pr.view("conv_f_w").rearrange("p (j f) -> p j f", j=CONV_F)
    conv_bias = pr.view("conv_f_b")

    def glu_group(g, t0, n, step):
        def scalar(view, j):
            if isinstance(g, int):
                return view[:, 8 * g + j:8 * g + j + 1]
            return view[:, j:j + 9][:, bass.ds(g * 8, 1)]
        for j in range(n):
            t = t0 + 2 * j
            slot = (START["glu0"] + 2 * j) % RING
            src, dst = m["g_in"][:, j % 2], m["g_act"][:, j % 2]
            dve.wait_ge(sem("tile_out"), t + 1)
            step.link(v.tensor_scalar(dst, src[:, 0:S], scalar(conv_w[:, 0], j), scalar(conv_bias, j),
                                      ALU.mult, ALU.add))
            step.link(v.scalar_tensor_tensor(dst, src[:, 1:S + 1], scalar(conv_w[:, 1], j), dst, ALU.mult, ALU.add))
            v.scalar_tensor_tensor(dst, src[:, 2:S + 2], scalar(conv_w[:, 2], j), dst, ALU.mult, ALU.add)\
                .then_inc(sem("glu_conv"), 1)
            dve.wait_ge(sem("glu_gelu"), g * 8 + (j + 1))
            dve.wait_ge(sem("tile_out"), t + 2)
            step.link(v.tensor_tensor(xt[:, j % 2], dst, z[:, (slot + 1) % RING], ALU.mult))
            split(xt[:, j % 2], m["y_hi"][:, j], m["y_lo"][:, j], "glu_hidden", step)
        for c in range(KC):
            dve.wait_ge(sem("tile_out"), t0 + (2 * n + c + 1))
            slot = (START["glu0"] + 2 * n + c) % RING
            v.tensor_tensor(h[:, c], h[:, c], z[:, slot], ALU.add).then_inc(sem("glu_resid"), 1)

    with dve.Fori(0, 2) as g:
        glu_group(g, g * 24 + START["glu0"], 8, Own(dve, sem("glu_step"), g * 32))
    glu_group(2, START["glu2"], 6, Own(dve, sem("glu_tail_step")))
    rms("fin", h, "final_g", m["x_hi"], m["x_lo"], keep=True)

    t0 = START["nsa_in"]
    pos = pr.view("cmp_pos").rearrange("p (i j) -> p i j", i=2)
    own.mark(v.memset(m["u_n"][:, :, 0:16], 0.0))
    for i in range(2):
        dve.wait_ge(sem("tile_out"), t0 + 2 + i)
        halves = m["k_cmp"][:, i].rearrange("p (b j) -> p b j", j=CMP_STRIDE)
        for half in range(2):
            j = blk(half, CMP_STRIDE)
            v.tensor_tensor(m["blocks"][:, i, :, j], halves[:, half:half + N_CMP],
                            pos[:, i, j].unsqueeze(1).to_broadcast([P, N_CMP, CMP_STRIDE]), ALU.add)\
                .then_inc(sem("blocks"), 1)

    gates = m["gate_t"].rearrange("p b (g c r) -> p b g c r", g=2, c=4)
    dve.wait_ge(sem("gate_t"), 1)
    dve.wait_ge(sem("small2_in"), 16)
    neg = pr.view("cmp_neg").rearrange("p (b n) -> p b n", b=16)[:, :, 0:N_CMP]
    seen = pr.view("cmp01").rearrange("p (b n) -> p b n", b=16)[:, :, 0:N_CMP]
    mx, sm = m["c_mx"], m["c_sum"]

    def spread(a):
        return a.unsqueeze(2).to_broadcast([P, 16, N_CMP])

    for g in range(2):
        e = m["e_c"][:, g, :, 0:N_CMP]
        dve.wait_ge(sem("cmp_scores"), g + 1)
        own.link(v.tensor_tensor(e, misc[:, g, :].rearrange("p (b n) -> p b n", b=16)[:, :, 0:N_CMP], neg, ALU.add))
        own.link(v.tensor_reduce(mx, e, AX.X, ALU.max))
        v.tensor_tensor(e, e, spread(mx), ALU.subtract).then_inc(sem("cmp_gap"), 1)
    for g in range(2):
        e = m["e_c"][:, g, :, 0:N_CMP]
        dve.wait_ge(sem("cmp_exp"), g + 1)
        own.link(v.tensor_tensor(e, e, seen, ALU.mult))
        own.link(v.tensor_reduce(sm, e, AX.X, ALU.add))
        own.link(v.tensor_scalar(sm, sm, 1e-30, None, ALU.max))
        own.link(v.reciprocal(sm, sm))
        own.link(v.tensor_tensor(sm.rearrange("p (b c) -> p b c", b=TB), sm.rearrange("p (b c) -> p b c", b=TB),
                                 gates[:, :, g, :, 0], ALU.mult))
        v.tensor_tensor(e, e, spread(sm), ALU.mult).then_inc(sem("cmp_p"), 1)

    dve.wait_ge(sem("tile_out"), END["nsa_in"])
    inv = pr.view("pool_inv").rearrange("p (g t) -> p g t", g=4)
    for g in range(4):
        u = m["u_n"][:, g]
        if g:
            dve.wait_ge(sem("pool_r"), g)
        src = u
        for step in range(g + 1):
            d = 2 ** step
            lo = 2 * d - 1
            dst = m["pool_s"][:, step % 2]
            own.link(v.tensor_tensor(dst[:, lo:], src[:, lo:], src[:, lo - d:S + 16 - d], ALU.add))
            src = dst
        other = m["pool_s"][:, (g + 1) % 2]
        own.link(v.tensor_tensor(other[:, 0:16], src[:, 16:32], inv[:, g], ALU.mult))
        own.mark(v.tensor_tensor(u[:, 16:32], other[:, 0:16], u[:, 16:32], ALU.subtract))
        v.scalar_tensor_tensor(u[:, 32:], src[:, 32:], 1.0 / 2 ** (g + 1), u[:, 32:], ALU.mult, ALU.subtract)\
            .then_inc(sem("pool_r"), 1)

    def n_max(i, tb):
        n = (tb + 1) * P
        dve.wait_ge(sem("n_scores"), 4 * i + tb + 1)
        own.link(v.tensor_reduce(m["n_max"][:, i % 2, tb:tb + 1], acc[:, tb % 2, 0:n], AX.X, ALU.max))
        v.tensor_scalar(m["n_neg"][:, i % 2, tb:tb + 1], m["n_max"][:, i % 2, tb:tb + 1], -0.125, None, ALU.mult)\
            .then_inc(sem("n_max"), 1)

    def n_final(i):
        c, g, br = i // 4, i // 2 % 2, i % 2
        r = m["n_r"][:, i % 2]
        dve.wait_ge(sem("n_exp"), 4 * i + 4)
        own.link(v.reciprocal(r, m["n_sum"][:, i % 2]))
        own.link(v.tensor_tensor(r, r, gates[:, :, g, c, 1 + br], ALU.mult))
        for tb in range(TB):
            p = m["p_n"][:, i % 2, tb, 0:(tb + 1) * P]
            v.tensor_scalar(p, p, r[:, tb:tb + 1], None, ALU.mult).then_inc(sem("n_p"), 1)

    def n_y(c):
        dve.wait_ge(sem("n_o"), 4 * c + 4)
        split(acc[:, 2 + c % 2, :], m["y_hi"][:, c], m["y_lo"][:, c], "n_y")

    for tb in range(TB):
        n_max(0, tb)
    for i in range(16):
        if i < 15:
            n_max(i + 1, 0)
            n_max(i + 1, 1)
        if i % 4 == 0 and i:
            n_y(i // 4 - 1)
        n_final(i)
        if i < 15:
            n_max(i + 1, 2)
            n_max(i + 1, 3)
    n_y(3)
    for g in range(4):
        dve.wait_ge(sem("pool_out"), g + 1)
        split(m["u_n"][:, g, 16:], m["y_hi"][:, 4 + g], m["y_lo"][:, 4 + g], "n_y")
    residual("nsa_out", "nsa_resid", ALPHA)

    def layer_norm(name, gain, bias, at, halves=True):
        dve.wait_ge(sem("ln_mean_out"), LAYER_NORMS.index(name) + 1)
        for k in range(KC):
            v.tensor_tensor(h[:, k], h[:, k], m["mean"], ALU.subtract).then_inc(sem("ln_centred"), 1)
        dve.wait_ge(sem("norm_rstd"), NORMS.index(name) + 1)
        for k in range(KC):
            own.link(v.scalar_tensor_tensor(h[:, k], h[:, k], pr.col(gain, at + k), m["rstd"], ALU.mult, ALU.mult))
            shift = v.tensor_scalar(h[:, k], h[:, k], pr.col(bias, at + k), None, ALU.add)
            if halves:
                own.link(shift)
                split(h[:, k], m["x_hi"][:, k], m["x_lo"][:, k], "norm_ready")
            else:
                shift.then_inc(sem("norm_ready"), 1)

    def mlp(name):
        hidden, resid = name + "_hidden", name + "_resid"
        for k in range(KC):
            v.tensor_scalar(h[:, k], h[:, k], ALPHA, None, ALU.mult).then_inc(sem(resid), 1)
        dve.wait_ge(sem(resid), KC)
        with dve.Fori(0, GROUPS) as g:
            step = Own(dve, sem(name + "_step"), g * 16)
            for j in range(16):
                t, slot = g * 16 + (START[name] + j), (START[name] + j) % RING
                dve.wait_ge(sem("tile_out"), t + 1)
                if j < 8:
                    step.link(v.tensor_tensor(xt[:, j % 2], z[:, slot], z[:, slot], ALU.mult))
                    split(xt[:, j % 2], m["y_hi"][:, j], m["y_lo"][:, j], hidden, step)
                else:
                    v.tensor_tensor(h[:, j - 8], h[:, j - 8], z[:, slot], ALU.add).then_inc(sem(resid), 1)

    layer_norm("ln1a", "ln1_g", "ln1_b", 0)
    mlp("mlp_a")
    layer_norm("ln2a", "ln2_g", "ln2_b", 0)

    t0 = START["gla_in"]
    gz, gt, gb = m["gz"], m["gt"], m["gb"]
    per_chunk = gb.rearrange("p (n c) -> p n c", c=GLA_CHUNK)
    for head in range(4):
        dve.wait_ge(sem("gla_ln"), head + 1)
        own.link(v.scalar_tensor_tensor(gz, gz, 0.0, gt, ALU.min, ALU.subtract))
        v.tensor_tensor_scan(gb, pr.view("keep"), gz, 0.0, ALU.mult, ALU.add).then_inc(sem("gla_b"), 1)
        dve.wait_ge(sem("gla_exp"), 3 * head + 2)
        own.mark(v.tensor_tensor(m["kt_g"][:, head], m["k_g"][:, head], gt, ALU.mult))
        own.mark(v.scalar_tensor_tensor(m["q_g"][:, head], m["q_g"][:, head], float(P) ** -0.5, gz, ALU.mult, ALU.mult))
        own.settle()
        v.tensor_tensor(gz.rearrange("p (n c) -> p n c", c=GLA_CHUNK),
                        per_chunk[:, :, GLA_CHUNK - 1:].to_broadcast([P, 8, GLA_CHUNK]), per_chunk, ALU.subtract)\
            .then_inc(sem("gla_rest"), 1)
        dve.wait_ge(sem("gla_exp"), 3 * head + 3)
        v.tensor_tensor(m["k_g"][:, head], m["k_g"][:, head], gz, ALU.mult).then_inc(sem("gla_k"), 1)
    dve.wait_ge(sem("tile_out"), END["gla_in"])
    own.link(v.memset(m["state"][:, 0], 0.0))

    def gla_local(head):
        dve.wait_ge(sem("gla_scores"), head + 1)
        v.tensor_tensor(m["att_g"], misc[:, 0, 0:256].rearrange("p (b n) -> p b n", b=TB),
                        pr.view("gla01").rearrange("p (b n) -> p b n", b=TB), ALU.mult).then_inc(sem("gla_att"), 1)
        for n in range(7):
            i = 7 * head + n
            dve.wait_ge(sem("gla_update"), i + 1)
            if n:
                dve.wait_ge(sem("gla_state"), i)
            v.scalar_tensor_tensor(m["state"][:, n + 1], m["state"][:, n], m["decay"][:, head, n:n + 1],
                                   misc[:, 1 + i % 2, 0:256], ALU.mult, ALU.add).then_inc(sem("gla_state"), 1)

    gla_local(0)
    for head in range(4):
        if head < 3:
            gla_local(head + 1)
        dve.wait_ge(sem("gla_rstd"), head + 1)
        dve.wait_ge(sem("gla_o_out"), 2 * head + 2)
        for e in range(2):
            c = 2 * head + e
            x = xt[:, e]
            own.link(v.scalar_tensor_tensor(x, m["o_g"][:, e], pr.col("gla_g", e), m["rstd"], ALU.mult, ALU.mult))
            own.link(v.tensor_tensor(x, x, m["r_g"][:, c], ALU.mult))
            split(x, m["y_hi"][:, c], m["y_lo"][:, c], "gla_y")
    residual("gla_out", "gla_resid", ALPHA)
    layer_norm("ln1b", "ln1_g", "ln1_b", 8)
    mlp("mlp_b")
    layer_norm("ln2b", "ln2_g", "ln2_b", 8, halves=False)


def gpsimd_program(pr, pool):
    nc, m, sem = pr.nc, pr.m, pr.sem

    def split(slot, t, turn):
        pool.wait_ge(sem("weights_in%d" % slot), turn * 16)
        if not isinstance(t, int) or t >= RING:
            pool.wait_ge(sem("tile_done"), t - RING + 1)
        pool.sem_inc(sem("tile_claimed"), 1)
        hi = m["w_hi"][:, slot].rearrange("p k n -> p (k n)")
        nc.gpsimd.tensor_scalar(hi, m["raw"][:, slot], 1.0, 0.0, ALU.mult, ALU.add).then_inc(sem("weights_high"), 1)
        pool.wait_ge(sem("weights_high"), t + 1)
        nc.gpsimd.tensor_tensor(m["w_lo"][:, slot].rearrange("p k n -> p (k n)"), m["raw"][:, slot], bf(hi),
                                ALU.subtract).then_inc(sem("weights_split"), 1)

    for slot in range(RING):
        split(slot, slot, 1)
    with pool.Fori(1, N_TILES // RING) as r:
        for slot in range(RING):
            split(slot, r * RING + slot, r + 1)
    for slot in range(N_TILES % RING):
        split(slot, N_TILES // RING * RING + slot, N_TILES // RING + 1)


def sync_program(pr, sp):
    m, sem, dram = pr.m, pr.sem, pr.dram
    sp.dma_start(m["mem_in"], dram["mem"]).then_inc(sem("mem_in"), 16)
    sp.dma_start(m["h"], dram["x"]).then_inc(sem("x_in"), 16)
    sp.dma_start(m["const"], dram["const"]).then_inc(sem("const_in"), 16)
    sp.dma_start(m["par"], dram["par"]).then_inc(sem("par_in"), 16)
    rounds = N_TILES // RING
    stream = dram["weights"][0:rounds * RING].rearrange("(r j) p n -> r j p n", j=RING)
    for slot in range(RING):
        sp.dma_start(m["raw"][:, slot], dram["weights"][slot]).then_inc(sem("weights_in%d" % slot), 16)
    with sp.Fori(1, rounds) as r:
        for slot in range(RING):
            sp.wait_ge(sem("weights_split"), r * RING + (slot - RING + 1))
            sp.dma_start(m["raw"][:, slot], stream[bass.ds(r, 1), slot].rearrange("a p n -> p (a n)"))\
                .then_inc(sem("weights_in%d" % slot), 16)
    for slot in range(N_TILES % RING):
        sp.wait_ge(sem("weights_split"), (rounds - 1) * RING + slot + 1)
        sp.dma_start(m["raw"][:, slot], dram["weights"][rounds * RING + slot])\
            .then_inc(sem("weights_in%d" % slot), 16)


def build(nc, dram):
    with ExitStack() as ctx:
        pr = Program(nc, ctx, dram)
        block = ctx.enter_context(nc.Block())

        @block.sync
        def _(sp):
            sync_program(pr, sp)

        @block.gpsimd
        def _(pool):
            gpsimd_program(pr, pool)

        @block.scalar
        def _(act):
            scalar_program(pr, act)

        @block.vector
        def _(dve):
            vector_program(pr, dve)

        @block.tensor
        def _(pe):
            tensor_program(pr, pe)


def kernel(**inputs):
    import concourse.bacc as bacc
    from concourse.bass_utils import run_bass_kernel_spmd as run

    i = {name: np.asarray(a) for name, a in inputs.items()}
    by_chunk = lambda a: np.ascontiguousarray(a.T.reshape(KC, P, -1).transpose(1, 0, 2))
    w1 = i["a_cmp_w1_2"][0].reshape(2 * CMP_BLOCK, 64, 64).transpose(1, 0, 2)
    arrays = {"x": by_chunk(i["x"][0]), "mem": by_chunk(i["mem"][0]), "weights": weight_stream(i),
              "const": shape_constants(), "par": params(i), "small1": small1(i), "small2": small2(i),
              "w_cmp": block_diagonal(w1).reshape(P, 2, CMP_BLOCK, P)}
    nc = bacc.Bacc("TRN2", target_bir_lowering=False, num_devices=1)
    dram = {name: nc.dram_tensor(name + "_dram", a.shape, F32, kind="ExternalInput").ap() for name, a in arrays.items()}
    dram["out"] = nc.dram_tensor("out_dram", (P, KC, S), F32, kind="ExternalOutput").ap()
    build(nc, dram)
    result = run(nc, [{name + "_dram": a for name, a in arrays.items()}], core_ids=[0])
    out = result.results[0]["out_dram"]
    return out.transpose(1, 0, 2).reshape(1, D, S).transpose(0, 2, 1)
```

```python
from contextlib import ExitStack

import numpy as np

import concourse.bass as bass
from concourse import mybir

F32 = mybir.dt.float32
F32R = mybir.dt.float32r
ACT = mybir.ActivationFunctionType
ALU = mybir.AluOpType
AX = mybir.AxisListType

P = 128
D = 1024
S = 512
MEM = 256
KC = D // P
TB = S // P
DFF = 2816
FC = DFF // P
HID = 4096
GROUPS = HID // P // KC
CONV_B, CONV_C, CONV_F = 31, 4, 3
RING = 4
TILE = KC * P
RMS_EPS, LN_EPS = 1e-6, 1e-5
ALPHA = 4.0 ** 0.25
N_CMP, CMP_BLOCK, CMP_STRIDE = 31, 32, 16
GLA_CHUNK = 64
NEG = -1e30

GLU_GROUPS = [8, 8, 6]
STAGES = [("mix_in", 17), ("mem_kv", 16), ("mix_out", 8), ("xq", 8), ("xo", 8),
          ("glu0", 24), ("glu1", 24), ("glu2", 20),
          ("nsa_in", 15), ("nsa_out", 8), ("mlp_a", 64), ("gla_in", 25), ("gla_out", 8), ("mlp_b", 64)]
START, END = {}, {}
_at = 0
for _name, _n in STAGES:
    START[_name], END[_name] = _at, _at + _n
    _at += _n
N_TILES = _at

NORMS = ["mix", "mem", "xat", "ffn", "fin", "ln1a", "ln2a", "ln1b", "ln2b"]
LAYER_NORMS = NORMS[5:]


HALF = KC // 2


def chunks_before(name):
    return KC * NORMS.index(name)


PARAMS = [("norm_mix_g", 8), ("norm_x_g", 8), ("norm_mem_g", 8), ("norm_ffn_g", 8), ("final_g", 8),
          ("ln1_g", 16), ("ln1_b", 16), ("ln2_g", 16), ("ln2_b", 16),
          ("conv_b_w", 2 * CONV_B), ("conv_b_b", 2), ("gn_b_g", 2), ("gn_b_b", 2),
          ("conv_c_w", 4 * CONV_C), ("conv_c_b", 4), ("hn_c_g", 4), ("skip_c", 4),
          ("conv_f_w", FC * CONV_F), ("conv_f_b", FC), ("pool_scale", 4), ("cmp_b1", 2), ("cmp_pos", 64),
          ("gate_b", 4), ("gla_g", 2), ("b_igate", 1), ("b_fgate", 1)]
CONSTS = [("ident", P), ("tri01", P), ("causal_neg", P), ("avg64", P), ("avg128", P), ("ones", P),
          ("den_sel", 16), ("row_sel", 4 * P)]
SMALL1 = [("wqkv", 12 * P), ("wsT", 4 * P), ("ln_a_g", 256), ("ln_a_b", 256), ("b_s", 4 * P)]
SMALL2 = [("gate_w2", 512), ("pool_w", 512), ("cmp_w2", 256), ("cmp_neg", 512), ("cmp01", 512),
          ("keep", 512), ("gla01", 256), ("pool_inv", 64)]


def columns(table):
    at, out = 0, {}
    for name, n in table:
        out[name] = (at, n)
        at += n
    return out, at


def tile_of(w, k0, kc, cols):
    out = np.zeros((P, KC, P), np.float32)
    block = w[k0 * P:(k0 + kc) * P, cols]
    out[:, :kc, :block.shape[1]] = block.reshape(kc, P, block.shape[1]).transpose(1, 0, 2)
    return out.reshape(P, TILE)


def chunk(c):
    return slice(c * P, (c + 1) * P)


def weight_stream(i):
    w_in, w_up, w_down = i["w_in"][0], i["w_up"][0], i["w_down"][0]
    a_in, c_in = i["a_w_in_2"][0], i["c_w_in_2"][0]
    tiles = []

    def add(w, cols, k0=0, kc=KC):
        tiles.append(tile_of(w, k0, kc, cols))

    def add_wide(w, width):
        per = TILE // width
        for k0 in range(0, KC, per):
            tiles.append(w[k0 * P:(k0 + per) * P].reshape(per, P, width).transpose(1, 0, 2).reshape(P, TILE))

    gates = np.zeros((D, P), np.float32)
    gates[:, 0:4], gates[:, 32:36] = w_in[:, 2048:2052], w_in[:, 2052:2056]
    add(gates, slice(0, P))
    for c in [8, 9, 10, 11, 4, 5, 6, 7, 12, 13, 14, 15]:
        add(w_in, chunk(c))
    add_wide(w_in[:, 256:512], 256)
    for c in (0, 1):
        add(w_in, chunk(c))
    for c in range(KC):
        add(i["w_xkv"][0], chunk(c))
    for half in range(2):
        add_wide(i["w_xkv"][0][:, D + half * 512:D + (half + 1) * 512], 512)
    for name in ("w_out", "w_xq", "w_xo"):
        for c in range(KC):
            add(i[name][0], chunk(c))
    f0 = 0
    for n in GLU_GROUPS:
        for f in range(f0, f0 + n):
            add(w_up, chunk(f))
            add(w_up, chunk(FC + f))
        for c in range(KC):
            add(w_down, chunk(c), f0, n)
        f0 += n
    add(a_in, slice(1280, 1304))
    for c in (0, 1, 2, 4):
        add(a_in, slice(512 + c * P, 512 + (c + 1) * P))
    add_wide(np.concatenate([a_in[:, 512 + c * P:512 + (c + 1) * P] for c in (3, 5)], axis=1), 256)
    order = np.arange(512).reshape(2, 4, 64).transpose(1, 0, 2).reshape(512)
    q = a_in[:, :512].reshape(D, 2, 4, 64).transpose(0, 2, 1, 3).reshape(D, 512)
    for c in range(4):
        add(q, chunk(c))
    for c in range(4):
        add(a_in, slice(1304 + c * P, 1304 + (c + 1) * P))
    a_out = i["a_w_out_2"][0]
    a_out = np.concatenate([a_out[:512].reshape(2, 4, 64, D).transpose(1, 0, 2, 3).reshape(512, D), a_out[512:]])
    for c in range(KC):
        add(a_out, chunk(c))

    def mlp(layer):
        for g in range(GROUPS):
            for j in range(KC):
                add(i["mlp_w1_2"][layer], chunk(g * KC + j))
            for c in range(KC):
                add(i["mlp_w2_2"][layer], chunk(c), g * KC, KC)

    mlp(0)
    add(c_in, slice(3072, 3088))
    for c in range(8):
        add(c_in, chunk(c))
    for half in range(2):
        add_wide(c_in[:, D + half * 512:D + (half + 1) * 512], 512)
    for c in range(16, 24):
        add(c_in, chunk(c))
    for c in range(KC):
        add(i["c_w_out_2"][0], chunk(c))
    mlp(1)
    return np.stack(tiles)


def by_feature(v):
    v = np.asarray(v)
    v = v.reshape(-1, v.shape[-1] // P, P)
    return v.transpose(2, 0, 1).reshape(P, -1)


def pack(table, values):
    where, width = columns(table)
    out = np.zeros((P, width), np.float32)
    for name, (at, n) in where.items():
        v = np.asarray(values[name])
        out[:v.shape[0], at:at + n] = v.reshape(v.shape[0], n)
    return out


def params(i):
    col4 = lambda v: v[0][:, None]
    return pack(PARAMS, {
        "norm_mix_g": by_feature(i["norm_mix_g"][0]), "norm_x_g": by_feature(i["norm_x_g"][0]),
        "norm_mem_g": by_feature(i["norm_mem_g"][0]), "norm_ffn_g": by_feature(i["norm_ffn_g"][0]),
        "final_g": by_feature(i["final_g"]),
        "ln1_g": by_feature(i["ln1_g_2"]), "ln1_b": by_feature(i["ln1_b_2"]),
        "ln2_g": by_feature(i["ln2_g_2"]), "ln2_b": by_feature(i["ln2_b_2"]),
        "conv_b_w": by_feature(i["conv_b_w"][0]), "conv_b_b": by_feature(i["conv_b_b"][0]),
        "gn_b_g": by_feature(i["gn_b_g"][0]), "gn_b_b": by_feature(i["gn_b_b"][0]),
        "conv_c_w": by_feature(i["conv_c_w"][0]), "conv_c_b": by_feature(i["conv_c_b"][0]),
        "hn_c_g": by_feature(i["hn_c_g"][0]), "skip_c": by_feature(i["skip_c"][0]),
        "conv_f_w": by_feature(i["conv_f_w"][0]), "conv_f_b": by_feature(i["conv_f_b"][0]),
        "pool_scale": by_feature(i["a_pool_scale_2"][0]),
        "cmp_b1": np.concatenate([i["a_cmp_b1_2"][0].T] * 2),
        "cmp_pos": np.concatenate([i["a_cmp_pos_2"][0].transpose(2, 0, 1).reshape(64, 64)] * 2),
        "gate_b": by_feature(i["c_gate_b_2"][0]), "gla_g": by_feature(i["c_norm_g_2"][0]),
        "b_igate": col4(i["b_igate"]), "b_fgate": col4(i["b_fgate"])})


def block_diagonal(w):
    out = np.zeros((P, w.shape[1], P), np.float32)
    out[:64, :, :64] = w
    out[64:, :, 64:] = w
    return out


def shape_constants():
    r = np.arange(P)
    avg64 = (r[:, None] // 64 == r[None, :] // 64) / 64.0
    den_sel = np.zeros((P, 4, 4)); row_sel = np.zeros((4, 4, P))
    for h in range(4):
        den_sel[:, h, h] = 1.0
        row_sel[h, h, :] = 1.0
    return pack(CONSTS, {
        "ident": np.eye(P), "tri01": r[:, None] <= r[None, :],
        "causal_neg": np.where(r[None, :] <= r[:, None], 0.0, NEG),
        "avg64": avg64, "avg128": np.full((P, P), 1.0 / P), "ones": np.ones((P, P)),
        "den_sel": den_sel.reshape(P, 16), "row_sel": row_sel.reshape(4, 4 * P)})


def small1(i):
    wqkv = np.stack([i["w_q_c"][0], i["w_k_c"][0], i["w_v_c"][0]])
    return pack(SMALL1, {
        "wqkv": wqkv.transpose(2, 0, 1, 3).reshape(P, 12 * P),
        "wsT": i["w_s"][0].transpose(2, 0, 1).reshape(P, 4 * P),
        "ln_a_g": np.broadcast_to(i["ln_a_g"][0], (P, 256)), "ln_a_b": np.broadcast_to(i["ln_a_b"][0], (P, 256)),
        "b_s": i["b_s"][0].reshape(1, 4 * P)})


def small2(i):
    t = np.arange(S).reshape(TB, P).T
    seen = (np.arange(N_CMP) * CMP_STRIDE + CMP_BLOCK - 1)[None, None, :] <= t[:, :, None]
    cmp01 = np.zeros((P, TB, 4, 32)); cmp_neg = np.zeros((P, TB, 4, 32))
    cmp01[..., :N_CMP] = seen[:, :, None, :]
    cmp_neg[..., :N_CMP] = np.where(seen, 0.0, NEG)[:, :, None, :]
    pool_inv = np.zeros((P, 4, 16))
    for g in range(4):
        pool_inv[:, g] = 1.0 / np.minimum(np.arange(1, 17), 2 ** (g + 1))
    j = np.arange(P) % GLA_CHUNK
    gla01 = np.broadcast_to((j[:, None] <= np.arange(GLA_CHUNK)[None, :])[:, None, :], (P, TB, GLA_CHUNK))
    return pack(SMALL2, {
        "gate_w2": i["c_gate_w2_2"][0], "pool_w": i["a_pool_w_2"][0].transpose(1, 0, 2).reshape(P, 512),
        "cmp_w2": block_diagonal(i["a_cmp_w2_2"][0].transpose(1, 0, 2)).reshape(P, 256),
        "cmp_neg": cmp_neg.reshape(P, 512), "cmp01": cmp01.reshape(P, 512),
        "keep": np.broadcast_to(np.arange(S) % GLA_CHUNK != 0, (P, S)),
        "gla01": gla01.reshape(P, 256), "pool_inv": pool_inv.reshape(P, 64)})


def memory_map(nc):
    m = {}
    at = 16512

    def place(name, shape, dtype, offset):
        m[name] = nc.alloc_sbuf_tensor_at(name, [P] + shape, dtype, offset=offset, align_bytes=4)[:]

    def region(nbytes):
        nonlocal at
        start = at
        at += nbytes
        return start

    def fill(start, table):
        for name, shape in table:
            place(name, shape, F32, start)
            start += 4 * int(np.prod(shape))
        return start

    ring = region(4 * RING * TILE)
    place("raw", [RING, TILE], F32, ring)
    place("w_hi", [RING, KC, P], F32R, region(4 * RING * TILE))
    place("w_lo", [RING, KC, P], F32R, region(4 * RING * TILE))
    place("h", [KC, S], F32, region(4 * KC * S))
    x = region(8 * KC * S)
    place("x_hi", [KC, S], F32R, x)
    place("x_lo", [KC, S], F32R, x + 4 * KC * S)
    y = region(8 * KC * S)
    place("y_hi", [KC, S], F32R, y)
    place("y_lo", [KC, S], F32R, y + 4 * KC * S)
    place("z", [RING, S], F32, region(4 * RING * S))
    place("const", [columns(CONSTS)[1]], F32, region(4 * columns(CONSTS)[1]))
    place("par", [columns(PARAMS)[1]], F32, region(4 * columns(PARAMS)[1] + 8))
    small = region(4 * columns(SMALL2)[1])
    place("small1", [columns(SMALL1)[1]], F32, small)
    place("small2", [columns(SMALL2)[1]], F32, small)
    arena = fill(at, [("sq", [2, S]), ("xt", [2, S]), ("rstd", [S]), ("mean", [S])])
    end = nc.sbuf_usable_end

    a = fill(arena, [("mem_k", [KC, MEM]), ("mem_v", [2, D])])
    place("mem_in", [KC, MEM], F32, arena)
    fill(a, [("sum_sq", [S]), ("sum_h", [S])])
    e = fill(a, [("xc", [4, S + CONV_C - 1]), ("xconv", [4, S]), ("b_in", [2, S + CONV_B - 1]), ("v_tok", [TB, 256]),
                 ("v_stats", [TB, 6]), ("v_mv", [TB, 2]), ("v_rstd", [TB]), ("g_col", [TB, 4])])
    assert e <= end, (e, end)
    fill(x, [("row_t", [S]), ("row_F", [S]), ("row_M", [S]), ("row_em", [S]), ("row_den", [S]),
             ("q_c", [S]), ("k_c", [S]), ("v_c", [TB, P]), ("w_c", [TB, S]), ("p_c", [TB, S])])
    place("mn_hi", [KC, MEM], F32R, y)
    place("mn_lo", [KC, MEM], F32R, y + 4 * KC * MEM)
    place("cell", [4, S], F32, y + 4 * 4 * S)
    place("u_a", [2, S], F32, y + 4 * 8 * S)
    place("conv_b", [2, S], F32, y + 4 * 10 * S)
    place("oc_gate", [4, S], F32, y + 4 * 12 * S)
    place("q_x", [KC, S], F32, a)
    e = fill(a + 4 * KC * S, [("xa_neg", [4]), ("xa_sum", [4]), ("xa_max", [4])])
    assert e <= end
    fill(x, [("p_x", [2, TB, MEM]), ("pt_x", [2, S])])
    fill(arena, [("g_in", [2, S + CONV_F - 1]), ("g_act", [2, S])])
    e = fill(arena, [("k_cmp", [2, S]), ("blocks", [2, N_CMP, CMP_BLOCK]), ("k_br", [2, S]), ("v_br", [2, TB, P]),
                     ("q_n", [4, S]), ("u_n", [4, S + 16]), ("gate_f", [S]), ("gate_t", [TB, 24]), ("hid_c", [2, 32]),
                     ("kc", [32]), ("vc", [P]), ("n_max", [2, TB]), ("n_neg", [2, TB]), ("n_sum", [2, TB]),
                     ("n_r", [2, TB]), ("c_mx", [16]), ("c_sum", [16])])
    assert e <= end, (e, end)
    place("pool_s", [2, S + 16], F32, arena + 4 * 2 * S)
    fill(x, [("p_n", [2, TB, S]), ("pt_n", [TB, S])])
    place("e_c", [2, 16, 32], F32, x)
    place("w_cmp", [2, CMP_BLOCK, P], F32, y)
    place("pct0", [4, S], F32, y + 4 * 4 * S)
    place("pct1", [4, S], F32, y + 4 * 12 * S)
    e = fill(arena, [("a_g", [S]), ("q_g", [4, S]), ("k_g", [4, S]), ("v_g", [TB, D]), ("gz", [S]), ("gt", [S]),
                     ("gb", [S]), ("decay", [4, 8])])
    assert e <= end, (e, end)
    place("kt_g", [4, S], F32, y + 4 * 4 * S)
    place("r_g", [KC, S], F32, y + 4 * 8 * S)
    fill(x, [("att_g", [TB, GLA_CHUNK]), ("kd_tok", [TB, P]), ("state", [8, 256]), ("o_g", [2, S])])
    return m


class Program:

    def __init__(self, nc, ctx, dram):
        self.nc, self.ctx, self.dram = nc, ctx, dram
        self.m = memory_map(nc)
        self.acc = ctx.enter_context(nc.psum_tensor("acc", [P, RING, 512], F32))[:]
        self.misc = ctx.enter_context(nc.psum_tensor("misc", [P, 4, 512], F32))[:]
        self.sems = {}
        self.tables = [(self.m["const"], columns(CONSTS)[0]), (self.m["par"], columns(PARAMS)[0]),
                       (self.m["small1"], columns(SMALL1)[0]), (self.m["small2"], columns(SMALL2)[0])]

    def sem(self, name):
        if name not in self.sems:
            self.sems[name] = self.ctx.enter_context(self.nc.semaphore(name))
        return self.sems[name]

    def view(self, name):
        for tensor, where in self.tables:
            if name in where:
                at, n = where[name]
                return tensor[:, at:at + n]
        raise KeyError(name)

    def col(self, name, c, rows=P):
        return self.view(name)[0:rows, c:c + 1]


class Own:

    def __init__(self, engine, sem, base=0):
        self.engine, self.sem, self.base, self.n = engine, sem, base, 0

    def mark(self, instruction):
        instruction.then_inc(self.sem, 1)
        self.n += 1
        return self.n

    def settle(self, n=None):
        self.engine.wait_ge(self.sem, self.base + (self.n if n is None else n))

    def link(self, instruction):
        self.mark(instruction)
        self.settle()


def blk(b, n=P):
    return slice(b * n, (b + 1) * n)


def bf(ap):
    return ap.bitcast(F32)


def tensor_program(pr, pe):
    nc, m, acc, misc, sem = pr.nc, pr.m, pr.acc, pr.misc, pr.sem
    mm, turn = nc.tensor.matmul, nc.tensor.transpose
    ident, ones = pr.view("ident"), pr.view("ones")
    x_hi, x_lo, y_hi, y_lo = m["x_hi"], m["x_lo"], m["y_hi"], m["y_lo"]

    def claim(t):
        pe.wait_ge(sem("weights_split"), t + 1)
        if not isinstance(t, int) or t >= RING:
            pe.wait_ge(sem("tile_out"), t - RING + 1)

    def dense(t, slot, hi, lo, kc=KC, n=S, ready=None, first=1):
        claim(t)
        out = acc[:, slot, 0:n]
        for k in range(kc):
            if ready:
                pe.wait_ge(sem(ready), first + k)
            mm(out, m["w_hi"][:, slot, k], hi[:, k, 0:n], start=k == 0, stop=False)
            mm(out, m["w_hi"][:, slot, k], lo[:, k, 0:n], start=False, stop=False)
            last = mm(out, m["w_lo"][:, slot, k], hi[:, k, 0:n], start=False, stop=k == kc - 1)
        last.then_inc(sem("tile_done"), 1)

    def opening(t0, first_tile, norm):
        slots = [(first_tile + j) % RING for j in range(3)]
        for j in range(3):
            claim(t0 + j)
        for k in range(KC):
            pe.wait_ge(sem("norm_ready"), chunks_before(norm) + k + 1)
            for slot in slots:
                out = acc[:, slot]
                mm(out, m["w_hi"][:, slot, k], x_hi[:, k], start=k == 0, stop=False)
                mm(out, m["w_hi"][:, slot, k], x_lo[:, k], start=False, stop=False)
                last = mm(out, m["w_lo"][:, slot, k], x_hi[:, k], start=False, stop=k == KC - 1)
                if k == KC - 1:
                    last.then_inc(sem("tile_done"), 1)

    def tokens(t0, width, hi, lo, blocks):
        per = TILE // width
        tiles = KC // per
        pe.wait_ge(sem("tile_out"), t0)
        for j in range(tiles):
            claim(t0 + j)
            w_hi, w_lo = (m[w][:, (t0 + j) % RING].rearrange("p k n -> p (k n)") for w in ("w_hi", "w_lo"))
            for b in range(blocks):
                per_bank = 512 // width
                first, final = b % per_bank == 0, b % per_bank == per_bank - 1
                out = acc[:, (t0 + b // per_bank) % RING, blk(b % per_bank, width)]
                for i in range(per):
                    k = j * per + i
                    mm(out, hi[:, k, blk(b)], w_hi[:, blk(i, width)], start=k == 0 and first, stop=False)
                    mm(out, hi[:, k, blk(b)], w_lo[:, blk(i, width)], start=False, stop=False)
                    last = mm(out, lo[:, k, blk(b)], w_hi[:, blk(i, width)], start=False,
                              stop=k == KC - 1 and final)
            last.then_inc(sem("tile_done"), 1)

    def stage(name, hi, lo, n, at=0, width=S, norm=None, ready=None):
        if norm:
            opening(START[name], START[name], norm)
        for i in range(3 if norm else 0, n):
            t = START[name] + at + i
            dense(t, t % RING, hi, lo, n=width, ready=ready if i == 0 else None)

    def sum_squares(name, n=S):
        pe.wait_ge(sem("norm_added"), chunks_before(name) + KC)
        mm(misc[:, 1, 0:n], ones, m["sum_sq"][:, 0:n], start=True, stop=True).then_inc(sem("norm_summed"), 1)

    def sum_features(name, part):
        i = LAYER_NORMS.index(name)
        pe.wait_ge(sem("ln_sum"), 2 * i + part + 1)
        if part:
            pe.wait_ge(sem("ln_mean_out"), 3 * i + 1)
        mm(misc[:, 0, :], ones, m["sum_h"], start=True, stop=True).then_inc(sem("ln_mean"), 1)

    pe.wait_ge(sem("const_in"), 16)
    sum_squares("mix")
    opening(0, 0, "mix")
    pe.wait_ge(sem("norm_rstd"), 1)
    sum_squares("mem", MEM)
    stage("mix_in", x_hi, x_lo, 10, at=3)
    tokens(13, 256, x_hi, x_lo, TB)
    stage("mix_in", x_hi, x_lo, 2, at=15)
    pe.wait_ge(sem("norm_ready"), chunks_before("mem") + KC)
    stage("mem_kv", m["mn_hi"], m["mn_lo"], 8, width=MEM)
    for half in range(2):
        tokens(START["mem_kv"] + 8 + 4 * half, 512, m["mn_hi"], m["mn_lo"], MEM // P)

    ws = pr.view("wsT").rearrange("p (h t) -> p h t", h=4)
    b_s = pr.view("b_s")
    pe.wait_ge(sem("small1_in"), 16)
    pe.wait_ge(sem("v_a_ready"), 1)
    for c in range(2):
        for tb in range(TB):
            for hh in range(2):
                head = 2 * c + hh
                out = misc[blk(hh, 64), c, blk(tb)]
                mm(out, m["v_tok"][:, tb, blk(head, 64)], ws[:, head], start=True, stop=False)
                last = mm(out, ones[0:1, 0:64], b_s[0:1, blk(head)], start=False, stop=True)
        last.then_inc(sem("gating"), 1)

    pe.wait_ge(sem("rows"), 2)
    for sb in range(TB):
        last = turn(misc[:, 3, blk(sb, 4)], m["z"][0:4, 0, blk(sb)], ident[0:4, 0:4])
    last.then_inc(sem("g_turned"), 1)

    row_sel = pr.view("row_sel").rearrange("p (h n) -> p h n", h=4)
    den_sel = pr.view("den_sel").rearrange("p (h n) -> p h n", h=4)
    wqkv = pr.view("wqkv").rearrange("p (x h e) -> p x h e", x=3, h=4)

    def std_mean(i, src, avg, ready, count):
        pe.wait_ge(sem(ready), count)
        if i >= 2:
            pe.wait_ge(sem("std_centred"), i - 1)
        mm(misc[:, i % 2, :], pr.view(avg), src, start=True, stop=True).then_inc(sem("std_mean"), 1)

    def std_var(i, avg):
        pe.wait_ge(sem("std_sq"), i + 1)
        if i >= 2:
            pe.wait_ge(sem("std_rstd"), i - 1)
        mm(misc[:, 2 + i % 2, :], pr.view(avg), m["sq"][:, i % 2], start=True, stop=True)\
            .then_inc(sem("std_var"), 1)

    pe.wait_ge(sem("y_ready"), 2)
    pe.wait_ge(sem("g_col"), 1)
    for c in range(2):
        std_mean(c, m["conv_b"][:, c], "avg64", "conv_b", c + 1)
    for c in range(2):
        std_var(c, "avg64")
    pe.wait_ge(sem("std_rstd"), 2)

    for head in range(4):
        pe.wait_ge(sem("xconv"), head + 1)
        if head:
            pe.wait_ge(sem("p_c"), 4 * head)
            pe.wait_ge(sem("cell_out"), head)
            pe.wait_ge(sem("den_added"), head)
        xconv = m["xconv"][:, head]
        mm(misc[:, 0, :], wqkv[:, 0, head], xconv, start=True, stop=True).then_inc(sem("qkv"), 1)
        mm(misc[:, 1, :], wqkv[:, 1, head], xconv, start=True, stop=True).then_inc(sem("qkv"), 1)
        for tb in range(TB):
            at = CONV_C - 1 + tb * P
            last = mm(misc[:, 2, blk(tb)], m["xc"][:, head, at:at + P], wqkv[:, 2, head], start=True, stop=True)
        last.then_inc(sem("qkv"), 1)
        pe.wait_ge(sem("rows"), 3)
        mm(misc[:, 3, :], row_sel[0:4, head], m["row_M"][0:4], start=True, stop=True).then_inc(sem("M_spread"), 1)
        pe.wait_ge(sem("qkv_out"), 3 * head + 3)

        def scores(sb):
            mm(misc[:, sb % 2, sb * P:S], m["k_c"][:, blk(sb)], m["q_c"][:, sb * P:S], start=True, stop=True)\
                .then_inc(sem("scores_c"), 1)

        scores(0)
        scores(1)
        for sb in range(TB):
            pe.wait_ge(sem("p_c"), 4 * head + sb + 1)
            p = m["p_c"][:, sb, sb * P:S]
            mm(misc[:, 2, sb * P:S], m["v_c"][:, sb], p, start=sb == 0, stop=sb == TB - 1)
            last = mm(misc[0:4, 3, sb * P:S], den_sel[:, head], p, start=sb == 0, stop=sb == TB - 1)
            if sb + 2 < TB:
                scores(sb + 2)
        last.then_inc(sem("cell_sum"), 1)

    pe.wait_ge(sem("den_ready"), 1)
    for head in range(4):
        if head == 2:
            pe.wait_ge(sem("cell_out"), 4)
        mm(misc[:, head, :], row_sel[0:4, head], m["row_den"][0:4], start=True, stop=True)\
            .then_inc(sem("den_spread"), 1)
    for i in range(2, 6):
        std_mean(i, m["cell"][:, i - 2], "avg128", "cell_ready", 4)
    for i in range(2, 6):
        std_var(i, "avg128")

    stage("mix_out", y_hi, y_lo, KC, ready="y_ready")
    sum_squares("xat")
    stage("xq", x_hi, x_lo, KC, norm="xat")

    def x_scores(head):
        for tb in range(TB):
            i = 4 * head + tb
            if i == 0:
                pe.wait_ge(sem("tile_out"), END["xq"])
            if i >= 2:
                pe.wait_ge(sem("xa_exp"), i - 1)
            for c in range(2):
                last = mm(misc[:, tb % 2, 0:MEM], m["q_x"][:, 2 * head + c, blk(tb)], m["mem_k"][:, 2 * head + c],
                          start=c == 0, stop=c == 1)
            last.then_inc(sem("xa_scores"), 1)

    x_scores(0)
    for head in range(4):
        if head < 3:
            x_scores(head + 1)
        if head:
            pe.wait_ge(sem("xa_pt"), 2 * head)
        for tb in range(TB):
            pe.wait_ge(sem("xa_p"), 4 * head + tb + 1)
            for mb in range(2):
                last = turn(misc[:, 2 + mb, blk(tb)], m["p_x"][:, head % 2, tb, blk(mb)], ident)
        last.then_inc(sem("xa_turned"), 1)
        pe.wait_ge(sem("xa_pt"), 2 * head + 2)
        for e in range(2):
            c = 2 * head + e
            if head >= 2:
                pe.wait_ge(sem("xa_y"), c - 3)
            for mb in range(2):
                last = mm(acc[:, c % 4, :], m["mem_v"][:, mb, blk(c)], m["pt_x"][:, mb], start=mb == 0, stop=mb == 1)
            last.then_inc(sem("xa_o"), 1)
    pe.wait_ge(sem("xa_y"), KC)
    stage("xo", y_hi, y_lo, KC)

    sum_squares("ffn")

    def glu_group(g, t0, n):
        opening(t0, START["glu0"], "ffn")
        for j in range(3, 2 * n):
            dense(t0 + j, (START["glu0"] + j) % RING, x_hi, x_lo)
        for c in range(KC):
            j = 2 * n + c
            dense(t0 + j, (START["glu0"] + j) % RING, y_hi, y_lo, kc=n,
                  ready="glu_hidden" if c == 0 else None, first=8 * g + 1)

    with pe.Fori(0, 2) as g:
        glu_group(g, g * 24 + START["glu0"], 8)
    glu_group(2, START["glu2"], 6)
    sum_squares("fin")

    stage("nsa_in", x_hi, x_lo, 5, norm="fin")
    tokens(START["nsa_in"] + 5, 256, x_hi, x_lo, TB)
    stage("nsa_in", x_hi, x_lo, 8, at=7)
    for tb in range(TB):
        last = turn(misc[:, 2, tb * 32:tb * 32 + 24], m["gate_f"][0:24, blk(tb)], ident[0:24, 0:24])
    last.then_inc(sem("gates_turned"), 1)
    pe.wait_ge(sem("small2_in"), 16)
    pe.wait_ge(sem("w_cmp_in"), 16)
    pe.wait_ge(sem("blocks"), 4)
    for i in range(2):
        for j in range(CMP_BLOCK):
            last = mm(misc[:, 0, i * 32:i * 32 + N_CMP], m["w_cmp"][:, i, j], m["blocks"][:, i, :, j],
                      start=j == 0, stop=j == CMP_BLOCK - 1)
    last.then_inc(sem("cmp_hidden"), 1)
    cmp_w2 = pr.view("cmp_w2").rearrange("p (i e) -> p i e", i=2)
    pe.wait_ge(sem("gate_t"), 1)
    pe.wait_ge(sem("cmp_act"), 2)
    mm(misc[:, 3, 0:N_CMP], cmp_w2[:, 0], m["hid_c"][:, 0, 0:N_CMP], start=True, stop=True)\
        .then_inc(sem("cmp_kv"), 1)
    mm(misc[0:N_CMP, 2, 256:384], m["hid_c"][:, 1, 0:N_CMP], cmp_w2[:, 1], start=True, stop=True)\
        .then_inc(sem("cmp_kv"), 1)
    pe.wait_ge(sem("cmp_kv_out"), 2)
    pe.wait_ge(sem("tile_out"), START["nsa_in"] + 11)
    for g in range(2):
        for tb in range(TB):
            for c in range(4):
                at = (tb * 4 + c) * 32
                last = mm(misc[:, g, at:at + N_CMP], m["q_n"][blk(g, 64), c, blk(tb)], m["kc"][blk(g, 64), 0:N_CMP],
                          start=True, stop=True)
        last.then_inc(sem("cmp_scores"), 1)
    pe.wait_ge(sem("cmp_p"), 2)
    for g in range(2):
        for c in range(4):
            if g:
                pe.wait_ge(sem("cmp_pt"), c + 1)
            for tb in range(TB):
                last = turn(misc[0:N_CMP, c, blk(tb)], m["e_c"][:, g, tb * 4 + c, 0:N_CMP], ident)
            last.then_inc(sem("cmp_turned"), 1)
    pe.wait_ge(sem("cmp_pt"), 8)
    pe.wait_ge(sem("tile_out"), END["nsa_in"])

    def n_scores(i, tb):
        c, g, br = i // 4, i // 2 % 2, i % 2
        n = (tb + 1) * P
        if 4 * i + tb >= 2:
            pe.wait_ge(sem("n_exp"), 4 * i + tb - 1)
        mm(acc[:, tb % 2, 0:n], m["q_n"][blk(g, 64), c, blk(tb)], m["k_br"][blk(g, 64), br, 0:n], start=True, stop=False)
        mm(acc[:, tb % 2, tb * P:n], ident, pr.view("causal_neg"), start=False, stop=True)\
            .then_inc(sem("n_scores"), 1)

    for tb in range(TB):
        n_scores(0, tb)
    for i in range(16):
        c, g, br = i // 4, i // 2 % 2, i % 2
        if i < 15:
            n_scores(i + 1, 0)
            n_scores(i + 1, 1)
        pe.wait_ge(sem("n_p"), 4 * i + 4)
        for sb in range(TB):
            for tb in range(sb, TB):
                last = turn(misc[:, sb, blk(tb)], m["p_n"][:, i % 2, tb, blk(sb)], ident)
            last.then_inc(sem("n_turned"), 1)
        if i < 15:
            n_scores(i + 1, 2)
            n_scores(i + 1, 3)
        out = acc[blk(g, 64), 2 + c % 2]
        if br == 0:
            if c >= 2 and g == 0:
                pe.wait_ge(sem("n_y"), c - 1)
            mm(out, m["vc"][0:N_CMP, blk(g, 64)], m["pct%d" % g][0:N_CMP, c], start=True, stop=False)
        for sb in range(TB):
            pe.wait_ge(sem("n_pt"), 4 * i + sb + 1)
            last = mm(out[:, sb * P:S], m["v_br"][:, br, sb, blk(g, 64)], m["pt_n"][:, sb, sb * P:S],
                      start=False, stop=br == 1 and sb == TB - 1)
        last.then_inc(sem("n_o"), 1)
    pool_w = pr.view("pool_w").rearrange("p (g n) -> p g n", g=4)
    pe.wait_ge(sem("pool_r"), 4)
    for g in range(4):
        mm(misc[:, g, :], pool_w[:, g], m["u_n"][:, g, 16:], start=True, stop=True).then_inc(sem("pool_o"), 1)
    pe.wait_ge(sem("n_y"), KC)

    def normed_stage(name, norm):
        for c in range(KC):
            if c == HALF + 1:
                sum_features(norm, 0)
            dense(START[name] + c, (START[name] + c) % RING, y_hi, y_lo)
        sum_features(norm, 1)
        sum_squares(norm)

    def mlp_group(name, g, norm, hidden, next_norm=None):
        t0 = g * 16 + START[name]
        opening(t0, START[name], norm)
        for j in range(3, 16):
            slot = (START[name] + j) % RING
            if j < 8:
                dense(t0 + j, slot, x_hi, x_lo)
            else:
                if next_norm and j == 8 + HALF + 1:
                    sum_features(next_norm, 0)
                dense(t0 + j, slot, y_hi, y_lo, ready=hidden if j == 8 else None, first=g * 8 + 1)
        if next_norm:
            sum_features(next_norm, 1)
            sum_squares(next_norm)

    def mlp(name, norm, hidden, next_norm):
        with pe.Fori(0, GROUPS - 1) as g:
            mlp_group(name, g, norm, hidden)
        mlp_group(name, GROUPS - 1, norm, hidden, next_norm)

    normed_stage("nsa_out", "ln1a")
    mlp("mlp_a", "ln1a", "mlp_a_hidden", "ln2a")

    stage("gla_in", x_hi, x_lo, 9, norm="ln2a")
    gate_w2 = pr.view("gate_w2").rearrange("p (h n) -> p h n", h=4)
    pe.wait_ge(sem("tile_out"), START["gla_in"] + 1)
    for head in range(4):
        mm(misc[:, head, :], gate_w2[0:16, head], m["a_g"][0:16], start=True, stop=True).then_inc(sem("gla_z"), 1)
    for half in range(2):
        tokens(START["gla_in"] + 9 + 4 * half, 512, x_hi, x_lo, TB)
    stage("gla_in", x_hi, x_lo, 8, at=17)

    def gla_local(head):
        pe.wait_ge(sem("gla_k"), head + 1)
        if head:
            pe.wait_ge(sem("gla_att"), head)
            pe.wait_ge(sem("gla_kd"), head)
        for n in range(8):
            last = mm(misc[blk(n % 2, 64), 0, blk(n // 2, 64)], m["kt_g"][:, head, blk(n, 64)],
                      m["q_g"][:, head, blk(n, 64)], start=True, stop=True)
        last.then_inc(sem("gla_scores"), 1)
        for tb in range(TB):
            last = turn(misc[:, 3, blk(tb)], m["k_g"][:, head, blk(tb)], ident)
        last.then_inc(sem("gla_turned"), 1)
        pe.wait_ge(sem("gla_kd"), head + 1)
        for n in range(7):
            i = 7 * head + n
            if i >= 2:
                pe.wait_ge(sem("gla_state"), i - 1)
            mm(misc[:, 1 + i % 2, 0:256], m["kd_tok"][blk(n % 2, 64), n // 2], m["v_g"][blk(n % 2, 64), n // 2, blk(head, 256)],
               start=True, stop=True).then_inc(sem("gla_update"), 1)

    def gla_out(head):
        pe.wait_ge(sem("gla_att"), head + 1)
        pe.wait_ge(sem("gla_state"), 7 * head + 7)
        if head:
            pe.wait_ge(sem("gla_rstd"), head)
        for n in range(8):
            for e in range(2):
                at = e * 256 + n // 2 * 64
                out = acc[:, 2 * (head % 2) + n % 2, at:at + 64]
                mm(out, m["v_g"][blk(n % 2, 64), n // 2, head * 256 + e * P:head * 256 + (e + 1) * P],
                   m["att_g"][blk(n % 2, 64), n // 2], start=True, stop=False)
                last = mm(out, m["state"][:, n, blk(e)], m["q_g"][:, head, blk(n, 64)], start=False, stop=True)
        last.then_inc(sem("gla_o"), 1)

    def gla_sum(head):
        for e in range(2):
            pe.wait_ge(sem("gla_sq"), 2 * head + 2)
            last = mm(acc[:, 2 * ((head + 1) % 2), :], ones, m["sq"][:, e], start=e == 0, stop=e == 1)
        last.then_inc(sem("gla_ss"), 1)

    gla_local(0)
    pe.wait_ge(sem("tile_out"), END["gla_in"])
    for head in range(4):
        gla_out(head)
        gla_sum(head)
        if head < 3:
            gla_local(head + 1)
    pe.wait_ge(sem("gla_y"), KC)
    normed_stage("gla_out", "ln1b")
    mlp("mlp_b", "ln1b", "mlp_b_hidden", "ln2b")


def scalar_program(pr, act):
    nc, m, acc, misc, sem = pr.nc, pr.m, pr.acc, pr.misc, pr.sem
    f = nc.scalar.activation
    z = m["z"]
    own = Own(act, sem("act_step"))

    def out(t, slot, dst, func=ACT.Copy, src=None, **more):
        act.wait_ge(sem("tile_done"), t + 1)
        f(dst, acc[:, slot] if src is None else src, func, **more).then_inc(sem("tile_out"), 1)

    def out_wide(t, last, dst, func=ACT.Copy, src=None):
        act.wait_ge(sem("tile_done"), last + 1)
        f(dst, acc[:, t % RING] if src is None else src, func).then_inc(sem("tile_out"), 1)

    def rsqrt(dst, src, scale, eps, name):
        own.link(f(dst, src, ACT.Ln, bias=eps, scale=scale))
        f(dst, dst, ACT.Exp, scale=-0.5).then_inc(sem(name), 1)

    def square(name, k, src, n=S):
        if k >= 2:
            act.wait_ge(sem("norm_added"), chunks_before(name) + k - 1)
        f(m["sq"][:, k % 2, 0:n], src[:, k], ACT.Square).then_inc(sem("norm_sq"), 1)

    def rms_rstd(name, n=S):
        act.wait_ge(sem("norm_summed"), NORMS.index(name) + 1)
        rsqrt(m["rstd"][:, 0:n], misc[:, 1, 0:n], 1.0 / D, RMS_EPS, "norm_rstd")

    def residual_rms(name, resid, first, take_out):
        for k in range(KC):
            take_out(k)
            if k:
                act.wait_ge(sem(resid), first + k - 1)
                square(name, k - 1, m["h"])
        act.wait_ge(sem(resid), first + KC - 1)
        square(name, KC - 1, m["h"])
        rms_rstd(name)

    def residual_ln(name, resid, first, take_out):
        i = LAYER_NORMS.index(name)
        for k in range(HALF + 1):
            take_out(k)
        act.wait_ge(sem("ln_mean"), 2 * i + 1)
        f(m["mean"], misc[:, 0, :], ACT.Copy, scale=1.0 / (HALF * P)).then_inc(sem("ln_mean_out"), 1)
        for k in range(HALF):
            act.wait_ge(sem("ln_centred"), HALF * i + k + 1)
            square(name, k, m["h"])
        for k in range(HALF, KC):
            if k > HALF:
                take_out(k)
            act.wait_ge(sem(resid), first + k)
            square(name, k, m["h"])
        act.wait_ge(sem("ln_mean"), 2 * i + 2)
        f(m["mean"], misc[:, 0, :], ACT.Copy, scale=1.0 / D).then_inc(sem("ln_mean_out"), 1)
        act.wait_ge(sem("norm_added"), chunks_before(name) + KC)
        f(m["sq"][:, 0], misc[:, 0, :], ACT.Square, scale=1.0 / D).then_inc(sem("ln_mean_out"), 1)
        act.wait_ge(sem("ln_var"), i + 1)
        rsqrt(m["rstd"], m["rstd"], 1.0, LN_EPS, "norm_rstd")
        bias, at = name[:3] + "_b", KC * (name[3] == "b")
        for k in range(KC):
            act.wait_ge(sem("ln_scaled"), KC * i + k + 1)
            b = pr.col(bias, at + k)
            f(m["h"][:, k], m["xt"][:, k % 2], ACT.Identity, bias=b).then_inc(sem("ln_out"), 1)
            if name != LAYER_NORMS[-1]:
                f(m["x_hi"][:, k], m["xt"][:, k % 2], ACT.Identity, bias=b).then_inc(sem("ln_out"), 1)

    def stage_out(name, resid):
        def take_out(k):
            t = START[name] + k
            if k >= RING:
                act.wait_ge(sem(resid), k - RING + 1)
            out(t, t % RING, z[:, t % RING])
        return take_out

    act.dma_start(m["small1"], pr.dram["small1"]).then_inc(sem("small1_in"), 16)

    for k in range(KC):
        act.wait_ge(sem("x_in%d" % (k // HALF)), 16)
        square("mix", k, m["h"])
    rms_rstd("mix")
    act.wait_ge(sem("mem_in"), 16)
    for k in range(KC):
        square("mem", k, m["mem_in"], MEM)
    rms_rstd("mem", MEM)
    act.wait_ge(sem("par_in"), 16)
    act.wait_ge(sem("tile_done"), 1)
    own.mark(f(z[0:4, 0], acc[0:4, 0], ACT.Identity, bias=pr.col("b_igate", 0, 4)))
    out(0, 0, z[0:4, 1], src=acc[32:36, 0])
    for c in range(4):
        out(1 + c, (1 + c) % RING, m["xc"][:, c, CONV_C - 1:])
    for c in range(2):
        out(5 + c, (5 + c) % RING, m["b_in"][:, c, CONV_B - 1:])
    for c in range(2):
        out(7 + c, (7 + c) % RING, z[:, 2 + c], ACT.Sigmoid)
    for c in range(4):
        out(9 + c, (9 + c) % RING, m["oc_gate"][:, c], ACT.Sigmoid)
    for i in range(2):
        out_wide(13 + i, 14, m["v_tok"][:, 2 * i:2 * i + 2], ACT.Gelu,
                 src=acc[:, (13 + i) % RING].rearrange("p (b n) -> p b n", b=2))
    for c in range(2):
        out(15 + c, (15 + c) % RING, m["u_a"][:, c], ACT.Gelu)
    for c in range(4):
        act.wait_ge(sem("xconv_pre"), c + 1)
        f(m["xconv"][:, c], m["xconv"][:, c], ACT.Silu).then_inc(sem("xconv"), 1)

    fr, rt = z[0:4, 1], m["row_t"][0:4]
    own.link(f(fr, fr, ACT.Identity, bias=pr.col("b_fgate", 0, 4)))
    own.link(f(rt, fr, ACT.Abs))
    own.link(f(rt, rt, ACT.Exp, scale=-1.0))
    f(rt, rt, ACT.Ln, bias=1.0).then_inc(sem("row_ln"), 1)
    act.wait_ge(sem("v_a_stats"), 1)
    rsqrt(m["v_rstd"], m["v_mv"][:, :, 1], 1.0, LN_EPS, "v_a_rstd")
    act.wait_ge(sem("rows"), 4)
    f(m["row_em"][0:4], m["row_em"][0:4], ACT.Exp, scale=-1.0).then_inc(sem("row_em"), 1)

    for c in range(8):
        t = START["mem_kv"] + c
        out(t, t % RING, m["mem_k"][:, c], src=acc[:, t % RING, 0:MEM])
    for half in range(2):
        t = START["mem_kv"] + 8 + 4 * half
        out_wide(t, t + 3, m["mem_v"][:, 0, blk(half, 512)])
        f(m["mem_v"][:, 1, blk(half, 512)], acc[:, (t + 1) % RING], ACT.Copy).then_inc(sem("tile_out"), 3)
    act.wait_ge(sem("g_turned"), 1)
    f(m["g_col"], misc[:, 3, 0:16].rearrange("p (b h) -> p b h", b=TB), ACT.Copy).then_inc(sem("g_col"), 1)

    ring = [m["rstd"], m["mean"]]

    def std(i, src):
        act.wait_ge(sem("std_centred"), i + 1)
        if i >= 2:
            act.wait_ge(sem("std_var"), i - 1)
        f(m["sq"][:, i % 2], src, ACT.Square).then_inc(sem("std_sq"), 1)

    def std_rstd(i):
        act.wait_ge(sem("std_var"), i + 1)
        if i >= 2:
            act.wait_ge(sem("std_scaled"), i - 1)
        rsqrt(ring[i % 2], misc[:, 2 + i % 2, :], 1.0, LN_EPS, "std_rstd")

    for c in range(2):
        std(c, m["conv_b"][:, c])
    for c in range(2):
        std_rstd(c)
    for c in range(2):
        act.wait_ge(sem("std_scaled"), c + 1)
        f(m["conv_b"][:, c], m["conv_b"][:, c], ACT.Silu, scale=pr.col("gn_b_g", c), bias=pr.col("gn_b_b", c))\
            .then_inc(sem("conv_b_act"), 1)

    for head in range(4):
        for x, dst in enumerate((m["q_c"], m["k_c"], m["v_c"])):
            act.wait_ge(sem("qkv"), 3 * head + x + 1)
            src = misc[:, x, :] if x < 2 else misc[:, x, :].rearrange("p (b n) -> p b n", b=TB)
            f(dst, src, ACT.Copy).then_inc(sem("qkv_out"), 1)
        for sb in range(TB):
            act.wait_ge(sem("gap"), 4 * head + sb + 1)
            w = m["w_c"][:, sb, sb * P:]
            f(w, w, ACT.Exp, scale=-1.0).then_inc(sem("w_exp"), 1)
        act.wait_ge(sem("cell_sum"), head + 1)
        f(m["cell"][:, head], misc[:, 2, :], ACT.Copy).then_inc(sem("cell_out"), 1)
    act.wait_ge(sem("den_added"), 4)
    f(m["row_den"][0:4], m["row_den"][0:4], ACT.Abs).then_inc(sem("den_abs"), 1)
    for i in range(2, 6):
        std(i, m["cell"][:, i - 2])
        if i >= 3:
            std_rstd(i - 1)
    std_rstd(5)

    residual_rms("xat", "mix_resid", 1, stage_out("mix_out", "mix_resid"))
    for c in range(KC):
        t = START["xq"] + c
        out(t, t % RING, m["q_x"][:, c])

    def x_exp(head):
        for tb in range(TB):
            act.wait_ge(sem("xa_max"), 4 * head + tb + 1)
            if head >= 2:
                act.wait_ge(sem("xa_turned"), head - 1)
            f(m["p_x"][:, head % 2, tb], misc[:, tb % 2, 0:MEM], ACT.Exp, scale=1.0 / 16, bias=m["xa_neg"][:, tb:tb + 1],
              accum_out=m["xa_sum"][:, tb:tb + 1]).then_inc(sem("xa_exp"), 1)

    x_exp(0)
    for head in range(4):
        if head < 3:
            x_exp(head + 1)
        act.wait_ge(sem("xa_turned"), head + 1)
        for mb in range(2):
            f(m["pt_x"][:, mb], misc[:, 2 + mb, :], ACT.Copy).then_inc(sem("xa_pt"), 1)
    residual_rms("ffn", "xo_resid", 1, stage_out("xo", "xo_resid"))

    def glu_group(g, t0, n, norm=None):
        for j in range(n):
            t = t0 + 2 * j
            slot = (START["glu0"] + 2 * j) % RING
            act.wait_ge(sem("glu_conv"), g * 8 + (j + 1))
            out(t, slot, m["g_in"][:, j % 2, CONV_F - 1:])
            act.wait_ge(sem("glu_conv"), g * 8 + (j + 3))
            f(m["g_act"][:, j % 2], m["g_act"][:, j % 2], ACT.Gelu).then_inc(sem("glu_gelu"), 1)
            if j < 2:
                act.wait_ge(sem("glu_resid"), g * 8 + 2)
            else:
                act.wait_ge(sem("glu_hidden"), g * 8 + (j - 1))
            out(t + 1, (slot + 1) % RING, z[:, (slot + 1) % RING])

        def take_out(c):
            t = t0 + 2 * n + c
            slot = (START["glu0"] + 2 * n + c) % RING
            if c >= RING:
                act.wait_ge(sem("glu_resid"), g * 8 + (2 + c - RING + 1))
            out(t, slot, z[:, slot])

        if norm:
            residual_rms(norm, "glu_resid", 2 + g * 8 + 1, take_out)
        else:
            for c in range(KC):
                take_out(c)

    with act.Fori(0, 2) as g:
        glu_group(g, g * 24 + START["glu0"], 8)
    glu_group(2, START["glu2"], 6, "fin")
    act.dma_start(m["small2"], pr.dram["small2"]).then_inc(sem("small2_in"), 16)
    act.dma_start(m["w_cmp"], pr.dram["w_cmp"]).then_inc(sem("w_cmp_in"), 16)

    t0 = START["nsa_in"]
    out(t0, t0 % RING, m["gate_f"][0:24], ACT.Sigmoid, src=acc[0:24, t0 % RING])
    for dst, j in ((m["k_cmp"][:, 0], 1), (m["k_cmp"][:, 1], 2), (m["k_br"][:, 0], 3), (m["k_br"][:, 1], 4)):
        out(t0 + j, (t0 + j) % RING, dst)
    for i in range(2):
        out_wide(t0 + 5 + i, t0 + 6, m["v_br"].rearrange("p r b n -> p b r n")[:, 2 * i:2 * i + 2],
                 src=acc[:, (t0 + 5 + i) % RING].rearrange("p (b r n) -> p b r n", b=2, r=2))
    for c in range(4):
        out(t0 + 7 + c, (t0 + 7 + c) % RING, m["q_n"][:, c])
    for c in range(4):
        out(t0 + 11 + c, (t0 + 11 + c) % RING, m["u_n"][:, c, 16:])
    act.wait_ge(sem("gates_turned"), 1)
    f(m["gate_t"], misc[:, 2, 0:P].rearrange("p (b n) -> p b n", b=TB)[:, :, 0:24], ACT.Copy).then_inc(sem("gate_t"), 1)
    act.wait_ge(sem("cmp_hidden"), 1)
    for i in range(2):
        f(m["hid_c"][:, i, 0:N_CMP], misc[:, 0, i * 32:i * 32 + N_CMP], ACT.Gelu_apprx_tanh, bias=pr.col("cmp_b1", i))\
            .then_inc(sem("cmp_act"), 1)
    act.wait_ge(sem("cmp_kv"), 1)
    f(m["kc"][:, 0:N_CMP], misc[:, 3, 0:N_CMP], ACT.Copy).then_inc(sem("cmp_kv_out"), 1)
    act.wait_ge(sem("cmp_kv"), 2)
    f(m["vc"][0:N_CMP], misc[0:N_CMP, 2, 256:384], ACT.Copy).then_inc(sem("cmp_kv_out"), 1)
    for g in range(2):
        act.wait_ge(sem("cmp_gap"), g + 1)
        e = m["e_c"][:, g, :, 0:N_CMP]
        f(e, e, ACT.Exp, scale=0.125).then_inc(sem("cmp_exp"), 1)
    for g in range(2):
        for c in range(4):
            act.wait_ge(sem("cmp_turned"), 4 * g + c + 1)
            f(m["pct%d" % g][0:N_CMP, c], misc[0:N_CMP, c, :], ACT.Copy).then_inc(sem("cmp_pt"), 1)

    def n_exp(i, tb):
        n = (tb + 1) * P
        act.wait_ge(sem("n_max"), 4 * i + tb + 1)
        if i >= 2 and tb == 0:
            act.wait_ge(sem("n_turned"), 4 * (i - 2) + 4)
        f(m["p_n"][:, i % 2, tb, 0:n], acc[:, tb % 2, 0:n], ACT.Exp, scale=0.125, bias=m["n_neg"][:, i % 2, tb:tb + 1],
          accum_out=m["n_sum"][:, i % 2, tb:tb + 1]).then_inc(sem("n_exp"), 1)

    act.wait_ge(sem("cmp_turned"), 8)
    for tb in range(TB):
        n_exp(0, tb)
    for i in range(16):
        if i < 15:
            n_exp(i + 1, 0)
            n_exp(i + 1, 1)
        for sb in range(TB):
            act.wait_ge(sem("n_turned"), 4 * i + sb + 1)
            if i:
                act.wait_ge(sem("n_o"), i)
            f(m["pt_n"][:, sb, sb * P:], misc[:, sb, sb * P:], ACT.Copy).then_inc(sem("n_pt"), 1)
        if i < 15:
            n_exp(i + 1, 2)
            n_exp(i + 1, 3)
    for g in range(4):
        act.wait_ge(sem("pool_o"), g + 1)
        f(m["u_n"][:, g, 16:], misc[:, g, :], ACT.Copy, scale=pr.col("pool_scale", g)).then_inc(sem("pool_out"), 1)
    residual_ln("ln1a", "nsa_resid", 1, stage_out("nsa_out", "nsa_resid"))

    def mlp(name, norm):
        hidden, resid = sem(name + "_hidden"), sem(name + "_resid")

        def mlp_out(g, j):
            t, slot = g * 16 + (START[name] + j), (START[name] + j) % RING
            if j < 4:
                act.wait_ge(resid, g * 8 + (j + 5))
            elif j < 12:
                act.wait_ge(hidden, g * 8 + (j - 3))
            else:
                act.wait_ge(resid, g * 8 + (8 + j - 8 - RING + 1))
            out(t, slot, z[:, slot], ACT.Relu if j < 8 else ACT.Copy)

        with act.Fori(0, GROUPS - 1) as g:
            for j in range(16):
                mlp_out(g, j)
        for j in range(8):
            mlp_out(GROUPS - 1, j)
        residual_ln(norm, name + "_resid", 8 * GROUPS + 1, lambda c: mlp_out(GROUPS - 1, 8 + c))

    mlp("mlp_a", "ln2a")

    t0 = START["gla_in"]
    out(t0, t0 % RING, m["a_g"][0:16], src=acc[0:16, t0 % RING])
    for c in range(4):
        out(t0 + 1 + c, (t0 + 1 + c) % RING, m["q_g"][:, c])
    for c in range(4):
        out(t0 + 5 + c, (t0 + 5 + c) % RING, m["k_g"][:, c])
    gz, gt, gb = m["gz"], m["gt"], m["gb"]
    for head in range(4):
        act.wait_ge(sem("gla_z"), head + 1)
        if head:
            act.wait_ge(sem("gla_k"), head)
        own.link(f(gz, misc[:, head, :], ACT.Identity, bias=pr.col("gate_b", head)))
        own.link(f(gt, gz, ACT.Abs))
        own.link(f(gt, gt, ACT.Exp, scale=-1.0))
        f(gt, gt, ACT.Ln, bias=1.0).then_inc(sem("gla_ln"), 1)
        act.wait_ge(sem("gla_b"), head + 1)
        f(gz, gb, ACT.Exp, scale=1.0 / 16).then_inc(sem("gla_exp"), 1)
        f(gt, gb, ACT.Exp, scale=-1.0 / 16).then_inc(sem("gla_exp"), 1)
        own.mark(f(m["decay"][:, head], gb.rearrange("p (n c) -> p n c", c=GLA_CHUNK)[:, :, GLA_CHUNK - 1],
                   ACT.Exp, scale=1.0 / 16))
        act.wait_ge(sem("gla_rest"), head + 1)
        f(gz, gz, ACT.Exp, scale=1.0 / 16).then_inc(sem("gla_exp"), 1)
        if head % 2:
            t = t0 + 9 + 4 * (head // 2)
            for b in range(TB):
                out_wide(t + b, t + 3, m["v_g"][:, b, blk(head // 2, 512)])
    for c in range(KC):
        out(t0 + 17 + c, (t0 + 17 + c) % RING, m["r_g"][:, c], ACT.Silu)

    def gla_kd(head):
        act.wait_ge(sem("gla_turned"), head + 1)
        f(m["kd_tok"], misc[:, 3, :].rearrange("p (b n) -> p b n", b=TB), ACT.Copy).then_inc(sem("gla_kd"), 1)

    gla_kd(0)
    for head in range(4):
        act.wait_ge(sem("gla_o"), head + 1)
        if head:
            act.wait_ge(sem("gla_y"), 2 * head)
        for odd in range(2):
            def chunks(a):
                return a.rearrange("p e (b odd c) -> p e b odd c", odd=2, c=GLA_CHUNK)[:, :, :, odd]
            src = acc[:, 2 * (head % 2) + odd, :].rearrange("p (e b c) -> p e b c", e=2, c=GLA_CHUNK)
            f(chunks(m["sq"]), src, ACT.Square).then_inc(sem("gla_sq"), 1)
            f(chunks(m["o_g"]), src, ACT.Copy).then_inc(sem("gla_o_out"), 1)
        act.wait_ge(sem("gla_ss"), head + 1)
        rsqrt(m["rstd"], acc[:, 2 * ((head + 1) % 2), :], 1.0 / 256, LN_EPS, "gla_rstd")
        if head < 3:
            gla_kd(head + 1)
    residual_ln("ln1b", "gla_resid", 1, stage_out("gla_out", "gla_resid"))
    mlp("mlp_b", "ln2b")


def vector_program(pr, dve):
    nc, m, acc, misc, sem = pr.nc, pr.m, pr.acc, pr.misc, pr.sem
    v = nc.vector
    z, h, xt = m["z"], m["h"], m["xt"]
    own = Own(dve, sem("dve_step"))

    def split(src, hi, lo, name, step=own):
        step.link(v.tensor_copy(hi, src))
        v.tensor_tensor(lo, src, bf(hi), ALU.subtract).then_inc(sem(name), 1)

    def add_squares(name, k, n=S):
        if k == 0:
            return
        before = chunks_before(name)
        dve.wait_ge(sem("norm_sq"), before + k + 1)
        total, sq = m["sum_sq"][:, 0:n], m["sq"][:, :, 0:n]
        if k == 1:
            if before:
                dve.wait_ge(sem("norm_summed"), NORMS.index(name))
            v.tensor_tensor(total, sq[:, 0], sq[:, 1], ALU.add).then_inc(sem("norm_added"), 2)
        else:
            dve.wait_ge(sem("norm_added"), before + k)
            v.tensor_tensor(total, total, sq[:, k % 2], ALU.add).then_inc(sem("norm_added"), 1)

    def rms(name, src, gain, hi, lo, n=S, keep=False):
        def place(k):
            return src[:, k] if keep else xt[:, k % 2, 0:n]

        def scale(k):
            return own.mark(v.scalar_tensor_tensor(place(k), src[:, k], pr.col(gain, k), m["rstd"][:, 0:n],
                                                   ALU.mult, ALU.mult))
        before = chunks_before(name)
        dve.wait_ge(sem("norm_rstd"), NORMS.index(name) + 1)
        scaled = scale(0)
        for k in range(KC):
            own.settle(scaled)
            high = own.mark(v.tensor_copy(hi[:, k], place(k)))
            if k + 1 < KC:
                if k:
                    dve.wait_ge(sem("norm_ready"), before + k)
                scaled = scale(k + 1)
            own.settle(high)
            v.tensor_tensor(lo[:, k], place(k), bf(hi[:, k]), ALU.subtract).then_inc(sem("norm_ready"), 1)

    def residual_rms(name, add):
        for k in range(KC):
            add(k)
            if k >= 2:
                add_squares(name, k - 1)
        add_squares(name, KC - 1)

    def residual_ln(name, resid, first, prescale, add):
        i = LAYER_NORMS.index(name)
        total, mean = m["sum_h"], m["mean"]
        for k in range(HALF):
            add(k)
            if k == 0:
                continue
            dve.wait_ge(sem(resid), first + k)
            if k == 1:
                if i:
                    dve.wait_ge(sem("ln_mean"), 2 * i)
                own.link(v.tensor_tensor(total, h[:, 0], h[:, 1], ALU.add))
            elif k < HALF - 1:
                own.link(v.tensor_tensor(total, total, h[:, k], ALU.add))
            else:
                v.tensor_tensor(total, total, h[:, k], ALU.add).then_inc(sem("ln_sum"), 1)
        dve.wait_ge(sem("ln_mean_out"), 3 * i + 1)
        for k in range(HALF):
            v.tensor_tensor(h[:, k], h[:, k], mean, ALU.subtract).then_inc(sem("ln_centred"), 1)
        for k in range(HALF, KC):
            shifted = own.mark(v.scalar_tensor_tensor(h[:, k], h[:, k], prescale, mean, ALU.mult, ALU.subtract))
        own.mark(v.scalar_tensor_tensor(total, mean, -float(HALF), total, ALU.mult, ALU.add))
        for k in range(1, HALF):
            add_squares(name, k)
        own.settle()
        for k in range(HALF, KC):
            add(k, plain=True)
            dve.wait_ge(sem(resid), first + k)
            if k < KC - 1:
                own.link(v.tensor_tensor(total, total, h[:, k], ALU.add))
            else:
                v.tensor_tensor(total, total, h[:, k], ALU.add).then_inc(sem("ln_sum"), 1)
            add_squares(name, k)
        gain, at = name[:3] + "_g", KC * (name[3] == "b")
        dve.wait_ge(sem("norm_summed"), NORMS.index(name) + 1)
        dve.wait_ge(sem("ln_mean_out"), 3 * i + 3)
        v.scalar_tensor_tensor(m["rstd"], misc[:, 1, :], 1.0 / D, m["sq"][:, 0], ALU.mult, ALU.subtract)\
            .then_inc(sem("ln_var"), 1)

        def centre(k):
            return own.mark(v.tensor_tensor(h[:, k], h[:, k], mean, ALU.subtract))

        last_norm = name == LAYER_NORMS[-1]
        outs = 1 if last_norm else 2
        before = KC * 2 * i
        centred = [centre(k) for k in range(3)]
        dve.wait_ge(sem("norm_rstd"), NORMS.index(name) + 1)

        def rest(k):
            dve.wait_ge(sem("ln_out"), before + 2 * (k + 1))
            v.tensor_tensor(m["x_lo"][:, k], h[:, k], bf(m["x_hi"][:, k]), ALU.subtract).then_inc(sem("norm_ready"), 1)

        for k in range(KC):
            own.settle(centred[k])
            if k >= 2:
                dve.wait_ge(sem("ln_out"), before + outs * (k - 1))
            v.scalar_tensor_tensor(xt[:, k % 2], h[:, k], pr.col(gain, at + k), m["rstd"], ALU.mult, ALU.mult)\
                .then_inc(sem("ln_scaled"), 1)
            if k + 3 < KC:
                centred.append(centre(k + 3))
            if k and not last_norm:
                rest(k - 1)
        if not last_norm:
            rest(KC - 1)

    def stage_add(name, resid, scale=1.0):
        def add(k, plain=False):
            t = START[name] + k
            dve.wait_ge(sem("tile_out"), t + 1)
            if scale == 1.0 or plain:
                v.tensor_tensor(h[:, k], h[:, k], z[:, t % RING], ALU.add).then_inc(sem(resid), 1)
            else:
                v.scalar_tensor_tensor(h[:, k], h[:, k], scale, z[:, t % RING], ALU.mult, ALU.add)\
                    .then_inc(sem(resid), 1)
        return add

    for k in range(1, KC):
        add_squares("mix", k)
    dve.wait_ge(sem("par_in"), 16)
    rms("mix", h, "norm_mix_g", m["x_hi"], m["x_lo"])
    for k in range(1, KC):
        add_squares("mem", k, MEM)
    rms("mem", m["mem_in"], "norm_mem_g", m["mn_hi"], m["mn_lo"], MEM)
    own.mark(v.memset(m["xc"][:, :, 0:CONV_C - 1], 0.0))
    own.mark(v.memset(m["b_in"][:, :, 0:CONV_B - 1], 0.0))
    dve.wait_ge(sem("const_in"), 16)
    dve.wait_ge(sem("small1_in"), 16)
    ws = pr.view("wsT").rearrange("p (h t) -> p h t", h=4)
    dve.wait_ge(sem("norm_ready"), 2 * KC)
    own.mark(v.memset(xt[0:4, 1], 1.0))
    own.settle()
    for head in range(4):
        own.mark(v.tensor_tensor(ws[:, head], ws[:, head], pr.view("tri01"), ALU.mult))

    def conv_step(dst, src, w, bias):
        if bias is not None:
            return v.tensor_scalar(dst, src, w, bias, ALU.mult, ALU.add)
        return v.scalar_tensor_tensor(dst, src, w, dst, ALU.mult, ALU.add)

    dve.wait_ge(sem("tile_out"), 5)
    before = own.n
    for j in range(CONV_C):
        for c in range(4):
            if j:
                own.settle(before + 4 * (j - 1) + c + 1)
            step = conv_step(m["xconv"][:, c], m["xc"][:, c, j:j + S], pr.col("conv_c_w", 4 * j + c),
                             pr.col("conv_c_b", c) if j == 0 else None)
            if j < CONV_C - 1:
                own.mark(step)
            else:
                step.then_inc(sem("xconv_pre"), 1)
    dve.wait_ge(sem("tile_out"), 9)
    for c in range(2):
        own.mark(v.tensor_tensor(m["b_in"][:, c, CONV_B - 1:], m["b_in"][:, c, CONV_B - 1:], z[:, 2 + c], ALU.mult))

    dve.wait_ge(sem("tile_out"), 15)
    for tb in range(TB):
        own.mark(v.bn_stats(m["v_stats"][:, tb], m["v_tok"][:, tb]))
    own.settle()
    for tb in range(TB):
        last = v.bn_aggr(m["v_mv"][:, tb], m["v_stats"][:, tb])
        if tb < TB - 1:
            own.mark(last)
    last.then_inc(sem("v_a_stats"), 1)

    li, fr, row = z[0:4, 0], z[0:4, 1], lambda name: m[name][0:4]
    dve.wait_ge(sem("row_ln"), 1)
    own.link(v.scalar_tensor_tensor(fr, fr, 0.0, row("row_t"), ALU.min, ALU.subtract))
    v.tensor_tensor_scan(row("row_F"), xt[0:4, 1], fr, 0.0, ALU.mult, ALU.add).then_inc(sem("rows"), 1)
    dve.wait_ge(sem("rows"), 1)
    v.tensor_tensor(li, li, row("row_F"), ALU.subtract).then_inc(sem("rows"), 1)
    dve.wait_ge(sem("rows"), 2)
    v.tensor_tensor_scan(row("row_M"), li, li, 0.0, ALU.max, ALU.max).then_inc(sem("rows"), 1)
    dve.wait_ge(sem("rows"), 3)
    v.tensor_tensor(row("row_em"), row("row_F"), row("row_M"), ALU.add).then_inc(sem("rows"), 1)

    dve.wait_ge(sem("v_a_rstd"), 1)
    vt, mv = m["v_tok"], m["v_mv"]
    for tb in range(TB):
        own.mark(v.tensor_scalar(vt[:, tb], vt[:, tb], mv[:, tb, 0:1], m["v_rstd"][:, tb:tb + 1],
                                 ALU.subtract, ALU.mult))
    before = own.n - TB
    for tb in range(TB):
        own.settle(before + tb + 1)
        own.mark(v.tensor_tensor(vt[:, tb], vt[:, tb], pr.view("ln_a_g"), ALU.mult))
    for tb in range(TB):
        own.settle(before + TB + tb + 1)
        last = v.tensor_tensor(vt[:, tb], vt[:, tb], pr.view("ln_a_b"), ALU.add)
    last.then_inc(sem("v_a_ready"), 1)

    before = own.n
    for j in range(CONV_B):
        for c in range(2):
            if j:
                own.settle(before + 2 * (j - 1) + c + 1)
            elif c == 0:
                own.settle()
            step = conv_step(m["conv_b"][:, c], m["b_in"][:, c, j:j + S], pr.col("conv_b_w", 2 * j + c),
                             pr.col("conv_b_b", c) if j == 0 else None)
            if j < CONV_B - 1:
                own.mark(step)
            else:
                step.then_inc(sem("conv_b"), 1)

    for c in range(2):
        dve.wait_ge(sem("gating"), c + 1)
        own.link(v.tensor_tensor(xt[:, c], m["u_a"][:, c], misc[:, c, :], ALU.mult))
        split(xt[:, c], m["y_hi"][:, c], m["y_lo"][:, c], "y_ready")

    def centre(i, src):
        dve.wait_ge(sem("std_mean"), i + 1)
        v.tensor_tensor(src, src, misc[:, i % 2, :], ALU.subtract).then_inc(sem("std_centred"), 1)

    ring = [m["rstd"], m["mean"]]
    for c in range(2):
        centre(c, m["conv_b"][:, c])
    for c in range(2):
        dve.wait_ge(sem("std_rstd"), c + 1)
        v.tensor_tensor(m["conv_b"][:, c], m["conv_b"][:, c], ring[c], ALU.mult).then_inc(sem("std_scaled"), 1)
    for c in range(2):
        dve.wait_ge(sem("conv_b_act"), c + 1)
        own.link(v.tensor_copy(xt[:, c], m["conv_b"][:, c]))
        split(xt[:, c], m["y_hi"][:, 2 + c], m["y_lo"][:, 2 + c], "y_ready")

    dve.wait_ge(sem("g_col"), 1)
    for head in range(4):
        dve.wait_ge(sem("M_spread"), head + 1)
        for sb in range(TB):
            v.tensor_scalar(m["w_c"][:, sb, sb * P:], misc[:, 3, sb * P:], m["g_col"][:, sb, head:head + 1], 0.0,
                            ALU.subtract, ALU.max).then_inc(sem("gap"), 1)
        for sb in range(TB):
            dve.wait_ge(sem("w_exp"), 4 * head + sb + 1)
            own.link(v.tensor_tensor(m["w_c"][:, sb, blk(sb)], m["w_c"][:, sb, blk(sb)], pr.view("tri01"), ALU.mult))
            dve.wait_ge(sem("scores_c"), 4 * head + sb + 1)
            v.scalar_tensor_tensor(m["p_c"][:, sb, sb * P:], misc[:, sb % 2, sb * P:], float(P) ** -0.5,
                                   m["w_c"][:, sb, sb * P:], ALU.mult, ALU.mult).then_inc(sem("p_c"), 1)
        dve.wait_ge(sem("cell_sum"), head + 1)
        den = row("row_den")
        if head == 0:
            v.tensor_copy(den, misc[0:4, 3, :]).then_inc(sem("den_added"), 1)
        else:
            dve.wait_ge(sem("den_added"), head)
            v.tensor_tensor(den, den, misc[0:4, 3, :], ALU.add).then_inc(sem("den_added"), 1)
    dve.wait_ge(sem("den_abs"), 1)
    dve.wait_ge(sem("row_em"), 1)
    own.link(v.tensor_tensor(den, den, row("row_em"), ALU.max))
    v.reciprocal(den, den).then_inc(sem("den_ready"), 1)
    dve.wait_ge(sem("cell_out"), 4)
    for head in range(4):
        dve.wait_ge(sem("den_spread"), head + 1)
        v.tensor_tensor(m["cell"][:, head], m["cell"][:, head], misc[:, head, :], ALU.mult)\
            .then_inc(sem("cell_ready"), 1)
    dve.wait_ge(sem("cell_ready"), 4)

    def cell_final(i):
        head = i - 2
        cell = m["cell"][:, head]
        x = xt[:, i % 2]
        dve.wait_ge(sem("std_rstd"), i + 1)
        v.scalar_tensor_tensor(x, cell, pr.col("hn_c_g", head), ring[i % 2], ALU.mult, ALU.mult)\
            .then_inc(sem("std_scaled"), 1)
        dve.wait_ge(sem("std_scaled"), i + 1)
        own.link(v.scalar_tensor_tensor(x, m["xconv"][:, head], pr.col("skip_c", head), x, ALU.mult, ALU.add))
        own.link(v.tensor_tensor(x, x, m["oc_gate"][:, head], ALU.mult))
        split(x, m["y_hi"][:, 4 + head], m["y_lo"][:, 4 + head], "y_ready")

    for i in range(2, 6):
        centre(i, m["cell"][:, i - 2])
        if i >= 4:
            cell_final(i - 2)
    cell_final(4)
    cell_final(5)
    residual_rms("xat", stage_add("mix_out", "mix_resid"))
    rms("xat", h, "norm_x_g", m["x_hi"], m["x_lo"])

    def x_max(head, tb):
        dve.wait_ge(sem("xa_scores"), 4 * head + tb + 1)
        own.link(v.tensor_reduce(m["xa_max"][:, tb:tb + 1], misc[:, tb % 2, 0:MEM], AX.X, ALU.max))
        v.tensor_scalar(m["xa_neg"][:, tb:tb + 1], m["xa_max"][:, tb:tb + 1], -1.0 / 16, None, ALU.mult)\
            .then_inc(sem("xa_max"), 1)

    def x_norm(head, tb):
        dve.wait_ge(sem("xa_exp"), 4 * head + tb + 1)
        own.link(v.reciprocal(m["xa_sum"][:, tb:tb + 1], m["xa_sum"][:, tb:tb + 1]))
        p = m["p_x"][:, head % 2, tb]
        v.tensor_scalar(p, p, m["xa_sum"][:, tb:tb + 1], None, ALU.mult).then_inc(sem("xa_p"), 1)

    def x_out(head):
        for c in (2 * head, 2 * head + 1):
            dve.wait_ge(sem("xa_o"), c + 1)
            split(acc[:, c % 4, :], m["y_hi"][:, c], m["y_lo"][:, c], "xa_y")

    x_max(0, 0)
    for i in range(16):
        if i < 15:
            x_max((i + 1) // 4, (i + 1) % 4)
        x_norm(i // 4, i % 4)
        if i % 4 == 3 and i > 3:
            x_out(i // 4 - 1)
    x_out(3)
    residual_rms("ffn", stage_add("xo", "xo_resid"))
    rms("ffn", h, "norm_ffn_g", m["x_hi"], m["x_lo"])

    for b in range(2):
        v.memset(m["g_in"][:, b, 0:CONV_F - 1], 0.0).then_inc(sem("glu_conv"), 1)
    dve.wait_ge(sem("norm_ready"), chunks_before("ffn") + KC)
    for b in range(2):
        v.memset(xt[:, b, 0:1], 0.0).then_inc(sem("glu_resid"), 1)
    dve.wait_ge(sem("glu_resid"), 2)
    conv_w = pr.view("conv_f_w").rearrange("p (j f) -> p j f", j=CONV_F)
    conv_bias = pr.view("conv_f_b")

    def glu_group(g, t0, n, step, norm=None):
        def scalar(view, j):
            if isinstance(g, int):
                return view[:, 8 * g + j:8 * g + j + 1]
            return view[:, j:j + 9][:, bass.ds(g * 8, 1)]
        for j in range(n):
            t = t0 + 2 * j
            slot = (START["glu0"] + 2 * j) % RING
            src, dst = m["g_in"][:, j % 2], m["g_act"][:, j % 2]
            dve.wait_ge(sem("tile_out"), t + 1)
            step.link(v.tensor_scalar(dst, src[:, 0:S], scalar(conv_w[:, 0], j), scalar(conv_bias, j),
                                      ALU.mult, ALU.add))
            step.link(v.scalar_tensor_tensor(dst, src[:, 1:S + 1], scalar(conv_w[:, 1], j), dst, ALU.mult, ALU.add))
            v.scalar_tensor_tensor(dst, src[:, 2:S + 2], scalar(conv_w[:, 2], j), dst, ALU.mult, ALU.add)\
                .then_inc(sem("glu_conv"), 1)
            dve.wait_ge(sem("glu_gelu"), g * 8 + (j + 1))
            dve.wait_ge(sem("tile_out"), t + 2)
            step.link(v.tensor_tensor(xt[:, j % 2], dst, z[:, (slot + 1) % RING], ALU.mult))
            split(xt[:, j % 2], m["y_hi"][:, j], m["y_lo"][:, j], "glu_hidden", step)

        def add(c):
            dve.wait_ge(sem("tile_out"), t0 + (2 * n + c + 1))
            slot = (START["glu0"] + 2 * n + c) % RING
            v.tensor_tensor(h[:, c], h[:, c], z[:, slot], ALU.add).then_inc(sem("glu_resid"), 1)

        if norm:
            residual_rms(norm, add)
        else:
            for c in range(KC):
                add(c)

    with dve.Fori(0, 2) as g:
        glu_group(g, g * 24 + START["glu0"], 8, Own(dve, sem("glu_step"), g * 32))
    glu_group(2, START["glu2"], 6, Own(dve, sem("glu_tail_step")), "fin")
    rms("fin", h, "final_g", m["x_hi"], m["x_lo"], keep=True)

    t0 = START["nsa_in"]
    pos = pr.view("cmp_pos").rearrange("p (i j) -> p i j", i=2)
    own.mark(v.memset(m["u_n"][:, :, 0:16], 0.0))
    for i in range(2):
        dve.wait_ge(sem("tile_out"), t0 + 2 + i)
        halves = m["k_cmp"][:, i].rearrange("p (b j) -> p b j", j=CMP_STRIDE)
        for half in range(2):
            j = blk(half, CMP_STRIDE)
            v.tensor_tensor(m["blocks"][:, i, :, j], halves[:, half:half + N_CMP],
                            pos[:, i, j].unsqueeze(1).to_broadcast([P, N_CMP, CMP_STRIDE]), ALU.add)\
                .then_inc(sem("blocks"), 1)

    gates = m["gate_t"].rearrange("p b (g c r) -> p b g c r", g=2, c=4)
    dve.wait_ge(sem("gate_t"), 1)
    dve.wait_ge(sem("small2_in"), 16)
    neg = pr.view("cmp_neg").rearrange("p (b n) -> p b n", b=16)[:, :, 0:N_CMP]
    seen = pr.view("cmp01").rearrange("p (b n) -> p b n", b=16)[:, :, 0:N_CMP]
    mx, sm = m["c_mx"], m["c_sum"]

    def spread(a):
        return a.unsqueeze(2).to_broadcast([P, 16, N_CMP])

    for g in range(2):
        e = m["e_c"][:, g, :, 0:N_CMP]
        dve.wait_ge(sem("cmp_scores"), g + 1)
        own.link(v.tensor_tensor(e, misc[:, g, :].rearrange("p (b n) -> p b n", b=16)[:, :, 0:N_CMP], neg, ALU.add))
        own.link(v.tensor_reduce(mx, e, AX.X, ALU.max))
        v.tensor_tensor(e, e, spread(mx), ALU.subtract).then_inc(sem("cmp_gap"), 1)
    for g in range(2):
        e = m["e_c"][:, g, :, 0:N_CMP]
        dve.wait_ge(sem("cmp_exp"), g + 1)
        own.link(v.tensor_tensor(e, e, seen, ALU.mult))
        own.link(v.tensor_reduce(sm, e, AX.X, ALU.add))
        own.link(v.tensor_scalar(sm, sm, 1e-30, None, ALU.max))
        own.link(v.reciprocal(sm, sm))
        own.link(v.tensor_tensor(sm.rearrange("p (b c) -> p b c", b=TB), sm.rearrange("p (b c) -> p b c", b=TB),
                                 gates[:, :, g, :, 0], ALU.mult))
        v.tensor_tensor(e, e, spread(sm), ALU.mult).then_inc(sem("cmp_p"), 1)

    dve.wait_ge(sem("tile_out"), END["nsa_in"])
    inv = pr.view("pool_inv").rearrange("p (g t) -> p g t", g=4)
    for g in range(4):
        u = m["u_n"][:, g]
        if g:
            dve.wait_ge(sem("pool_r"), g)
        src = u
        for step in range(g + 1):
            d = 2 ** step
            lo = 2 * d - 1
            dst = m["pool_s"][:, step % 2]
            own.link(v.tensor_tensor(dst[:, lo:], src[:, lo:], src[:, lo - d:S + 16 - d], ALU.add))
            src = dst
        other = m["pool_s"][:, (g + 1) % 2]
        own.link(v.tensor_tensor(other[:, 0:16], src[:, 16:32], inv[:, g], ALU.mult))
        own.mark(v.tensor_tensor(u[:, 16:32], other[:, 0:16], u[:, 16:32], ALU.subtract))
        v.scalar_tensor_tensor(u[:, 32:], src[:, 32:], 1.0 / 2 ** (g + 1), u[:, 32:], ALU.mult, ALU.subtract)\
            .then_inc(sem("pool_r"), 1)

    def n_max(i, tb):
        n = (tb + 1) * P
        dve.wait_ge(sem("n_scores"), 4 * i + tb + 1)
        own.link(v.tensor_reduce(m["n_max"][:, i % 2, tb:tb + 1], acc[:, tb % 2, 0:n], AX.X, ALU.max))
        v.tensor_scalar(m["n_neg"][:, i % 2, tb:tb + 1], m["n_max"][:, i % 2, tb:tb + 1], -0.125, None, ALU.mult)\
            .then_inc(sem("n_max"), 1)

    def n_final(i):
        c, g, br = i // 4, i // 2 % 2, i % 2
        r = m["n_r"][:, i % 2]
        dve.wait_ge(sem("n_exp"), 4 * i + 4)
        own.link(v.reciprocal(r, m["n_sum"][:, i % 2]))
        own.link(v.tensor_tensor(r, r, gates[:, :, g, c, 1 + br], ALU.mult))
        for tb in range(TB):
            p = m["p_n"][:, i % 2, tb, 0:(tb + 1) * P]
            v.tensor_scalar(p, p, r[:, tb:tb + 1], None, ALU.mult).then_inc(sem("n_p"), 1)

    def n_y(c):
        dve.wait_ge(sem("n_o"), 4 * c + 4)
        split(acc[:, 2 + c % 2, :], m["y_hi"][:, c], m["y_lo"][:, c], "n_y")

    for tb in range(TB):
        n_max(0, tb)
    for i in range(16):
        if i < 15:
            n_max(i + 1, 0)
            n_max(i + 1, 1)
        if i % 4 == 0 and i:
            n_y(i // 4 - 1)
        n_final(i)
        if i < 15:
            n_max(i + 1, 2)
            n_max(i + 1, 3)
    n_y(3)
    for g in range(4):
        dve.wait_ge(sem("pool_out"), g + 1)
        split(m["u_n"][:, g, 16:], m["y_hi"][:, 4 + g], m["y_lo"][:, 4 + g], "n_y")
    residual_ln("ln1a", "nsa_resid", 1, ALPHA, stage_add("nsa_out", "nsa_resid", ALPHA))

    def mlp(name, norm):
        hidden, resid = name + "_hidden", name + "_resid"
        for k in range(KC):
            v.tensor_scalar(h[:, k], h[:, k], ALPHA, None, ALU.mult).then_inc(sem(resid), 1)
        dve.wait_ge(sem(resid), KC)

        def up(g, step):
            for j in range(8):
                t, slot = g * 16 + (START[name] + j), (START[name] + j) % RING
                dve.wait_ge(sem("tile_out"), t + 1)
                step.link(v.tensor_tensor(xt[:, j % 2], z[:, slot], z[:, slot], ALU.mult))
                split(xt[:, j % 2], m["y_hi"][:, j], m["y_lo"][:, j], hidden, step)

        def down(g, c):
            dve.wait_ge(sem("tile_out"), g * 16 + (START[name] + 8 + c + 1))
            v.tensor_tensor(h[:, c], h[:, c], z[:, (START[name] + 8 + c) % RING], ALU.add).then_inc(sem(resid), 1)

        with dve.Fori(0, GROUPS - 1) as g:
            up(g, Own(dve, sem(name + "_step"), g * 16))
            for c in range(KC):
                down(g, c)
        up(GROUPS - 1, own)
        residual_ln(norm, resid, 8 * GROUPS + 1, 1.0, lambda c, plain=False: down(GROUPS - 1, c))

    mlp("mlp_a", "ln2a")

    t0 = START["gla_in"]
    gz, gt, gb = m["gz"], m["gt"], m["gb"]
    per_chunk = gb.rearrange("p (n c) -> p n c", c=GLA_CHUNK)
    for head in range(4):
        dve.wait_ge(sem("gla_ln"), head + 1)
        own.link(v.scalar_tensor_tensor(gz, gz, 0.0, gt, ALU.min, ALU.subtract))
        v.tensor_tensor_scan(gb, pr.view("keep"), gz, 0.0, ALU.mult, ALU.add).then_inc(sem("gla_b"), 1)
        dve.wait_ge(sem("gla_exp"), 3 * head + 2)
        own.mark(v.tensor_tensor(m["kt_g"][:, head], m["k_g"][:, head], gt, ALU.mult))
        own.mark(v.scalar_tensor_tensor(m["q_g"][:, head], m["q_g"][:, head], float(P) ** -0.5, gz, ALU.mult, ALU.mult))
        own.settle()
        v.tensor_tensor(gz.rearrange("p (n c) -> p n c", c=GLA_CHUNK),
                        per_chunk[:, :, GLA_CHUNK - 1:].to_broadcast([P, 8, GLA_CHUNK]), per_chunk, ALU.subtract)\
            .then_inc(sem("gla_rest"), 1)
        dve.wait_ge(sem("gla_exp"), 3 * head + 3)
        v.tensor_tensor(m["k_g"][:, head], m["k_g"][:, head], gz, ALU.mult).then_inc(sem("gla_k"), 1)
    dve.wait_ge(sem("tile_out"), END["gla_in"])
    own.link(v.memset(m["state"][:, 0], 0.0))

    def gla_local(head):
        dve.wait_ge(sem("gla_scores"), head + 1)
        v.tensor_tensor(m["att_g"], misc[:, 0, 0:256].rearrange("p (b n) -> p b n", b=TB),
                        pr.view("gla01").rearrange("p (b n) -> p b n", b=TB), ALU.mult).then_inc(sem("gla_att"), 1)
        for n in range(7):
            i = 7 * head + n
            dve.wait_ge(sem("gla_update"), i + 1)
            if n:
                dve.wait_ge(sem("gla_state"), i)
            v.scalar_tensor_tensor(m["state"][:, n + 1], m["state"][:, n], m["decay"][:, head, n:n + 1],
                                   misc[:, 1 + i % 2, 0:256], ALU.mult, ALU.add).then_inc(sem("gla_state"), 1)

    gla_local(0)
    for head in range(4):
        if head < 3:
            gla_local(head + 1)
        dve.wait_ge(sem("gla_rstd"), head + 1)
        dve.wait_ge(sem("gla_o_out"), 2 * head + 2)
        for e in range(2):
            c = 2 * head + e
            x = xt[:, e]
            own.link(v.scalar_tensor_tensor(x, m["o_g"][:, e], pr.col("gla_g", e), m["rstd"], ALU.mult, ALU.mult))
            own.link(v.tensor_tensor(x, x, m["r_g"][:, c], ALU.mult))
            split(x, m["y_hi"][:, c], m["y_lo"][:, c], "gla_y")
    residual_ln("ln1b", "gla_resid", 1, ALPHA, stage_add("gla_out", "gla_resid", ALPHA))
    mlp("mlp_b", "ln2b")


def gpsimd_program(pr, pool):
    nc, m, sem = pr.nc, pr.m, pr.sem

    def split(slot, t, turn):
        pool.wait_ge(sem("weights_in%d" % slot), turn * 16)
        if not isinstance(t, int) or t >= RING:
            pool.wait_ge(sem("tile_done"), t - RING + 1)
        pool.sem_inc(sem("tile_claimed"), 1)
        hi = m["w_hi"][:, slot].rearrange("p k n -> p (k n)")
        nc.gpsimd.tensor_scalar(hi, m["raw"][:, slot], 1.0, 0.0, ALU.mult, ALU.add).then_inc(sem("weights_high"), 1)
        pool.wait_ge(sem("weights_high"), t + 1)
        nc.gpsimd.tensor_tensor(m["w_lo"][:, slot].rearrange("p k n -> p (k n)"), m["raw"][:, slot], bf(hi),
                                ALU.subtract).then_inc(sem("weights_split"), 1)

    for slot in range(RING):
        split(slot, slot, 1)
    with pool.Fori(1, N_TILES // RING) as r:
        for slot in range(RING):
            split(slot, r * RING + slot, r + 1)
    for slot in range(N_TILES % RING):
        split(slot, N_TILES // RING * RING + slot, N_TILES // RING + 1)


def sync_program(pr, sp):
    m, sem, dram = pr.m, pr.sem, pr.dram
    for half in range(2):
        k = blk(half, HALF)
        sp.dma_start(m["h"][:, k], dram["x"][:, k]).then_inc(sem("x_in%d" % half), 16)
    sp.dma_start(m["const"], dram["const"]).then_inc(sem("const_in"), 16)
    sp.dma_start(m["par"], dram["par"]).then_inc(sem("par_in"), 16)
    rounds = N_TILES // RING
    stream = dram["weights"][0:rounds * RING].rearrange("(r j) p n -> r j p n", j=RING)
    for slot in range(RING):
        sp.dma_start(m["raw"][:, slot], dram["weights"][slot]).then_inc(sem("weights_in%d" % slot), 16)
    sp.dma_start(m["mem_in"], dram["mem"]).then_inc(sem("mem_in"), 16)
    with sp.Fori(1, rounds) as r:
        for slot in range(RING):
            sp.wait_ge(sem("weights_split"), r * RING + (slot - RING + 1))
            sp.dma_start(m["raw"][:, slot], stream[bass.ds(r, 1), slot].rearrange("a p n -> p (a n)"))\
                .then_inc(sem("weights_in%d" % slot), 16)
    for slot in range(N_TILES % RING):
        sp.wait_ge(sem("weights_split"), (rounds - 1) * RING + slot + 1)
        sp.dma_start(m["raw"][:, slot], dram["weights"][rounds * RING + slot])\
            .then_inc(sem("weights_in%d" % slot), 16)
    for k in range(KC):
        sp.wait_ge(sem("ln_out"), 2 * KC * (len(LAYER_NORMS) - 1) + k + 1)
        sp.dma_start(dram["out"][:, k], m["h"][:, k]).then_inc(sem("stored"), 16)
    sp.wait_ge(sem("stored"), 16 * KC)


def build(nc, dram):
    with ExitStack() as ctx:
        pr = Program(nc, ctx, dram)
        block = ctx.enter_context(nc.Block())

        @block.sync
        def _(sp):
            sync_program(pr, sp)

        @block.gpsimd
        def _(pool):
            gpsimd_program(pr, pool)

        @block.scalar
        def _(act):
            scalar_program(pr, act)

        @block.vector
        def _(dve):
            vector_program(pr, dve)

        @block.tensor
        def _(pe):
            tensor_program(pr, pe)


def kernel(**inputs):
    import concourse.bacc as bacc
    from concourse.bass_utils import run_bass_kernel_spmd as run

    i = {name: np.asarray(a) for name, a in inputs.items()}
    by_chunk = lambda a: np.ascontiguousarray(a.T.reshape(KC, P, -1).transpose(1, 0, 2))
    w1 = i["a_cmp_w1_2"][0].reshape(2 * CMP_BLOCK, 64, 64).transpose(1, 0, 2)
    arrays = {"x": by_chunk(i["x"][0]), "mem": by_chunk(i["mem"][0]), "weights": weight_stream(i),
              "const": shape_constants(), "par": params(i), "small1": small1(i), "small2": small2(i),
              "w_cmp": block_diagonal(w1).reshape(P, 2, CMP_BLOCK, P)}
    nc = bacc.Bacc("TRN2", target_bir_lowering=False, num_devices=1)
    dram = {name: nc.dram_tensor(name + "_dram", a.shape, F32, kind="ExternalInput").ap() for name, a in arrays.items()}
    dram["out"] = nc.dram_tensor("out_dram", (P, KC, S), F32, kind="ExternalOutput").ap()
    build(nc, dram)
    result = run(nc, [{name + "_dram": a for name, a in arrays.items()}], core_ids=[0])
    out = result.results[0]["out_dram"]
    return out.transpose(1, 0, 2).reshape(1, D, S).transpose(0, 2, 1)
```
